# Optimizing a Trainium2 kernel written in Bass

```python
import jax, jax.numpy as jnp
from jax import lax
import numpy as np

D_MODEL = 1024
BATCH = 1
SEQ = 1024
DEPTH = 1
DEC_BATCH = 8
DEC_SEQ = 1
PAST_LEN = 2048
PAGE_SIZE = 128

N_HEADS_NSA = 8
HEAD_DIM = 64
N_KV_HEADS = 2
GQA_GROUP = N_HEADS_NSA // N_KV_HEADS
CMP_BLOCK = 32
CMP_STRIDE = 16
CMP_HIDDEN = 256
SEL_BLOCK = 64
SEL_TOPK = 16
WINDOW = 512
N_BRANCH = 3
HG_HEADS = 4
HG_DK = 128
HG_DV = 128
HG_CHUNK = 32
NSA_WIDTH = N_HEADS_NSA * HEAD_DIM
HG_WIDTH = HG_HEADS * HG_DK
HG_VWIDTH = HG_HEADS * HG_DV
MIX_WIDTH = NSA_WIDTH + HG_VWIDTH
KV_WIDTH = 2 * N_KV_HEADS * HEAD_DIM
IN_SPLITS = (NSA_WIDTH, KV_WIDTH, KV_WIDTH, KV_WIDTH, N_BRANCH * N_HEADS_NSA,
             HG_WIDTH, HG_WIDTH, HG_VWIDTH, HG_VWIDTH)
IN_WIDTH = sum(IN_SPLITS)
D_FF = -(-8 * D_MODEL // (3 * 256)) * 256
D_PLE = 256
SEL_QBLOCK = 64
WIN_QBLOCK = 128
SCALE = HEAD_DIM ** -0.5
NEG_INF = -1e30
FORCED_SCORE = 1e9
EPS = 1e-6

kernel_name = "nsa_hgrn2_parallel_heads_decode_step"

def rms_norm(x, g):
    xf = x.astype(jnp.float32)
    y = xf * lax.rsqrt(jnp.mean(xf * xf, axis=-1, keepdims=True) + EPS) * g.astype(jnp.float32)
    return y.astype(x.dtype)

def masked_softmax(s, mask):
    s = jnp.where(mask, s.astype(jnp.float32), NEG_INF)
    return jax.nn.softmax(s, axis=-1) * mask

def compress_kv(kv, pos, w1, w2):
    B, L = kv.shape[:2]
    n_half = L // CMP_STRIDE
    halves = kv[:, :n_half * CMP_STRIDE].reshape(B, n_half, CMP_STRIDE, 2, N_KV_HEADS, HEAD_DIM)
    w1h = w1.reshape(2, 2, CMP_STRIDE, HEAD_DIM, CMP_HIDDEN)
    posh = pos.reshape(2, 2, CMP_STRIDE, HEAD_DIM).transpose(1, 2, 0, 3)
    h_lo = jnp.einsum('bnschd,csdf->bnchf', halves + posh[0][:, :, None, :], w1h[:, 0])
    h_hi = jnp.einsum('bnschd,csdf->bnchf', halves + posh[1][:, :, None, :], w1h[:, 1])
    hid = jax.nn.silu(h_lo[:, :-1] + h_hi[:, 1:])
    return jnp.einsum('bnchf,cfd->bnchd', hid, w2)

def compressed_attention(q, kv_blocks, qpos):
    n_cmp = kv_blocks.shape[1]
    s = jnp.einsum('btkgd,bnkd->bkgtn', q, kv_blocks[:, :, 0]) * SCALE
    blk_end = jnp.arange(n_cmp) * CMP_STRIDE + (CMP_BLOCK - 1)
    p = masked_softmax(s, blk_end[None, :] <= qpos[:, None])
    o = jnp.einsum('bkgtn,bnkd->btkgd', p, kv_blocks[:, :, 1])
    return o, p

def select_blocks(p_cmp, qpos, L):
    n_cmp = p_cmp.shape[-1]
    n_slc = -(-L // SEL_BLOCK)
    cs = jnp.arange(n_cmp) * CMP_STRIDE
    ss = jnp.arange(n_slc) * SEL_BLOCK
    overlap = ((cs[:, None] < ss[None, :] + SEL_BLOCK) &
               (cs[:, None] + CMP_BLOCK > ss[None, :])).astype(p_cmp.dtype)
    imp = jnp.einsum('bkgtn,ns->bkts', p_cmp, overlap)
    blk = jnp.arange(n_slc)[None, :]
    qblk = (qpos // SEL_BLOCK)[:, None]
    forced = (blk == 0) | (blk == qblk) | (blk == qblk - 1)
    valid = blk * SEL_BLOCK <= qpos[:, None]
    score = jnp.where(valid, jnp.where(forced, FORCED_SCORE, imp), NEG_INF)
    top_val, top_idx = lax.top_k(score, min(SEL_TOPK, n_slc))
    return top_idx, top_val > 0.5 * NEG_INF

def selected_attention(q, kv_all, top_idx, sel_ok, qpos):
    B, T = q.shape[:2]
    L = kv_all.shape[1]
    K = top_idx.shape[-1]
    kv_t = kv_all.transpose(0, 3, 1, 2, 4)
    qb = SEL_QBLOCK if T % SEL_QBLOCK == 0 else T
    nb = T // qb
    q_b = jnp.moveaxis(q.reshape(B, nb, qb, N_KV_HEADS, GQA_GROUP, HEAD_DIM), 1, 0)
    idx_b = jnp.moveaxis(top_idx.reshape(B, N_KV_HEADS, nb, qb, K), 2, 0)
    ok_b = jnp.moveaxis(sel_ok.reshape(B, N_KV_HEADS, nb, qb, K), 2, 0)
    pos_b = qpos.reshape(nb, qb)
    gather_rows = jax.vmap(jax.vmap(lambda rows, ii: rows[ii]))

    def one_block(args):
        qc, idx, ok, pos = args
        tok = idx[..., None] * SEL_BLOCK + jnp.arange(SEL_BLOCK)
        rows = gather_rows(kv_t, jnp.minimum(tok, L - 1).reshape(B, N_KV_HEADS, qb * K * SEL_BLOCK))
        rows = rows.reshape(B, N_KV_HEADS, qb, K * SEL_BLOCK, 2, HEAD_DIM)
        mask = (ok[..., None] & (tok <= pos[None, None, :, None, None])).reshape(
            B, N_KV_HEADS, qb, K * SEL_BLOCK)
        s = jnp.einsum('bqkgd,bkqnd->bkgqn', qc, rows[..., 0, :]) * SCALE
        p = masked_softmax(s, mask[:, :, None])
        return jnp.einsum('bkgqn,bkqnd->bqkgd', p, rows[..., 1, :])

    o = lax.map(one_block, (q_b, idx_b, ok_b, pos_b))
    return jnp.moveaxis(o, 0, 1).reshape(B, T, N_KV_HEADS, GQA_GROUP, HEAD_DIM)

def window_attention(q, kv_ext, kpos_ext, qpos, n_prefix):
    B, T = q.shape[:2]
    qb = WIN_QBLOCK if T % WIN_QBLOCK == 0 else T
    nb = T // qb
    span = n_prefix + qb

    def one_block(b):
        start = b * qb
        kv = lax.dynamic_slice_in_dim(kv_ext, start, span, axis=1)
        kp = lax.dynamic_slice_in_dim(kpos_ext, start, span)
        qc = lax.dynamic_slice_in_dim(q, start, qb, axis=1)
        qp = lax.dynamic_slice_in_dim(qpos, start, qb)
        dist = qp[:, None] - kp[None, :]
        mask = (dist >= 0) & (dist < WINDOW) & (kp[None, :] >= 0)
        s = jnp.einsum('bqkgd,bnkd->bkgqn', qc, kv[:, :, 0]) * SCALE
        p = masked_softmax(s, mask)
        return jnp.einsum('bkgqn,bnkd->bqkgd', p, kv[:, :, 1])

    o = lax.map(one_block, jnp.arange(nb))
    return jnp.moveaxis(o, 0, 1).reshape(B, T, N_KV_HEADS, GQA_GROUP, HEAD_DIM)

def hgrn2_chunked(q, log_f, v, S0):
    B, T, H, _ = q.shape
    C = HG_CHUNK
    n = -(-T // C)
    pad = n * C - T
    k = -jnp.expm1(log_f.astype(jnp.float32))

    def prep(a):
        a = jnp.pad(a.astype(jnp.float32), ((0, 0), (0, pad), (0, 0), (0, 0)))
        return a.reshape(B, n, C, H, a.shape[-1]).transpose(1, 0, 3, 2, 4)

    causal = jnp.tril(jnp.ones((C, C), dtype=bool))

    def step(S, xs):
        qi, lfi, ki, vi = xs
        cum = jnp.cumsum(lfi, axis=2)
        q_dec = qi * jnp.exp(cum)
        k_inv = ki * jnp.exp(-cum)
        attn = jnp.where(causal, jnp.einsum('bhck,bhsk->bhcs', q_dec, k_inv), 0.0)
        o = jnp.einsum('bhck,bhkv->bhcv', q_dec, S) + jnp.einsum('bhcs,bhsv->bhcv', attn, vi)
        last = cum[:, :, -1:]
        S = jnp.exp(last[:, :, 0])[..., None] * S + jnp.einsum(
            'bhck,bhcv->bhkv', ki * jnp.exp(last - cum), vi)
        return S, o

    S, o = lax.scan(step, S0.astype(jnp.float32), (prep(q), prep(log_f), prep(k), prep(v)))
    o = o.transpose(1, 0, 3, 2, 4).reshape(B, n * C, H, -1)[:, :T]
    return o, S

def hybrid_layer(h, p_emb, qpos, past_cmp, past_slc, win_prefix, win_kpos, S0, lb, buf_len, lw):
    (norm_mix, w_in, cmp_pos, cmp_w1, cmp_w2, norm_nsa_out, norm_hg_out, w_out,
     norm_ffn, w_gate_up, w_down, norm_ple, w_ple_gate, w_ple_proj) = lw
    B, T, _ = h.shape
    xn = rms_norm(h, norm_mix)
    proj = xn @ w_in
    q_a, kvc, kvs, kvw, gate_a, q_b, f_b, v_b, g_b = jnp.split(
        proj, [int(c) for c in np.cumsum(IN_SPLITS)[:-1]], axis=-1)
    q_a = q_a.reshape(B, T, N_KV_HEADS, GQA_GROUP, HEAD_DIM)
    kv_shape = (B, T, 2, N_KV_HEADS, HEAD_DIM)
    kvc, kvs, kvw = kvc.reshape(kv_shape), kvs.reshape(kv_shape), kvw.reshape(kv_shape)
    gate_a = jax.nn.sigmoid(gate_a.astype(jnp.float32)).reshape(
        B, T, N_BRANCH, N_KV_HEADS, GQA_GROUP, 1)
    kvc_all = kvc if past_cmp is None else jnp.concatenate([past_cmp, kvc], axis=1)
    kvs_all = kvs if past_slc is None else jnp.concatenate([past_slc, kvs], axis=1)
    kv_blocks = compress_kv(kvc_all, cmp_pos, cmp_w1, cmp_w2)
    o_cmp, p_cmp = compressed_attention(q_a, kv_blocks, qpos)
    top_idx, sel_ok = select_blocks(p_cmp, qpos, kvs_all.shape[1])
    o_slc = selected_attention(q_a, kvs_all, top_idx, sel_ok, qpos)
    kv_ext = jnp.concatenate([win_prefix, kvw], axis=1)
    o_win = window_attention(q_a, kv_ext, win_kpos, qpos, win_prefix.shape[1])
    o_nsa = (gate_a[:, :, 0] * o_cmp + gate_a[:, :, 1] * o_slc + gate_a[:, :, 2] * o_win)
    o_nsa = o_nsa.reshape(B, T, NSA_WIDTH).astype(h.dtype)
    q_b = jax.nn.silu(q_b).reshape(B, T, HG_HEADS, HG_DK)
    f = lb + (1.0 - lb) * jax.nn.sigmoid(f_b.astype(jnp.float32))
    log_f = jnp.log(f).reshape(B, T, HG_HEADS, HG_DK)
    o_hg, S_new = hgrn2_chunked(q_b, log_f, v_b.reshape(B, T, HG_HEADS, HG_DV), S0)
    o_hg = rms_norm(o_hg.astype(h.dtype), norm_hg_out.reshape(HG_HEADS, HG_DV)).reshape(B, T, HG_VWIDTH)
    o_hg = o_hg * jax.nn.silu(g_b)
    mix = jnp.concatenate([rms_norm(o_nsa, norm_nsa_out), o_hg], axis=-1)
    h = h + mix @ w_out
    gu = rms_norm(h, norm_ffn) @ w_gate_up
    g, u = jnp.split(gu, 2, axis=-1)
    h = h + (jax.nn.silu(g) * u) @ w_down
    h = h + jax.nn.sigmoid(rms_norm(h, norm_ple) @ w_ple_gate) * (p_emb @ w_ple_proj)
    return h, kvc, kvs, kv_ext[:, -buf_len:], S_new

def setup_inputs(seed: int = 0) -> dict:
    key = jax.random.key(seed)
    ks = jax.random.split(key, 28)
    n_pages = PAST_LEN // PAGE_SIZE
    n_used = DEC_BATCH * n_pages
    n_pool = n_used + n_used // 4
    w_buf = min(WINDOW, PAST_LEN)

    def nrm(k, shape, scale=1.0):
        return jax.random.normal(k, shape, jnp.float32) * scale

    def gain(k, shape):
        return 1.0 + 0.05 * nrm(k, shape)

    kv_page = (DEPTH, n_pool, PAGE_SIZE, 2, N_KV_HEADS, HEAD_DIM)
    perm = jax.random.permutation(ks[6], n_pool)
    page_table = perm[:n_used].reshape(DEC_BATCH, n_pages).astype(jnp.int32)
    return {
        "x_prompt": nrm(ks[0], (BATCH, SEQ, D_MODEL)),
        "x_sample": nrm(ks[1], (DEC_BATCH, DEC_SEQ, D_MODEL)),
        "cache_kv_cmp": nrm(ks[2], kv_page),
        "cache_kv_slc": nrm(ks[3], kv_page),
        "state_kv_win": nrm(ks[4], (DEPTH, DEC_BATCH, w_buf, 2, N_KV_HEADS, HEAD_DIM)),
        "state_hgrn": nrm(ks[5], (DEPTH, DEC_BATCH, HG_HEADS, HG_DK, HG_DV), 0.5),
        "page_table": page_table,
        "p_prompt": nrm(ks[7], (DEPTH, BATCH, SEQ, D_PLE)),
        "p_sample": nrm(ks[8], (DEPTH, DEC_BATCH, DEC_SEQ, D_PLE)),
        "norm_mix": gain(ks[9], (DEPTH, D_MODEL)),
        "w_in": nrm(ks[10], (DEPTH, D_MODEL, IN_WIDTH), D_MODEL ** -0.5),
        "cmp_pos": nrm(ks[11], (DEPTH, 2, CMP_BLOCK, HEAD_DIM), 0.2),
        "cmp_w1": nrm(ks[12], (DEPTH, 2, CMP_BLOCK * HEAD_DIM, CMP_HIDDEN), (CMP_BLOCK * HEAD_DIM) ** -0.5),
        "cmp_w2": nrm(ks[13], (DEPTH, 2, CMP_HIDDEN, HEAD_DIM), CMP_HIDDEN ** -0.5),
        "hg_lb": nrm(ks[14], (DEPTH + 1, HG_WIDTH), 0.1),
        "norm_nsa_out": gain(ks[15], (DEPTH, NSA_WIDTH)),
        "norm_hg_out": gain(ks[16], (DEPTH, HG_VWIDTH)),
        "w_out": nrm(ks[17], (DEPTH, MIX_WIDTH, D_MODEL), MIX_WIDTH ** -0.5),
        "norm_ffn": gain(ks[18], (DEPTH, D_MODEL)),
        "w_gate_up": nrm(ks[19], (DEPTH, D_MODEL, 2 * D_FF), D_MODEL ** -0.5),
        "w_down": nrm(ks[20], (DEPTH, D_FF, D_MODEL), D_FF ** -0.5),
        "norm_ple": gain(ks[21], (DEPTH, D_MODEL)),
        "w_ple_gate": nrm(ks[22], (DEPTH, D_MODEL, D_MODEL), D_MODEL ** -0.5),
        "w_ple_proj": nrm(ks[23], (DEPTH, D_PLE, D_MODEL), D_PLE ** -0.5),
        "norm_final": gain(ks[24], (D_MODEL,)),
    }

def reference(x_prompt, x_sample, cache_kv_cmp, cache_kv_slc, state_kv_win, state_hgrn, page_table,
              p_prompt, p_sample, norm_mix, w_in, cmp_pos, cmp_w1, cmp_w2, hg_lb, norm_nsa_out,
              norm_hg_out, w_out, norm_ffn, w_gate_up, w_down, norm_ple, w_ple_gate, w_ple_proj,
              norm_final):
    n_pages = PAST_LEN // PAGE_SIZE
    past_len = n_pages * PAGE_SIZE
    w_buf = state_kv_win.shape[2]
    lb_all = jnp.cumsum(jax.nn.softmax(hg_lb.astype(jnp.float32), axis=0), axis=0)
    qpos_p = jnp.arange(SEQ)
    qpos_s = past_len + jnp.arange(DEC_SEQ)
    kpos_p = jnp.arange(-WINDOW, SEQ)
    kpos_s = past_len - w_buf + jnp.arange(w_buf + DEC_SEQ)
    win_prefix_p = jnp.zeros((BATCH, WINDOW, 2, N_KV_HEADS, HEAD_DIM), x_prompt.dtype)
    S0_p = jnp.zeros((BATCH, HG_HEADS, HG_DK, HG_DV), jnp.float32)
    hp, hs = x_prompt, x_sample
    kvc_p, kvs_p, win_p, hg_p = [], [], [], []
    kvc_s, kvs_s, win_s, hg_s = [], [], [], []
    for l in range(DEPTH):
        lw = (norm_mix[l], w_in[l], cmp_pos[l], cmp_w1[l], cmp_w2[l], norm_nsa_out[l],
              norm_hg_out[l], w_out[l], norm_ffn[l], w_gate_up[l], w_down[l], norm_ple[l],
              w_ple_gate[l], w_ple_proj[l])
        hp, a, b, c, d = hybrid_layer(hp, p_prompt[l], qpos_p, None, None, win_prefix_p, kpos_p,
                                      S0_p, lb_all[l], min(WINDOW, SEQ), lw)
        kvc_p.append(a); kvs_p.append(b); win_p.append(c); hg_p.append(d)
        past_cmp = cache_kv_cmp[l][page_table].reshape(DEC_BATCH, past_len, 2, N_KV_HEADS, HEAD_DIM)
        past_slc = cache_kv_slc[l][page_table].reshape(DEC_BATCH, past_len, 2, N_KV_HEADS, HEAD_DIM)
        hs, a, b, c, d = hybrid_layer(hs, p_sample[l], qpos_s, past_cmp, past_slc, state_kv_win[l],
                                      kpos_s, state_hgrn[l], lb_all[l], w_buf, lw)
        kvc_s.append(a); kvs_s.append(b); win_s.append(c); hg_s.append(d)
    y_prompt = rms_norm(hp, norm_final)
    y_sample = rms_norm(hs, norm_final)
    return (y_prompt, y_sample,
            jnp.stack(kvc_p), jnp.stack(kvs_p), jnp.stack(win_p), jnp.stack(hg_p),
            jnp.stack(kvc_s), jnp.stack(kvs_s), jnp.stack(win_s), jnp.stack(hg_s))


_drawn_inputs = setup_inputs


def setup_inputs(seed=0):
    import zlib

    import numpy as np

    out = dict(_drawn_inputs(seed))
    spreads = {}
    factors = {'norm_hg_out': 3.397, 'norm_ple': 25.337, 'norm_nsa_out': 2.79}
    for name, (base, spread) in spreads.items():
        noise = np.random.default_rng([zlib.crc32(name.encode()), seed]).standard_normal(out[name].shape)
        drawn = base * np.exp(spread * noise) if base else spread * noise
        out[name] = __import__('jax').numpy.asarray(drawn.astype(out[name].dtype))
    for name, factor in factors.items():
        out[name] = (out[name] * factor).astype(out[name].dtype)
    return out
```

```python
from contextlib import ExitStack

import concourse.bass as bass
import concourse.mybir as mybir
from concourse.alu_op_type import AluOpType as ALU
import numpy as np

ACT = mybir.ActivationFunctionType
F32 = mybir.dt.float32
I32 = mybir.dt.int32
AX = mybir.AxisListType

P = 128
SEQ, DEC = 1024, 8
T = SEQ + DEC
GROUPS = 3
G = T // GROUPS
DM, DFF, DPLE = 1024, 2816, 256
KC = DM // P
FC = DFF // P
PAGES, PAGE, POOL = 16, 128, 160
HEAD, KVH, GQA = 64, 2, 4
NSA, HG, HGH = 512, 512, 4
WINDOW = 512
N_CMP_P, N_CMP_D = 63, 127
N_SEL = 33
TOPK = 16
SCALE = HEAD ** -0.5
NEG = -1e30
FORCED = 1e9
TILES = [(i * P, min(P, T - i * P)) for i in range(9)]
QT = SEQ // P
BLOCK32 = 32
TOK_GROUPS = ((0, 512), (512, 280), (792, 512))
V_MIX, V_NSA, V_HG, V_FFN, V_PLE, V_FINAL, V_LB, V_EPS = 0, 8, 12, 16, 24, 32, 40, 48
V_HEAD0, V_HEAD1, V_COLS = 49, 50, 51


class Chain:

    def __init__(self, engine, semaphore, count=0):
        self.engine, self.semaphore, self.count = engine, semaphore, count

    def __call__(self, instruction):
        instruction.then_inc(self.semaphore, 1)
        self.count = self.count + 1
        self.engine.wait_ge(self.semaphore, self.count)


class Tensors:

    def __init__(self, dram):
        self.dram = dram


USED = []


def phase(nc, stack):
    def sem(name):
        USED.append(stack.enter_context(nc.semaphore(name)))
        return USED[-1]
    return sem


def clear_semaphores(nc):
    for semaphore in USED:
        nc.sync.sem_clear(semaphore)
    USED.clear()
    nc.all_engine_barrier()


def cols(group):
    return slice(group * G, (group + 1) * G)


def rms_norm_features(nc, m, name, source, gain, target, load=None):
    with ExitStack() as stack:
        sem = phase(nc, stack)
        squares = stack.enter_context(nc.sbuf_tensor(f"{name}_squares", [P, 2, T], F32))
        total = stack.enter_context(nc.sbuf_tensor(f"{name}_total", [P, T], F32))
        scale = stack.enter_context(nc.sbuf_tensor(f"{name}_scale", [P, T], F32))
        loaded = sem(f"{name}_loaded")
        squared = sem(f"{name}_squared")
        added = sem(f"{name}_added")
        mean_ready = sem(f"{name}_mean")
        root_ready = sem(f"{name}_root")
        inverted = sem(f"{name}_inverted")
        block = stack.enter_context(nc.Block())

        @block.sync
        def _(sp):
            if load is not None:
                load(sp, loaded)

        @block.scalar
        def _(act):
            if load is not None:
                act.wait_ge(loaded, m.load_total)
            for c in range(KC):
                if c >= 2:
                    act.wait_ge(added, c - 1)
                nc.scalar.activation(squares[:, c % 2, :], source[:, c, :], ACT.Square).then_inc(squared, 1)
            for g in range(GROUPS):
                act.wait_ge(mean_ready, g + 1)
                nc.scalar.activation(scale[:, cols(g)], m.bank[g][:, 0:G], ACT.Sqrt,
                                     bias=m.vectors[:, V_EPS:V_EPS + 1]).then_inc(root_ready, 1)

        @block.vector
        def _(dve):
            for c in range(KC):
                dve.wait_ge(squared, c + 1)
                if c:
                    dve.wait_ge(added, c)
                    nc.vector.tensor_tensor(total[:], total[:], squares[:, c % 2, :], ALU.add).then_inc(added, 1)
                else:
                    nc.vector.tensor_copy(total[:], squares[:, 0, :]).then_inc(added, 1)
            for g in range(GROUPS):
                dve.wait_ge(root_ready, g + 1)
                nc.vector.reciprocal(scale[:, cols(g)], scale[:, cols(g)]).then_inc(inverted, 1)
            dve.wait_ge(inverted, GROUPS)
            for c in range(KC):
                nc.vector.scalar_tensor_tensor(out=target[:, c, :], in0=source[:, c, :],
                                               scalar=m.vectors[:, gain + c:gain + c + 1],
                                               in1=scale[:], op0=ALU.mult, op1=ALU.mult)

        @block.tensor
        def _(pe):
            pe.wait_ge(added, KC)
            for g in range(GROUPS):
                nc.tensor.matmul(m.bank[g][:, 0:G], m.mean_weights[:], total[:, cols(g)],
                                 start=True, stop=True).then_inc(mean_ready, 1)


FEATURE_CHUNKS = 16
SLOTS = 4


def project_features(nc, m):
    with ExitStack() as stack:
        sem = phase(nc, stack)
        ring = stack.enter_context(nc.sbuf_tensor("feature_weights", [P, SLOTS, KC, P], F32))
        arrived = [sem(f"feature_weights{s}") for s in range(SLOTS)]
        chunk_done = sem("feature_chunk_done")
        banks_free = sem("feature_banks_free")
        block = stack.enter_context(nc.Block())

        @block.sync
        def _(sp):
            for s in range(SLOTS):
                sp.dma_start(ring[:, s], m.dram["w_feature"][s]).then_inc(arrived[s], 16)
            with sp.Fori(1, FEATURE_CHUNKS // SLOTS) as i:
                for s in range(SLOTS):
                    sp.wait_ge(chunk_done, i * SLOTS + (s - SLOTS + 1))
                    sp.dma_start(ring[:, s], m.dram["w_feature"][i * SLOTS + s]).then_inc(arrived[s], 16)

        @block.tensor
        def _(pe):
            with pe.Fori(0, FEATURE_CHUNKS // SLOTS) as i:
                for s in range(SLOTS):
                    pe.wait_ge(arrived[s], i * 16 + 16)
                    pe.wait_ge(banks_free, i * SLOTS + (s + 1))
                    for g in range(GROUPS):
                        for k in range(KC):
                            last = nc.tensor.matmul(m.bank[3 * (s % 2) + g][:, 0:G], ring[:, s, k],
                                                    m.xn[:, k, cols(g)], start=k == 0, stop=k == KC - 1)
                    last.then_inc(chunk_done, 1)

        @block.scalar
        def _(act):
            act.sem_inc(banks_free, 2)
            kinds = ((m.q_a, ACT.Copy), (m.q_b, ACT.Silu), (m.gate_b, ACT.Silu), (m.forget, ACT.Sigmoid))
            for c in range(FEATURE_CHUNKS):
                target, function = kinds[c // 4]
                act.wait_ge(chunk_done, c + 1)
                for g in range(GROUPS):
                    last = nc.scalar.activation(target[:, c % 4, cols(g)], m.bank[3 * (c % 2) + g][:, 0:G],
                                                function)
                last.then_inc(banks_free, 1)


def lower_bound(nc, m):
    with ExitStack() as stack:
        sem = phase(nc, stack)
        step_done = sem("lower_step")
        exp_ready = sem("lower_exp")
        block = stack.enter_context(nc.Block())
        a0, a1 = m.vectors[:, V_LB:V_LB + 4], m.vectors[:, V_LB + 4:V_LB + 8]
        lb, rest, top, shifted = m.lower[:, 0:4], m.lower[:, 4:8], m.lower[:, 8:12], m.lower[:, 12:20]

        @block.vector
        def _(dve):
            step = Chain(dve, step_done)
            step(nc.vector.tensor_tensor(top, a0, a1, ALU.max))
            step(nc.vector.tensor_tensor(shifted[:, 0:4], a0, top, ALU.subtract))
            step(nc.vector.tensor_tensor(shifted[:, 4:8], a1, top, ALU.subtract))
            dve.wait_ge(exp_ready, 1)
            step(nc.vector.tensor_tensor(top, shifted[:, 0:4], shifted[:, 4:8], ALU.add))
            step(nc.vector.reciprocal(top, top))
            step(nc.vector.tensor_tensor(lb, shifted[:, 0:4], top, ALU.mult))
            step(nc.vector.tensor_scalar(rest, lb, -1.0, 1.0, ALU.mult, ALU.add))

        @block.scalar
        def _(act):
            act.wait_ge(step_done, 3)
            nc.scalar.activation(shifted, shifted, ACT.Exp).then_inc(exp_ready, 1)


def project_tokens(nc, m):
    with ExitStack() as stack:
        sem = phase(nc, stack)
        ring = stack.enter_context(nc.sbuf_tensor("token_weights", [P, 2, KC, 512], F32))
        arrived = [sem(f"token_weights{s}") for s in range(2)]
        tile_done = sem("token_tile_done")
        tile_kept = sem("token_tile_kept")
        turned = sem("keys_turned")
        keys_kept = sem("keys_kept")
        stored = sem("rows_stored")
        block = stack.enter_context(nc.Block())
        targets = (m.kv_a, m.kv_b, m.v_hg)

        @block.sync
        def _(sp):
            for n, (start, width) in enumerate(TOK_GROUPS):
                if n == 2:
                    sp.wait_ge(tile_done, 9)
                sp.dma_start(ring[:, n % 2, :, 0:width],
                             m.dram["w_token"][:, :, start:start + width]).then_inc(arrived[n % 2], 16)
            stores = 0
            sp.wait_ge(tile_kept, 9)
            rows = m.kv_a[:, 0:8]
            sp.dma_start(m.dram["out_cmp_p"].rearrange("(i p) f -> p i f", p=P), rows[:, :, 0:256]).then_inc(stored, 16)
            sp.dma_start(m.dram["out_slc_p"].rearrange("(i p) f -> p i f", p=P), rows[:, :, 256:512]).then_inc(stored, 16)
            sp.dma_start(m.dram["out_cmp_s"], m.kv_a[0:DEC, 8, 0:256]).then_inc(stored, 16)
            sp.dma_start(m.dram["out_slc_s"], m.kv_a[0:DEC, 8, 256:512]).then_inc(stored, 16)
            sp.dma_start(m.dram["out_win_s"][:, 0:WINDOW - 1], m.dram["window_rows"][:, 1:WINDOW]).then_inc(stored, 16)
            sp.wait_ge(tile_kept, 18)
            sp.dma_start(m.dram["out_win_p"].rearrange("(i p) f -> p i f", p=P), m.kv_b[:, 4:8, 0:256]).then_inc(stored, 16)
            sp.dma_start(m.dram["out_win_s"][:, WINDOW - 1], m.kv_b[0:DEC, 8, 0:256]).then_inc(stored, 16)
            sp.dma_start(m.dram["gate_rows"].rearrange("b h c -> b (h c)"), m.kv_b[0:DEC, 8, 256:280]).then_inc(stored, 16)
            sp.wait_ge(stored, 8 * 16)

        @block.tensor
        def _(pe):
            n = 0
            for group, (start, width) in enumerate(TOK_GROUPS):
                pe.wait_ge(arrived[group % 2], 16 * (group // 2 + 1))
                for i, (first, count) in enumerate(TILES):
                    if n >= 6:
                        pe.wait_ge(tile_kept, n - 5)
                    for k in range(KC):
                        last = nc.tensor.matmul(m.bank[n % 6][0:count, 0:width], m.xn[:, k, first:first + count],
                                                ring[:, group % 2, k, 0:width], start=k == 0, stop=k == KC - 1)
                    last.then_inc(tile_done, 1)
                    n += 1
            pe.wait_ge(tile_kept, 18)
            step = 0
            for keys in (m.kv_a[:, :, 256:384], m.kv_b[:, :, 0:128]):
                for tiles in (range(0, 4), range(4, 8), range(8, 9)):
                    if step >= 2:
                        pe.wait_ge(keys_kept, step - 1)
                    for i in tiles:
                        count = TILES[i][1]
                        last = nc.tensor.transpose(m.bank[6 + step % 2][:, (i % 4) * P:(i % 4) * P + count],
                                                   keys[0:count, i], m.identity[0:count, 0:count])
                    last.then_inc(turned, 1)
                    step += 1

        @block.vector
        def _(dve):
            n = 0
            for group, (start, width) in enumerate(TOK_GROUPS):
                for i, (first, count) in enumerate(TILES):
                    dve.wait_ge(tile_done, n + 1)
                    nc.vector.tensor_copy(targets[group][0:count, i, 0:width],
                                          m.bank[n % 6][0:count, 0:width]).then_inc(tile_kept, 1)
                    n += 1

        @block.scalar
        def _(act):
            step = 0
            for keys_t in (m.k_slc, m.k_win):
                for first, count in ((0, 512), (512, 512), (1024, DEC)):
                    act.wait_ge(turned, step + 1)
                    nc.scalar.activation(keys_t[:, first:first + count], m.bank[6 + step % 2][:, 0:count],
                                         ACT.Copy).then_inc(keys_kept, 1)
                    step += 1


def hgrn_prompt(nc, m):
    with ExitStack() as stack:
        sem = phase(nc, stack)

        def sb(name, shape):
            return stack.enter_context(nc.sbuf_tensor(name, shape, F32))

        W = HGH * P
        reset = sb("chunk_reset", [P, W])
        logf, cum, diff = sb("log_f", [P, W]), sb("cum_log_f", [P, W]), sb("cum_to_last", [P, W])
        grow, shrink = sb("exp_cum", [P, W]), sb("exp_minus_cum", [P, W])
        decay = sb("chunk_decay", [P, HGH, 4])
        key = sb("hgrn_key", [P, W])
        q_dec, k_inv, k_last = sb("q_dec", [P, HGH, P]), sb("k_inv", [P, HGH, P]), sb("k_last", [P, HGH, P])
        k_rows, values = sb("k_last_rows", [P, HGH, P]), sb("hgrn_values", [P, HGH, P])
        weights = sb("intra_weights", [P, HGH, P])
        state = sb("hgrn_state", [P, 2, HGH, P])
        prepared = sem("hgrn_reset_ready")
        forget_done = sem("forget_done")
        log_ready = sem("log_f_ready")
        cum_ready = sem("cum_ready")
        diff_ready = sem("diff_ready")
        exps_ready = sem("exps_ready")
        last_ready = sem("exp_last_ready")
        factors_ready = sem("factors_ready")
        k_last_ready = sem("k_last_ready")
        values_ready = sem("values_ready")
        scores_done = sem("intra_scores_done")
        rows_turned = sem("k_rows_turned")
        rows_kept = sem("k_rows_kept")
        weights_ready = sem("intra_weights_ready")
        update_done = sem("state_update_done")
        state_ready = sem("state_ready")
        out_done = sem("hgrn_out_done")
        out_kept = sem("hgrn_out_kept")
        stored = sem("hgrn_state_stored")
        block = stack.enter_context(nc.Block())
        GROUPS8 = SEQ // P
        bank_scores, bank_rows, bank_out, bank_update = m.bank[0], m.bank[1], m.bank[2], (m.bank[3], m.bank[4])

        def heads(ap):
            return ap.rearrange("p (h t) -> p h t", h=HGH)

        def window(ap, n):
            return ap[:, :, bass.ds(n * P, P)]

        @block.scalar
        def _(act):
            act.sem_inc(out_kept, 1)
            act.wait_ge(forget_done, HGH)
            with act.Fori(0, GROUPS8) as n:
                nc.scalar.activation(heads(logf[:]), window(m.forget, n), ACT.Ln).then_inc(log_ready, 1)
                act.wait_ge(cum_ready, n + 1)
                nc.scalar.activation(grow[:], cum[:], ACT.Exp)
                nc.scalar.activation(shrink[:], cum[:], ACT.Exp, scale=-1.0).then_inc(exps_ready, 1)
                act.wait_ge(diff_ready, n + 1)
                nc.scalar.activation(decay[:], heads(cum[:]).rearrange("p h (c s) -> p h c s", s=BLOCK32)[:, :, :, BLOCK32 - 1],
                                     ACT.Exp)
                nc.scalar.activation(logf[:], diff[:], ACT.Exp).then_inc(last_ready, 1)
                act.wait_ge(rows_turned, n + 1)
                nc.scalar.activation(k_rows[:].rearrange("p h t -> p (h t)"), bank_rows[:], ACT.Copy).then_inc(rows_kept, 1)
                act.wait_ge(out_done, n + 1)
                nc.scalar.activation(m.v_hg[:, bass.ds(n, 1), :].rearrange("p a f -> p (a f)"), bank_out[:],
                                     ACT.Copy).then_inc(out_kept, 1)
                act.wait_ge(k_last_ready, n + 1)

        @block.gpsimd
        def _(pool):
            with pool.Fori(0, GROUPS8) as n:
                pool.wait_ge(out_kept, n + 1)
                nc.gpsimd.tensor_copy(values[:].rearrange("p h t -> p (h t)"),
                                      m.v_hg[:, bass.ds(n, 1), :].rearrange("p a f -> p (a f)")).then_inc(values_ready, 1)

        @block.vector
        def _(dve):
            nc.vector.memset(state[:, 0], 0.0).then_inc(prepared, 1)
            nc.vector.memset(reset[:], 1.0).then_inc(prepared, 1)
            dve.wait_ge(prepared, 2)
            nc.vector.memset(reset[:].rearrange("p (c s) -> p c s", s=BLOCK32)[:, :, 0], 0.0).then_inc(prepared, 1)
            for h in range(HGH):
                nc.vector.tensor_scalar(m.forget[:, h], m.forget[:, h], m.lower[:, 4 + h:5 + h],
                                        m.lower[:, h:h + 1], ALU.mult, ALU.add).then_inc(forget_done, 1)
            dve.wait_ge(forget_done, HGH)
            dve.wait_ge(prepared, 3)
            with dve.Fori(0, GROUPS8) as n:
                nc.vector.tensor_scalar(heads(key[:]), window(m.forget, n), -1.0, 1.0, ALU.mult, ALU.add)
                dve.wait_ge(log_ready, n + 1)
                nc.vector.tensor_tensor_scan(cum[:], reset[:], logf[:], 0.0, ALU.mult, ALU.add).then_inc(cum_ready, 1)
                dve.wait_ge(cum_ready, n + 1)
                c4 = cum[:].rearrange("p (c s) -> p c s", s=BLOCK32)
                nc.vector.tensor_tensor(diff[:].rearrange("p (c s) -> p c s", s=BLOCK32),
                                        c4[:, :, BLOCK32 - 1:BLOCK32].to_broadcast([P, W // BLOCK32, BLOCK32]), c4,
                                        ALU.subtract).then_inc(diff_ready, 1)
                dve.wait_ge(exps_ready, n + 1)
                nc.vector.tensor_tensor(q_dec[:], window(m.q_b, n), heads(grow[:]), ALU.mult)
                nc.vector.tensor_tensor(k_inv[:], heads(key[:]), heads(shrink[:]), ALU.mult).then_inc(factors_ready, 1)
                dve.wait_ge(last_ready, n + 1)
                nc.vector.tensor_tensor(k_last[:], heads(key[:]), heads(logf[:]), ALU.mult).then_inc(k_last_ready, 1)
                dve.wait_ge(scores_done, n + 1)
                nc.vector.tensor_tensor(weights[:], bank_scores[:].rearrange("p (h t) -> p h t", h=HGH),
                                        m.intra_mask[:].rearrange("p (a t) -> p a t", a=1).to_broadcast([P, HGH, P]),
                                        ALU.mult).then_inc(weights_ready, 1)
                for j in range(4):
                    dve.wait_ge(update_done, n * 4 + (j + 1))
                    if j:
                        dve.wait_ge(state_ready, n * 4 + j)
                    for h in range(HGH):
                        last = nc.vector.scalar_tensor_tensor(
                            out=state[:, (j + 1) % 2, h], in0=state[:, j % 2, h], scalar=decay[:, h, j:j + 1],
                            in1=bank_update[j % 2][:, h * P:(h + 1) * P], op0=ALU.mult, op1=ALU.add)
                    last.then_inc(state_ready, 1)
                dve.wait_ge(state_ready, n * 4 + 4)

        @block.tensor
        def _(pe):
            pe.wait_ge(prepared, 1)
            with pe.Fori(0, GROUPS8) as n:
                pe.wait_ge(factors_ready, n + 1)
                for h in range(HGH):
                    last = nc.tensor.matmul(bank_scores[:, h * P:(h + 1) * P], k_inv[:, h], q_dec[:, h],
                                            start=True, stop=True)
                last.then_inc(scores_done, 1)
                pe.wait_ge(k_last_ready, n + 1)
                for h in range(HGH):
                    last = nc.tensor.transpose(bank_rows[:, h * P:(h + 1) * P], k_last[:, h], m.identity[:])
                last.then_inc(rows_turned, 1)
                pe.wait_ge(weights_ready, n + 1)
                pe.wait_ge(values_ready, n + 1)
                pe.wait_ge(out_kept, n + 1)
                for h in range(HGH):
                    nc.tensor.matmul(bank_out[:, h * P:(h + 1) * P], weights[:, h], values[:, h],
                                     start=h == 0, stop=False, skip_group_check=True)
                pe.wait_ge(rows_kept, n + 1)
                for j in range(4):
                    rows = slice(j * BLOCK32, (j + 1) * BLOCK32)
                    if j >= 2:
                        pe.wait_ge(state_ready, n * 4 + (j - 1))
                    for h in range(HGH):
                        last = nc.tensor.matmul(bank_update[j % 2][:, h * P:(h + 1) * P], k_rows[rows, h],
                                                values[rows, h], start=True, stop=True)
                    last.then_inc(update_done, 1)
                    if j:
                        pe.wait_ge(state_ready, n * 4 + j)
                    for h in range(HGH):
                        last = nc.tensor.matmul(bank_out[rows, h * P:(h + 1) * P], q_dec[:, h, rows],
                                                state[:, j % 2, h], start=False, stop=h == HGH - 1,
                                                skip_group_check=True)
                last.then_inc(out_done, 1)

        @block.sync
        def _(sp):
            sp.wait_ge(state_ready, GROUPS8 * 4)
            sp.dma_start(m.dram["out_hgrn_p"].rearrange("h k v -> k h v"), state[:, 0]).then_inc(stored, 16)
            sp.wait_ge(stored, 16)


def hgrn_decode(nc, m):
    with ExitStack() as stack:
        sem = phase(nc, stack)

        def sb(name, shape):
            return stack.enter_context(nc.sbuf_tensor(name, shape, F32))

        state = sb("decode_state", [P, 2, HGH, P])
        outer = sb("decode_outer", [P, HGH, P])
        key = sb("decode_key", [P, HGH, DEC])
        query = sb("decode_query", [P, HGH, DEC, DEC])
        loaded = [sem(f"decode_state_loaded{s}") for s in range(2)]
        query_ready = sem("decode_query_ready")
        spread = sem("decode_values_spread")
        outer_ready = sem("decode_outer_ready")
        updated = sem("decode_state_updated")
        read_out = sem("decode_state_read")
        stored = [sem(f"decode_state_stored{s}") for s in range(2)]
        kept = sem("decode_out_kept")
        block = stack.enter_context(nc.Block())
        bank_out = m.bank[2]

        @block.sync
        def _(sp):
            for b in range(DEC):
                if b >= 2:
                    sp.wait_ge(stored[b % 2], 16 * (b // 2))
                    sp.wait_ge(read_out, b - 1)
                sp.dma_start(state[:, b % 2], m.dram["state_hgrn"][b].rearrange("h k v -> k h v")).then_inc(loaded[b % 2], 16)

        @block.gpsimd
        def _(pool):
            for b in range(DEC):
                pool.wait_ge(updated, 4 * (b + 1))
                pool.dma_start(m.dram["out_hgrn_s"][b].rearrange("h k v -> k h v"), state[:, b % 2]).then_inc(stored[b % 2], 16)
            for s in range(2):
                pool.wait_ge(stored[s], 16 * (DEC // 2))

        @block.vector
        def _(dve):
            nc.vector.memset(query[:], 0.0).then_inc(query_ready, 1)
            nc.vector.tensor_scalar(key[:], m.forget[:, :, SEQ:T], -1.0, 1.0, ALU.mult, ALU.add).then_inc(query_ready, 1)
            dve.wait_ge(query_ready, 2)
            nc.vector.tensor_copy(query[:].rearrange("p h b c -> p h (b c)")[:, :, 0:DEC * DEC:DEC + 1],
                                  m.q_b[:, :, SEQ:T]).then_inc(query_ready, 1)
            for b in range(DEC):
                dve.wait_ge(spread, b + 1)
                for h in range(HGH):
                    last = nc.vector.tensor_scalar(outer[:, h], m.bank[b % 2][:, h * P:(h + 1) * P],
                                                   key[:, h, b:b + 1], None, ALU.mult)
                last.then_inc(outer_ready, 1)
                dve.wait_ge(outer_ready, b + 1)
                dve.wait_ge(loaded[b % 2], 16 * (b // 2 + 1))
                for h in range(HGH):
                    nc.vector.scalar_tensor_tensor(out=state[:, b % 2, h], in0=state[:, b % 2, h],
                                                   scalar=m.forget[:, h, SEQ + b:SEQ + b + 1], in1=outer[:, h],
                                                   op0=ALU.mult, op1=ALU.add).then_inc(updated, 1)
                dve.wait_ge(updated, 4 * (b + 1))

        @block.tensor
        def _(pe):
            pe.wait_ge(query_ready, 3)
            for b in range(DEC):
                if b >= 2:
                    pe.wait_ge(outer_ready, b - 1)
                nc.tensor.matmul(m.bank[b % 2][:], m.row_pick[0:DEC, b], m.v_hg[0:DEC, 8],
                                 start=True, stop=True).then_inc(spread, 1)
                pe.wait_ge(updated, 4 * (b + 1))
                for h in range(HGH):
                    last = nc.tensor.matmul(bank_out[0:DEC, h * P:(h + 1) * P], query[:, h, b], state[:, b % 2, h],
                                            start=b == 0 and h == 0, stop=b == DEC - 1, skip_group_check=True)
                last.then_inc(read_out, 1)

        @block.scalar
        def _(act):
            act.wait_ge(read_out, DEC)
            nc.scalar.activation(m.v_hg[0:DEC, 8], bank_out[0:DEC], ACT.Copy).then_inc(kept, 1)


HALF = 16
PAIRS = HALF // 2
HID = 256


def compress(nc, m, prompt):
    with ExitStack() as stack:
        sem = phase(nc, stack)
        n_half = SEQ // HALF if prompt else PAGES * PAGE // HALF
        per_page = n_half if prompt else PAGE // HALF
        pages = n_half // per_page
        count = 1 if prompt else DEC
        slots = 1 if prompt else 2
        tag = "prompt" if prompt else "cache"
        width = KVH * n_half

        def sb(name, shape):
            return stack.enter_context(nc.sbuf_tensor(f"{tag}_{name}", shape, F32))

        rows = sb("rows", [P, slots, pages, PAIRS, 2, KVH, per_page])
        high = sb("high_half", [P, KVH, n_half + 1])
        before = sb("hidden_before", [P, 2, KVH, n_half])
        hidden = sb("hidden", [P, 2, 2, KVH, n_half])
        row_halves = sb("row_halves", [SEQ // HALF, 2 * KVH, HALF, HEAD]) if prompt else None
        weights_in = sem("compress_weights_in")
        bias_done = sem("compress_bias_done")
        bias_kept = sem("compress_bias_kept")
        halves_in = sem("prompt_halves_in")
        turned = sem("prompt_halves_turned")
        rows_kept = sem("prompt_rows_kept")
        page_in = [sem(f"compress_page_in{s}") for s in range(slots)]
        table_in = sem("compress_table_in")
        product_done = sem("half_products_done")
        high_kept = sem("high_half_kept")
        sum_ready = sem("hidden_sum_ready")
        hidden_ready = sem("hidden_ready")
        blocks_done = sem("kv_blocks_done")
        blocks_kept = sem("kv_blocks_kept")
        zeroed = sem("high_half_zeroed")
        block = stack.enter_context(nc.Block())
        w1 = m.xn[:].rearrange("p c t -> p (c t)")[:, 0:2 * 2 * PAIRS * HID].rearrange(
            "p (c l s f) -> p c l s f", c=2, l=2, s=PAIRS)
        UNITS = 4

        def over_sequences(engine, work):
            if prompt:
                work(0, 0)
            else:
                with engine.Fori(0, DEC // 2) as i:
                    for s in range(2):
                        work(i * 2 + s, s)

        @block.sync
        def _(sp):
            if prompt:
                sp.dma_start(w1, m.dram["cmp_w1"]).then_inc(weights_in, 16)
                sp.dma_start(m.w2_k[:], m.dram["cmp_w2_k"]).then_inc(weights_in, 16)
                sp.dma_start(m.w2_v[:], m.dram["cmp_w2_v"]).then_inc(weights_in, 16)
                sp.dma_start(m.pos[:], m.dram["cmp_pos"]).then_inc(weights_in, 16)
                for a in range(2 * KVH):
                    sp.dma_start(row_halves[:, a], m.dram["out_cmp_p"][:, a * HEAD:(a + 1) * HEAD]
                                 .rearrange("(n s) d -> n s d", s=HALF)).then_inc(halves_in, 16)
            else:
                sp.dma_start(m.table[:], m.dram["page_table"]).then_inc(table_in, 16)
                sp.wait_ge(table_in, 16)

                def load_page(b, p, s, freed=None):
                    page = sp.value_load(m.table[0:1, bass.ds(b * PAGES + p, 1)], min_val=0, max_val=POOL - 1)
                    if freed is not None:
                        sp.wait_ge(product_done, freed)
                    sp.dma_start(rows[:, s, bass.ds(p, 1)].rearrange("p a s c k n -> p a (s c k n)"),
                                 m.dram["cache_cmp"][bass.ds(page, 1)].rearrange("a p f -> p a f")).then_inc(page_in[s], 16)

                for s in range(2):
                    with sp.Fori(0, PAGES) as p:
                        load_page(s, p, s)
                with sp.Fori(1, DEC // 2) as i:
                    for s in range(2):
                        load_page(i * 2 + s, 0, s, freed=(i * 2 + (s - 1)) * UNITS)
                        with sp.Fori(1, PAGES) as p:
                            load_page(i * 2 + s, p, s)

        @block.tensor
        def _(pe):
            if prompt:
                pe.wait_ge(weights_in, 4 * 16)
                for c in range(2):
                    for f in range(2):
                        for l in range(2):
                            for s in range(PAIRS):
                                last = nc.tensor.matmul(m.bank[7][:, 2 * c + f:2 * c + f + 1],
                                                        w1[:, c, l, s, f * P:(f + 1) * P], m.pos[:, c, l, s:s + 1],
                                                        start=l == 0 and s == 0, stop=l == 1 and s == PAIRS - 1)
                last.then_inc(bias_done, 1)
                pe.wait_ge(halves_in, 4 * 16)
                for c in range(2):
                    for k in range(KVH):
                        for s in range(PAIRS):
                            last = nc.tensor.transpose(m.bank[2 * c + k][:, s * n_half:(s + 1) * n_half],
                                                       row_halves[:, 2 * c + k, 2 * s:2 * s + 2].rearrange("n s d -> n (s d)"),
                                                       m.identity[0:n_half, 0:n_half])
                        last.then_inc(turned, 1)
                pe.wait_ge(rows_kept, 4)

            def work(n, slot):
                if not prompt:
                    pe.wait_ge(page_in[slot], (n - slot + 2) * (8 * PAGES))
                for c in range(2):
                    for f in range(2):
                        u = 2 * c + f
                        for l in range(2):
                            for s in range(PAIRS):
                                if prompt:
                                    out = m.bank[u][:, l * 256:l * 256 + width]
                                    moving = rows[:, slot, 0, s, c]
                                else:
                                    out = m.bank[u][:, l * 256:l * 256 + width].rearrange("p (a x) -> p a x", a=pages)
                                    moving = rows[:, slot, :, s, c].rearrange("p a k n -> p a (k n)")
                                last = nc.tensor.matmul(out, w1[:, c, l, s, f * P:(f + 1) * P], moving,
                                                        start=s == 0, stop=s == PAIRS - 1)
                        last.then_inc(product_done, 1)
                for c in range(2):
                    pe.wait_ge(hidden_ready, n * UNITS + 2 * (c + 1))
                    pe.wait_ge(blocks_kept, n * 2 + (c + 1))
                    for k in range(KVH):
                        for f in range(2):
                            if c == 0:
                                last = nc.tensor.matmul(m.bank[4][:, 0:n_half], m.w2_k[:, f, k],
                                                        hidden[:, 0, f, k], start=k == 0 and f == 0,
                                                        stop=k == 1 and f == 1)
                            else:
                                last = nc.tensor.matmul(m.bank[5][0:n_half, k * HEAD:(k + 1) * HEAD],
                                                        hidden[:, 1, f, k], m.w2_v[:, f],
                                                        start=f == 0, stop=f == 1)
                    last.then_inc(blocks_done, 1)

            over_sequences(pe, work)

        @block.vector
        def _(dve):
            nc.vector.memset(high[:], 0.0).then_inc(zeroed, 1)
            if prompt:
                dve.wait_ge(bias_done, 1)
                nc.vector.tensor_copy(m.hidden_bias[:], m.bank[7][:, 0:4]).then_inc(bias_kept, 1)
                for c in range(2):
                    for k in range(KVH):
                        dve.wait_ge(turned, 2 * c + k + 1)
                        nc.vector.tensor_copy(rows[:, 0, 0, :, c, k],
                                              m.bank[2 * c + k][:].rearrange("p (s n) -> p s n", s=PAIRS)).then_inc(rows_kept, 1)

            def work(n, slot):
                for u in range(UNITS):
                    dve.wait_ge(high_kept, n * UNITS + u + 1)
                    for k in range(KVH):
                        low = m.bank[u][:, 0:width].rearrange("p (a k n) -> p a k n", a=pages, k=KVH)[:, :, k]
                        last = nc.vector.tensor_tensor(
                            before[:, u % 2, k].rearrange("p (a n) -> p a n", a=pages), low,
                            high[:, k, 1:n_half + 1].rearrange("p (a n) -> p a n", a=pages), ALU.add)
                    last.then_inc(sum_ready, 1)

            over_sequences(dve, work)

        @block.scalar
        def _(act):
            act.sem_inc(blocks_kept, 2)
            act.wait_ge(zeroed, 1)
            if prompt:
                act.wait_ge(bias_kept, 1)

            def work(n, slot):
                for u in range(UNITS):
                    act.wait_ge(product_done, n * UNITS + u + 1)
                    for k in range(KVH):
                        part = m.bank[u][:, 256:256 + width].rearrange("p (a k n) -> p a k n", a=pages, k=KVH)[:, :, k]
                        last = nc.scalar.activation(high[:, k, 0:n_half].rearrange("p (a n) -> p a n", a=pages), part,
                                                    ACT.Copy)
                    last.then_inc(high_kept, 1)
                    act.wait_ge(sum_ready, n * UNITS + u + 1)
                    nc.scalar.activation(hidden[:, u // 2, u % 2], before[:, u % 2], ACT.Silu,
                                         bias=m.hidden_bias[:, u:u + 1]).then_inc(hidden_ready, 1)
                act.wait_ge(blocks_done, n * 2 + 1)
                target = m.kc_prompt[:, 0:n_half] if prompt else m.kc_cache[:, bass.ds(n, 1)].rearrange("p a n -> p (a n)")
                nc.scalar.activation(target, m.bank[4][:, 0:n_half], ACT.Copy).then_inc(blocks_kept, 1)
                act.wait_ge(blocks_done, n * 2 + 2)
                target = m.vc_prompt[0:n_half] if prompt else m.vc_cache[:, bass.ds(n, 1)].rearrange("p a n -> p (a n)")
                nc.scalar.activation(target, m.bank[5][0:n_half, 0:P], ACT.Copy).then_inc(blocks_kept, 1)

            over_sequences(act, work)


def gates_sigmoid(nc, m):
    with ExitStack() as stack:
        sem = phase(nc, stack)
        done = sem("gates_done")
        block = stack.enter_context(nc.Block())

        @block.scalar
        def _(act):
            nc.scalar.activation(m.gates[:], m.kv_b[:, 0:QT, 256:280], ACT.Sigmoid).then_inc(done, 1)


def prompt_items():
    items = []
    for k in range(KVH):
        for i in range(QT):
            items.append((k, i, "cmp", 0, 1))
            items.append((k, i, "slc", 0, i + 1))
            first = max(0, i - WINDOW // P)
            items.append((k, i, "win", first, i + 1 - first))
    return items


def prompt_attention(nc, m):
    with ExitStack() as stack:
        sem = phase(nc, stack)

        def sb(name, shape):
            return stack.enter_context(nc.sbuf_tensor(name, shape, F32))

        items = prompt_items()
        N = len(items)
        turns = QT + 1
        query = sb("query_pair", [P, SEQ])
        gate = sb("gate_pair", [P, QT, KVH, 3])
        probs = sb("probs", [P, 2, SEQ])
        probs_t = sb("probs_turned", [P, 2, QT, P])
        out = sb("out_pair", [P, QT, KVH, HEAD])
        top, bias, total = sb("score_max", [P, 2]), sb("exp_bias", [P, 2]), sb("exp_total", [P, 4])
        coefficient = sb("branch_coefficient", [P, 4])
        causal, beyond = sb("causal_add", [P, P]), sb("window_add", [P, P])
        cmp_add, cmp_keep = sb("cmp_add_sb", [P, 119]), sb("cmp_keep_sb", [P, 119])
        masks_in = sem("attention_masks_in")
        cleared = sem("probs_cleared")
        staged = sem("pair_staged")
        scores_done = sem("scores_done")
        masked = sem("scores_masked")
        max_ready = sem("max_ready")
        bias_ready = sem("exp_bias_ready")
        probs_ready = sem("probs_ready")
        probs_masked = sem("probs_masked")
        turned = sem("probs_turned_done")
        kept_act = sem("turned_kept_by_scalar")
        kept_dve = sem("turned_kept_by_vector")
        product_done = sem("value_product_done")
        inverse_ready = sem("inverse_total_ready")
        coefficient_ready = sem("coefficient_ready")
        combined = sem("branch_combined")
        written = sem("pair_written")
        block = stack.enter_context(nc.Block())
        NCMP = sum(1 for x in items if x[2] == "cmp")

        def width(item):
            return N_CMP_P if item[2] == "cmp" else item[4] * P

        @block.sync
        def _(sp):
            for target, source in ((causal, m.dram["causal_add"]), (beyond, m.dram["window_add"]), (cmp_add, m.dram["cmp_add"]),
                                   (cmp_keep, m.dram["cmp_keep"])):
                sp.dma_start(target[:], source).then_inc(masks_in, 16)

        @block.tensor
        def _(pe):
            def scores(j, n):
                k, i, branch, first, tiles = items[n]
                if n >= 2:
                    pe.wait_ge(probs_ready, j * N + (n - 1))
                half = slice(k * HEAD, (k + 1) * HEAD)
                lhs = query[half, i * P:(i + 1) * P]
                pair = m.pair[n % 2]
                if branch == "cmp":
                    last = nc.tensor.matmul(pair[:, 0:N_CMP_P], lhs, m.kc_prompt[half, 0:N_CMP_P], start=True, stop=True)
                else:
                    keys = m.k_slc if branch == "slc" else m.k_win
                    for a in range(0, tiles * P, 512):
                        b = min(a + 512, tiles * P)
                        last = nc.tensor.matmul(pair[:, a:b], lhs, keys[half, first * P + a:first * P + b],
                                                start=True, stop=True)
                last.then_inc(scores_done, 1)

            def turn(j, n):
                k, i, branch, first, tiles = items[n]
                if branch == "cmp":
                    pe.wait_ge(probs_masked, j * NCMP + sum(1 for x in items[:n] if x[2] == "cmp") + 1)
                else:
                    pe.wait_ge(probs_ready, j * N + n + 1)
                if n >= 1:
                    pe.wait_ge(kept_act, j * N + n)
                    pe.wait_ge(kept_dve, j * N + n)
                for t in range(tiles):
                    last = nc.tensor.transpose(m.turn_bank[t // 4][:, (t % 4) * P:(t % 4) * P + P],
                                               probs[:, n % 2, t * P:(t + 1) * P], m.identity[:])
                last.then_inc(turned, 1)

            def product(j, n):
                k, i, branch, first, tiles = items[n]
                pe.wait_ge(kept_act, j * N + n + 1)
                pe.wait_ge(kept_dve, j * N + n + 1)
                if n >= 2:
                    pe.wait_ge(combined, j * N + (n - 1))
                o = m.bank[6 + n % 2]
                for t in range(tiles):
                    if branch == "cmp":
                        lhs, rhs = probs_t[0:N_CMP_P, n % 2, 0], m.vc_prompt[0:N_CMP_P, k * HEAD:(k + 1) * HEAD]
                    else:
                        lhs = probs_t[:, n % 2, t]
                        v, at = (m.kv_a, 384) if branch == "slc" else (m.kv_b, 128)
                        rhs = v[:, first + t, at + k * HEAD:at + (k + 1) * HEAD]
                    last = nc.tensor.matmul(o[:, 0:HEAD], lhs, rhs, start=t == 0, stop=t == tiles - 1)
                last.then_inc(product_done, 1)

            with pe.Fori(0, GQA) as j:
                pe.wait_ge(staged, j * 2 + 2)
                scores(j, 0)
                for n in range(N + 1):
                    if n + 1 < N:
                        scores(j, n + 1)
                    if n < N:
                        turn(j, n)
                    if n >= 1:
                        product(j, n - 1)

        def keep_turned(copy, n, banks):
            tiles, c = items[n][4], min(P, width(items[n]))
            last = None
            for b in banks:
                t0, t1 = 4 * b, min(tiles, 4 * b + 4)
                if t0 < t1:
                    last = copy(probs_t[0:c, n % 2, t0:t1],
                                m.turn_bank[b][0:c, 0:(t1 - t0) * P].rearrange("p (t q) -> p t q", q=P))
            return last

        @block.scalar
        def _(act):
            def copy(to, source):
                return nc.scalar.activation(to, source, ACT.Copy)

            act.wait_ge(cleared, 1)
            with act.Fori(0, GQA) as j:
                for n in range(N + 1):
                    if n < N:
                        act.wait_ge(bias_ready, j * N + n + 1)
                        if n >= 2:
                            act.wait_ge(turned, j * N + (n - 1))
                            
                        w = width(items[n])
                        nc.scalar.activation(probs[:, n % 2, 0:w], m.pair[n % 2][:, 0:w], ACT.Exp, scale=SCALE,
                                             bias=bias[:, n % 2:n % 2 + 1],
                                             accum_out=total[:, n % 4:n % 4 + 1]).then_inc(probs_ready, 1)
                    if n >= 1:
                        act.wait_ge(turned, j * N + n)
                        if n >= 3:
                            act.wait_ge(product_done, j * N + (n - 2))
                        last = keep_turned(copy, n - 1, (1,) if items[n - 1][4] > 4 else ())
                        if last is not None:
                            last.then_inc(kept_act, 1)
                        else:
                            act.sem_inc(kept_act, 1)

        @block.vector
        def _(dve):
            nc.vector.memset(probs[:], 0.0).then_inc(cleared, 1)
            dve.wait_ge(masks_in, 4 * 16)
            MASKS = sum(2 if (x[2] == "win" and x[4] == 5) else 1 for x in items)

            def maximum(j, n, masks):
                k, i, branch, first, tiles = items[n]
                dve.wait_ge(scores_done, j * N + n + 1)
                pair, w = m.pair[n % 2], width(items[n])
                if branch == "cmp":
                    at = 56 - 8 * i
                    nc.vector.tensor_tensor(pair[:, 0:w], pair[:, 0:w], cmp_add[:, at:at + w], ALU.add).then_inc(masked, 1)
                    masks += 1
                else:
                    if branch == "win" and tiles == 5:
                        nc.vector.tensor_tensor(pair[:, 0:P], pair[:, 0:P], beyond[:], ALU.add).then_inc(masked, 1)
                        masks += 1
                    nc.vector.tensor_tensor(pair[:, w - P:w], pair[:, w - P:w], causal[:], ALU.add).then_inc(masked, 1)
                    masks += 1
                dve.wait_ge(masked, j * MASKS + masks)
                nc.vector.tensor_reduce(top[:, n % 2:n % 2 + 1], pair[:, 0:w], AX.X, ALU.max).then_inc(max_ready, 1)
                dve.wait_ge(max_ready, j * N + n + 1)
                if n >= 2:
                    dve.wait_ge(probs_ready, j * N + n - 1)
                nc.vector.tensor_scalar(bias[:, n % 2:n % 2 + 1], top[:, n % 2:n % 2 + 1], -SCALE, None,
                                        ALU.mult).then_inc(bias_ready, 1)
                return masks

            def keep(j, n):
                if items[n][2] == "cmp":
                    i = items[n][1]
                    at = 56 - 8 * i
                    dve.wait_ge(probs_ready, j * N + n + 1)
                    nc.vector.tensor_tensor(probs[:, n % 2, 0:N_CMP_P], probs[:, n % 2, 0:N_CMP_P],
                                            cmp_keep[:, at:at + N_CMP_P], ALU.mult).then_inc(probs_masked, 1)
                dve.wait_ge(turned, j * N + n + 1)
                if n >= 2:
                    dve.wait_ge(product_done, j * N + (n - 1))
                keep_turned(nc.vector.tensor_copy, n, (0,)).then_inc(kept_dve, 1)

            def combine(j, n):
                k, i, branch, first, tiles = items[n]
                r = {"cmp": 0, "slc": 1, "win": 2}[branch]
                c = coefficient[:, n % 4:n % 4 + 1]
                nc.vector.reciprocal(c, total[:, n % 4:n % 4 + 1]).then_inc(inverse_ready, 1)
                dve.wait_ge(inverse_ready, j * N + n + 1)
                nc.vector.tensor_tensor(c, c, gate[:, i, k, r:r + 1], ALU.mult).then_inc(coefficient_ready, 1)
                dve.wait_ge(coefficient_ready, j * N + n + 1)
                dve.wait_ge(product_done, j * N + n + 1)
                o = m.bank[6 + n % 2][:, 0:HEAD]
                if r == 0:
                    nc.vector.tensor_scalar(out[:, i, k], o, c, None, ALU.mult).then_inc(combined, 1)
                else:
                    dve.wait_ge(combined, j * N + n)
                    nc.vector.scalar_tensor_tensor(out=out[:, i, k], in0=o, scalar=c, in1=out[:, i, k],
                                                   op0=ALU.mult, op1=ALU.add).then_inc(combined, 1)

            with dve.Fori(0, GQA) as j:
                nc.vector.tensor_copy(query[:], m.q_a[:, bass.ds(j, 1), 0:SEQ].rearrange("p a t -> p (a t)")).then_inc(staged, 1)
                nc.vector.tensor_copy(gate[:].rearrange("p i k c -> p (i k) c"),
                                      m.gates[:].rearrange("p i (k g c) -> p (i k) g c", k=KVH, g=GQA)[:, :, bass.ds(j, 1), :]
                                      .rearrange("p i a c -> p i (a c)")).then_inc(staged, 1)
                dve.wait_ge(staged, j * 2 + 2)
                masks = 0
                for n in range(N + 2):
                    if n < N:
                        masks = maximum(j, n, masks)
                    if 1 <= n <= N:
                        keep(j, n - 1)
                    if n >= 2:
                        combine(j, n - 2)
                dve.wait_ge(combined, j * N + N)
                for k in range(KVH):
                    last = nc.vector.tensor_copy(
                        m.o_nsa[:, 0:QT].rearrange("p i (h d) -> p i h d", d=HEAD)[:, :, bass.ds(j + k * GQA, 1), :]
                        .rearrange("p i a d -> p i (a d)"), out[:, :, k])
                last.then_inc(written, 1)
                dve.wait_ge(written, j + 1)


def decode_attention(nc, m):
    with ExitStack() as stack:
        sem = phase(nc, stack)

        def sb(name, shape, dtype=F32):
            return stack.enter_context(nc.sbuf_tensor(name, shape, dtype))

        R = DEC * KVH * GQA
        KEYS = PAGES * PAGE
        KT = PAGES
        WT = WINDOW // P
        query = sb("decode_q", [P, DEC, R])
        ring = sb("decode_ring", [P, 2, KEYS + WINDOW])
        slc, win, cmp = sb("slc_scores", [R, KEYS + 1]), sb("win_scores", [R, WINDOW + 1]), sb("cmp_scores", [R, P])
        small = sb("decode_small", [R, 32])
        folded = sb("block_probs", [R, 136])
        importance, rank, barred = sb("importance", [R, N_SEL]), sb("rank", [R, N_SEL]), sb("barred", [R, N_SEL])
        new_probs = sb("new_probs", [R, 2, DEC])
        gate = sb("decode_gate", [R, 3])
        coefficient = sb("decode_coefficient", [R, 2, 3])
        group_sum, own = sb("group_sum_sb", [R, R]), sb("own_column_sb", [R, DEC])
        win_t, cmp_t = sb("win_probs_turned", [P, WT, DEC, R]), sb("cmp_probs_turned", [P, DEC, R])
        new_t = sb("new_probs_turned", [DEC, 2, R])
        out = sb("decode_out", [R, HEAD])
        slc_t = m.xn[:].rearrange("p c t -> p (c t)")[:, 0:KT * DEC * R].rearrange("p (t b r) -> p t b r", t=KT, b=DEC)
        spare = m.q_a[:].rearrange("p c t -> p (c t)")
        SS = N_SEL * N_SEL
        earlier, greater, equal = (spare[0:R, a * SS:(a + 1) * SS].rearrange("r (s u) -> r s u", s=N_SEL) for a in range(3))
        small_in = sem("decode_small_in")
        mask_in = sem("earlier_mask_in")
        cleared = sem("decode_cleared")
        query_ready = sem("decode_query_ready")
        k_in = [sem(f"decode_keys_in{s}") for s in range(2)]
        v_in = [sem(f"decode_values_in{s}") for s in range(2)]
        keys_read = sem("decode_keys_read")
        scores_done = sem("decode_scores_done")
        scores_kept = sem("decode_scores_kept")
        step_done = sem("decode_step")
        exp_done = sem("decode_exp_done")
        cmp_probs_ready = sem("cmp_probs_ready")
        imp_done = sem("importance_product_done")
        bars_ready = sem("bias_ready")
        probs_ready = sem("decode_probs_ready")
        turned = sem("decode_turned")
        turned_kept = sem("decode_turned_kept")
        values_read = sem("decode_values_read")
        products_done = sem("decode_products_done")
        stored, returned = sem("decode_out_stored"), sem("decode_out_returned")
        out_ready = sem("decode_out_ready")
        block = stack.enter_context(nc.Block())

        def load_pages(sp, cache, part, width, b, s, arrived):
            with sp.Fori(0, PAGES) as p:
                page = sp.value_load(m.table[0:1, bass.ds(p + b * PAGES, 1)], min_val=0, max_val=POOL - 1)
                sp.dma_start(ring[:, s, bass.ds(p * P, P)],
                             cache[bass.ds(page, 1)].rearrange("a p f -> p (a f)")).then_inc(arrived, 16)

        @block.sync
        def _(sp):
            sp.dma_start(gate[:], m.dram["gate_rows"].rearrange("b h c -> (b h) c")).then_inc(small_in, 16)
            sp.dma_start(group_sum[:], m.dram["group_sum"]).then_inc(small_in, 16)
            sp.dma_start(own[:], m.dram["own_column"]).then_inc(small_in, 16)
            for b in range(DEC):
                s = b % 2
                if b >= 2:
                    sp.wait_ge(keys_read, b - 1)
                load_pages(sp, m.dram["slc_k"], 0, P, b, s, k_in[s])
                sp.dma_start(ring[:, s, KEYS:], m.dram["win_k"][b]).then_inc(k_in[s], 16)
            sp.wait_ge(query_ready, 2)
            sp.dma_start(spare[0:R, 0:SS], m.dram["earlier"]).then_inc(mask_in, 16)
            for b in range(DEC):
                s = b % 2
                if b < 2:
                    sp.wait_ge(keys_read, DEC - 1 + s)
                else:
                    sp.wait_ge(values_read, b - 1)
                load_pages(sp, m.dram["slc_v"], 0, P, b, s, v_in[s])
                sp.dma_start(ring[:, s, KEYS:], m.dram["win_v"][b]).then_inc(v_in[s], 16)
            sp.wait_ge(out_ready, 1)
            sp.dma_start(m.dram["o_rows"], out[:]).then_inc(stored, 16)
            sp.wait_ge(stored, 16)
            sp.dma_start(m.o_nsa[0:DEC, 8], m.dram["o_rows"].rearrange("(b h) d -> b (h d)", b=DEC)).then_inc(returned, 16)
            sp.wait_ge(returned, 16)

        @block.gpsimd
        def _(pool):
            nc.gpsimd.memset(slc_t, 0.0).then_inc(cleared, 1)
            nc.gpsimd.memset(win_t[:], 0.0).then_inc(cleared, 1)
            nc.gpsimd.memset(cmp_t[:], 0.0).then_inc(cleared, 1)

        @block.tensor
        def _(pe):
            pe.wait_ge(query_ready, 2)
            for b in range(DEC):
                pe_last = nc.tensor.matmul(m.bank[5][0:R, 0:N_CMP_D], query[:, b], m.kc_cache[:, b, 0:N_CMP_D],
                                           start=b == 0, stop=b == DEC - 1)
            for n, keys in enumerate((m.k_slc, m.k_win)):
                for b in range(DEC):
                    pe_last = nc.tensor.matmul(m.bank[5][0:R, P + n:P + n + 1], query[:, b], keys[:, SEQ + b:SEQ + b + 1],
                                               start=b == 0, stop=b == DEC - 1)
            pe_last.then_inc(scores_done, 1)
            for b in range(DEC):
                s = b % 2
                pe.wait_ge(k_in[s], 16 * (PAGES + 1) * (b // 2 + 1))
                for a in range(5):
                    last = nc.tensor.matmul(m.bank[a][0:R, :], query[:, b], ring[:, s, a * 512:(a + 1) * 512],
                                            start=b == 0, stop=b == DEC - 1, skip_group_check=True)
                last.then_inc(keys_read, 1)
            pe.wait_ge(cmp_probs_ready, 1)
            nc.tensor.matmul(m.bank[6][0:R, 0:N_CMP_D], group_sum[:], cmp[:, 0:N_CMP_D],
                             start=True, stop=True).then_inc(imp_done, 1)
            pe.wait_ge(probs_ready, 1)
            for t in range(KT):
                nc.tensor.transpose(m.bank[t // 8][:, (t % 8) * R:(t % 8 + 1) * R], slc[:, t * P:(t + 1) * P],
                                    m.identity[0:R, 0:R])
            for t in range(WT):
                nc.tensor.transpose(m.bank[2][:, t * R:(t + 1) * R], win[:, t * P:(t + 1) * P], m.identity[0:R, 0:R])
            nc.tensor.transpose(m.bank[2][0:N_CMP_D, WT * R:(WT + 1) * R], cmp[:, 0:N_CMP_D], m.identity[0:R, 0:R])
            for n in range(2):
                last = nc.tensor.transpose(m.bank[3][0:DEC, n * R:(n + 1) * R], new_probs[:, n], m.identity[0:R, 0:R])
            last.then_inc(turned, 1)
            pe.wait_ge(turned_kept, 1)
            for b in range(DEC):
                nc.tensor.matmul(m.bank[5][0:R, 0:P], cmp_t[0:N_CMP_D, b], m.vc_cache[0:N_CMP_D, b],
                                 start=b == 0, stop=b == DEC - 1)
            nc.tensor.matmul(m.bank[6][0:R, 0:P], new_t[:, 0], m.kv_a[0:DEC, 8, 384:512], start=True, stop=False,
                             skip_group_check=True)
            nc.tensor.matmul(m.bank[7][0:R, 0:P], new_t[:, 1], m.kv_b[0:DEC, 8, 128:256], start=True, stop=False,
                             skip_group_check=True)
            for b in range(DEC):
                s = b % 2
                pe.wait_ge(v_in[s], 16 * (PAGES + 1) * (b // 2 + 1))
                for t in range(KT):
                    nc.tensor.matmul(m.bank[6][0:R, 0:P], slc_t[:, t, b], ring[:, s, t * P:(t + 1) * P],
                                     start=False, stop=b == DEC - 1 and t == KT - 1, skip_group_check=True)
                for t in range(WT):
                    last = nc.tensor.matmul(m.bank[7][0:R, 0:P], win_t[:, t, b],
                                            ring[:, s, KEYS + t * P:KEYS + (t + 1) * P],
                                            start=False, stop=b == DEC - 1 and t == WT - 1, skip_group_check=True)
                last.then_inc(values_read, 1)

        @block.scalar
        def _(act):
            act.wait_ge(small_in, 48)
            nc.scalar.activation(gate[:], gate[:], ACT.Sigmoid).then_inc(exp_done, 1)
            for n, scores in enumerate((cmp[:, 0:N_CMP_D], win[:], slc[:])):
                act.wait_ge(bars_ready, n + 1)
                nc.scalar.activation(scores, scores, ACT.Exp, scale=SCALE, bias=small[:, 3 + n:4 + n],
                                     accum_out=small[:, 6 + n:7 + n]).then_inc(exp_done, 1)

        @block.vector
        def _(dve):
            step = Chain(dve, step_done)
            step(nc.vector.memset(query[:], 0.0))
            for k in range(KVH):
                half = slice(k * HEAD, (k + 1) * HEAD)
                flat = query[half].rearrange("p b r -> p (b r)")
                for g in range(GQA):
                    at = k * GQA + g
                    last = nc.vector.tensor_copy(flat[:, at:at + (DEC - 1) * 72 + 1:72], m.q_a[half, g, SEQ:T])
                last.then_inc(query_ready, 1)
            dve.wait_ge(scores_done, 1)
            step(nc.vector.tensor_copy(cmp[:, 0:N_CMP_D], m.bank[5][0:R, 0:N_CMP_D]))
            step(nc.vector.tensor_copy(slc[:, KEYS:], m.bank[5][0:R, P:P + 1]))
            step(nc.vector.tensor_copy(win[:, WINDOW:], m.bank[5][0:R, P + 1:P + 2]))

            def exp_bias(n, scores):
                step(nc.vector.tensor_reduce(small[:, n:n + 1], scores, AX.X, ALU.max))
                nc.vector.tensor_scalar(small[:, 3 + n:4 + n], small[:, n:n + 1], -SCALE, None,
                                        ALU.mult).then_inc(bars_ready, 1)

            exp_bias(0, cmp[:, 0:N_CMP_D])
            dve.wait_ge(exp_done, 2)
            step(nc.vector.reciprocal(small[:, 9:10], small[:, 6:7]))
            nc.vector.tensor_scalar(cmp[:, 0:N_CMP_D], cmp[:, 0:N_CMP_D], small[:, 9:10], None,
                                    ALU.mult).then_inc(cmp_probs_ready, 1)
            step(nc.vector.memset(folded[:], 0.0))
            dve.wait_ge(imp_done, 1)
            step(nc.vector.tensor_copy(folded[:, 1:1 + N_CMP_D], m.bank[6][0:R, 0:N_CMP_D]))
            step(nc.vector.tensor_reduce(importance[:], folded[:, 0:4 * N_SEL].rearrange("r (s u) -> r s u", u=4),
                                         AX.X, ALU.add))
            step(nc.vector.tensor_tensor(importance[:], importance[:], folded[:, 4:4 * N_SEL + 1:4], ALU.add))
            step(nc.vector.memset(importance[:, 0:1], FORCED))
            step(nc.vector.memset(importance[:, N_SEL - 2:N_SEL], FORCED))
            dve.wait_ge(mask_in, 16)
            mine = importance[:].rearrange("r (s a) -> r s a", a=1).to_broadcast([R, N_SEL, N_SEL])
            other = importance[:].rearrange("r (a u) -> r a u", a=1).to_broadcast([R, N_SEL, N_SEL])
            step(nc.vector.tensor_tensor(greater, other, mine, ALU.is_gt))
            step(nc.vector.tensor_tensor(equal, other, mine, ALU.is_equal))
            step(nc.vector.tensor_tensor(equal, equal, earlier, ALU.mult))
            step(nc.vector.tensor_tensor(greater, greater, equal, ALU.add))
            step(nc.vector.tensor_reduce(rank[:], greater, AX.X, ALU.add))
            step(nc.vector.tensor_scalar(barred[:], rank[:], float(TOPK), None, ALU.is_ge))
            step(nc.vector.tensor_scalar(barred[:], barred[:], NEG, None, ALU.mult))
            dve.wait_ge(keys_read, DEC)
            step(nc.vector.tensor_copy(win[:, 0:WINDOW], m.bank[4][0:R, :]))
            step(nc.vector.tensor_scalar(win[:, 0:1], win[:, 0:1], NEG, None, ALU.add))
            exp_bias(1, win[:])
            for a in range(4):
                blocks = 512 // 64
                step(nc.vector.tensor_tensor(
                    slc[:, a * 512:(a + 1) * 512].rearrange("r (s u) -> r s u", u=64),
                    m.bank[a][0:R, :].rearrange("r (s u) -> r s u", u=64),
                    barred[:, a * blocks:(a + 1) * blocks].rearrange("r (s a) -> r s a", a=1).to_broadcast([R, blocks, 64]),
                    ALU.add))
            step(nc.vector.tensor_tensor(slc[:, KEYS:], slc[:, KEYS:], barred[:, N_SEL - 1:N_SEL], ALU.add))
            exp_bias(2, slc[:])
            dve.wait_ge(small_in, 48)
            dve.wait_ge(exp_done, 4)
            step(nc.vector.tensor_scalar(new_probs[:, 0], own[:], slc[:, KEYS:], None, ALU.mult))
            step(nc.vector.reciprocal(small[:, 10:12], small[:, 7:9]))
            nc.vector.tensor_scalar(new_probs[:, 1], own[:], win[:, WINDOW:], None, ALU.mult).then_inc(probs_ready, 1)
            for k in range(2):
                head = m.vectors[0:R, V_HEAD0 + k:V_HEAD0 + k + 1]
                step(nc.vector.tensor_scalar(coefficient[:, k], gate[:], head, None, ALU.mult))
                step(nc.vector.tensor_scalar(coefficient[:, k, 1:2], coefficient[:, k, 1:2], small[:, 11:12], None, ALU.mult))
                step(nc.vector.tensor_scalar(coefficient[:, k, 2:3], coefficient[:, k, 2:3], small[:, 10:11], None, ALU.mult))
            dve.wait_ge(turned, 1)
            dve.wait_ge(cleared, 3)

            for t in range(KT):
                flat = slc_t[:, t].rearrange("p b r -> p (b r)")
                nc.vector.tensor_copy(spread(flat, P), m.bank[t // 8][:, (t % 8) * R:(t % 8 + 1) * R]
                                      .rearrange("p (b h) -> p b h", b=DEC))
            for t in range(WT):
                nc.vector.tensor_copy(spread(win_t[:, t].rearrange("p b r -> p (b r)"), P),
                                      m.bank[2][:, t * R:(t + 1) * R].rearrange("p (b h) -> p b h", b=DEC))
            nc.vector.tensor_copy(spread(cmp_t[0:N_CMP_D].rearrange("p b r -> p (b r)"), N_CMP_D),
                                  m.bank[2][0:N_CMP_D, WT * R:(WT + 1) * R].rearrange("p (b h) -> p b h", b=DEC))
            nc.vector.tensor_copy(new_t[:].rearrange("b n r -> b (n r)"), m.bank[3][0:DEC, 0:2 * R]).then_inc(turned_kept, 1)
            dve.wait_ge(values_read, DEC)
            for n in range(3):
                for k in range(2):
                    source = m.bank[5 + n][0:R, k * HEAD:(k + 1) * HEAD]
                    c = coefficient[:, k, n:n + 1]
                    if n == 0 and k == 0:
                        step(nc.vector.tensor_scalar(out[:], source, c, None, ALU.mult))
                    else:
                        step(nc.vector.scalar_tensor_tensor(out=out[:], in0=source, scalar=c, in1=out[:],
                                                            op0=ALU.mult, op1=ALU.add))
            nc.vector.tensor_copy(out[:], out[:]).then_inc(out_ready, 1)


def spread(flat, partitions):
    R = DEC * KVH * GQA
    wide = flat.rearrange("p (b r) -> p b r", b=DEC)
    first = wide[:, 0:1, 0:8]
    return bass.AP(tensor=first.tensor, offset=first.offset, ap=[list(first.ap[0]), [R + 8, DEC], [1, 8]])


def mix_features(nc, m):
    with ExitStack() as stack:
        sem = phase(nc, stack)
        squares = stack.enter_context(nc.sbuf_tensor("row_squares", [P, 512], F32))
        sums = stack.enter_context(nc.sbuf_tensor("mix_sums", [P, 9, 5], F32))
        ready = sem("mix_sums_clear")
        summed = sem("mix_summed")
        rooted = sem("mix_rooted")
        inverted = sem("mix_inverted")
        scaled = sem("mix_scaled")
        turned = sem("mix_turned")
        kept_act, kept_dve = sem("mix_kept_by_scalar"), sem("mix_kept_by_vector")
        block = stack.enter_context(nc.Block())

        @block.scalar
        def _(act):
            act.wait_ge(ready, 1)
            for i, (first, count) in enumerate(TILES):
                act_step = 0
                nc.scalar.activation(squares[0:count], m.o_nsa[0:count, i], ACT.Square,
                                     accum_out=sums[0:count, i, 0:1]).then_inc(summed, 1)
                act.wait_ge(summed, 5 * i + 1)
                for h in range(HGH):
                    nc.scalar.activation(squares[0:count, h * P:(h + 1) * P], m.v_hg[0:count, i, h * P:(h + 1) * P],
                                         ACT.Square, accum_out=sums[0:count, i, 1 + h:2 + h]).then_inc(summed, 1)
                act.wait_ge(summed, 5 * i + 5)
            eps = m.vectors[:, V_EPS:V_EPS + 1]
            nc.scalar.activation(sums[:, :, 0], sums[:, :, 0], ACT.Sqrt, scale=1.0 / NSA, bias=eps).then_inc(rooted, 1)
            nc.scalar.activation(sums[:, :, 1:5], sums[:, :, 1:5], ACT.Sqrt, scale=1.0 / P, bias=eps).then_inc(rooted, 1)
            for i, (first, count) in enumerate(TILES):
                act.wait_ge(turned, 2 * i + 1)
                for c in range(4):
                    last = nc.scalar.activation(m.xn[:, c, first:first + count],
                                                m.bank[2 * (i % 2)][:, c * P:c * P + count], ACT.Copy,
                                                scale=m.vectors[:, V_NSA + c:V_NSA + c + 1])
                last.then_inc(kept_act, 1)

        @block.vector
        def _(dve):
            nc.vector.memset(sums[:], 1.0).then_inc(ready, 1)
            dve.wait_ge(rooted, 2)
            nc.vector.reciprocal(sums[:], sums[:]).then_inc(inverted, 1)
            dve.wait_ge(inverted, 1)

            def scale(i):
                count = TILES[i][1]
                nc.vector.tensor_scalar(m.o_nsa[0:count, i], m.o_nsa[0:count, i], sums[0:count, i, 0:1], None, ALU.mult)
                v = m.v_hg[0:count, i].rearrange("p (h d) -> p h d", h=HGH)
                nc.vector.tensor_tensor(v, v, sums[0:count, i, 1:5].rearrange("p (h a) -> p h a", a=1)
                                        .to_broadcast([count, HGH, P]), ALU.mult).then_inc(scaled, 1)

            scale(0)
            for i, (first, count) in enumerate(TILES):
                if i + 1 < 9:
                    scale(i + 1)
                dve.wait_ge(turned, 2 * i + 2)
                for c in range(4):
                    last = nc.vector.scalar_tensor_tensor(
                        out=m.xn[:, 4 + c, first:first + count], in0=m.bank[2 * (i % 2) + 1][:, c * P:c * P + count],
                        scalar=m.vectors[:, V_HG + c:V_HG + c + 1], in1=m.gate_b[:, c, first:first + count],
                        op0=ALU.mult, op1=ALU.mult)
                last.then_inc(kept_dve, 1)

        @block.tensor
        def _(pe):
            for i, (first, count) in enumerate(TILES):
                pe.wait_ge(scaled, i + 1)
                if i >= 2:
                    pe.wait_ge(kept_act, i - 1)
                    pe.wait_ge(kept_dve, i - 1)
                for n, source in enumerate((m.o_nsa, m.v_hg)):
                    for c in range(4):
                        last = nc.tensor.transpose(m.bank[2 * (i % 2) + n][:, c * P:c * P + count],
                                                   source[0:count, i, c * P:(c + 1) * P], m.identity[0:count, 0:count])
                    last.then_inc(turned, 1)


def add_linear(nc, m, name, weights, source, chunks_in):
    with ExitStack() as stack:
        sem = phase(nc, stack)
        ring = stack.enter_context(nc.sbuf_tensor(f"{name}_weights", [P, 2, chunks_in, P], F32))
        arrived = [sem(f"{name}_weights_in{s}") for s in range(2)]
        group_done = sem(f"{name}_group_done")
        group_added = sem(f"{name}_group_added")
        block = stack.enter_context(nc.Block())

        @block.sync
        def _(sp):
            for s in range(2):
                sp.dma_start(ring[:, s], weights[s]).then_inc(arrived[s], 16)
            with sp.Fori(1, KC // 2) as i:
                for s in range(2):
                    sp.wait_ge(group_done, (i * 2 + (s - 1)) * GROUPS)
                    sp.dma_start(ring[:, s], weights[i * 2 + s]).then_inc(arrived[s], 16)

        @block.tensor
        def _(pe):
            with pe.Fori(0, KC // 2) as i:
                for s in range(2):
                    pe.wait_ge(arrived[s], i * 16 + 16)
                    for g in range(GROUPS):
                        pe.wait_ge(group_added, (i * 2 + s) * GROUPS + (g + 1))
                        for k in range(chunks_in):
                            last = nc.tensor.matmul(m.bank[3 * s + g][:, 0:G], ring[:, s, k], source[:, k, cols(g)],
                                                    start=k == 0, stop=k == chunks_in - 1)
                        last.then_inc(group_done, 1)

        @block.vector
        def _(dve):
            dve.sem_inc(group_added, 2 * GROUPS)
            with dve.Fori(0, KC // 2) as i:
                for s in range(2):
                    for g in range(GROUPS):
                        dve.wait_ge(group_done, (i * 2 + s) * GROUPS + (g + 1))
                        h = m.h[:, bass.ds(i * 2 + s, 1), cols(g)].rearrange("p a t -> p (a t)")
                        nc.vector.tensor_tensor(h, m.bank[3 * s + g][:, 0:G], h, ALU.add).then_inc(group_added, 1)


def gated_pair(nc, m, name, weights, parts, chunks, function, finish):
    with ExitStack() as stack:
        sem = phase(nc, stack)
        total = sum(count for _, count in parts)
        ring = stack.enter_context(nc.sbuf_tensor(f"{name}_weights", [P, 2, total, P], F32))
        active = stack.enter_context(nc.sbuf_tensor(f"{name}_active", [P, GROUPS, G], F32))
        arrived = [sem(f"{name}_weights_in{s}") for s in range(2)]
        pair_done = sem(f"{name}_pair_done")
        active_ready = sem(f"{name}_active_ready")
        multiplied = sem(f"{name}_multiplied")
        finished = sem(f"{name}_finished")
        block = stack.enter_context(nc.Block())

        @block.sync
        def _(sp):
            for s in range(2):
                sp.dma_start(ring[:, s], weights[s]).then_inc(arrived[s], 16)
            with sp.Fori(1, chunks // 2) as i:
                for s in range(2):
                    sp.wait_ge(pair_done, (i * 2 + (s - 1)) * GROUPS)
                    sp.dma_start(ring[:, s], weights[i * 2 + s]).then_inc(arrived[s], 16)

        @block.tensor
        def _(pe):
            with pe.Fori(0, chunks // 2) as i:
                for s in range(2):
                    pe.wait_ge(arrived[s], i * 16 + 16)
                    for g in range(GROUPS):
                        pe.wait_ge(multiplied, (i * 2 + s) * GROUPS + (g + 1))
                        at = 0
                        for n, (source, count) in enumerate(parts):
                            for k in range(count):
                                last = nc.tensor.matmul(m.bank[2 * g + n][:, 0:G], ring[:, s, at + k],
                                                        source[:, k, cols(g)], start=k == 0, stop=k == count - 1)
                            at += count
                        last.then_inc(pair_done, 1)

        @block.scalar
        def _(act):
            with act.Fori(0, chunks // 2) as i:
                for s in range(2):
                    for g in range(GROUPS):
                        n = (i * 2 + s) * GROUPS + (g + 1)
                        act.wait_ge(pair_done, n)
                        act.wait_ge(multiplied, n)
                        nc.scalar.activation(active[:, g], m.bank[2 * g][:, 0:G], function).then_inc(active_ready, 1)

        @block.vector
        def _(dve):
            dve.sem_inc(multiplied, GROUPS)
            with dve.Fori(0, chunks // 2) as i:
                for s in range(2):
                    for g in range(GROUPS):
                        n = (i * 2 + s) * GROUPS + (g + 1)
                        dve.wait_ge(active_ready, n)
                        finish(dve, i * 2 + s, g, n, active[:, g], m.bank[2 * g + 1][:, 0:G], multiplied, finished)


def feed_forward(nc, m):
    def finish(dve, chunk, g, n, active, other, multiplied, finished):
        target = m.hidden[:, bass.ds(chunk, 1), cols(g)].rearrange("p a t -> p (a t)")
        nc.vector.tensor_tensor(target, other, active, ALU.mult).then_inc(multiplied, 1)

    gated_pair(nc, m, "ffn", m.dram["w_gate_up"], ((m.xn, KC), (m.xn, KC)), FC, ACT.Silu, finish)


def gated_embedding(nc, m):
    def finish(dve, chunk, g, n, active, other, multiplied, finished):
        nc.vector.tensor_tensor(m.embedded[:, g], other, active, ALU.mult).then_inc(multiplied, 1)
        dve.wait_ge(multiplied, n + GROUPS)
        h = m.h[:, bass.ds(chunk, 1), cols(g)].rearrange("p a t -> p (a t)")
        nc.vector.tensor_tensor(h, h, m.embedded[:, g], ALU.add).then_inc(finished, 1)

    gated_pair(nc, m, "ple", m.dram["w_ple"], ((m.xn, KC), (m.p_in, DPLE // P)), KC, ACT.Sigmoid, finish)


def load_residual(nc, m):
    with ExitStack() as stack:
        sem = phase(nc, stack)
        loaded = sem("residual_loaded")
        block = stack.enter_context(nc.Block())

        @block.sync
        def _(sp):
            sp.dma_start(m.h[:], m.dram["x"]).then_inc(loaded, 16)
            sp.dma_start(m.p_in[:], m.dram["p"]).then_inc(loaded, 16)
            sp.wait_ge(loaded, 32)


def store_result(nc, m):
    with ExitStack() as stack:
        sem = phase(nc, stack)
        stored = sem("result_stored")
        block = stack.enter_context(nc.Block())

        @block.sync
        def _(sp):
            sp.dma_start(m.dram["out_y"], m.xn[:]).then_inc(stored, 16)
            sp.wait_ge(stored, 16)


def load_inputs(nc, m, d):
    with ExitStack() as stack:
        sem = phase(nc, stack)
        loaded = sem("inputs_loaded")
        block = stack.enter_context(nc.Block())

        @block.sync
        def _(sp):
            pairs = ((m.identity, d["identity"]), (m.mean_weights, d["mean_weights"]), (m.vectors, d["vectors"]),
                     (m.intra_mask, d["intra_mask"]), (m.row_pick, d["row_pick"]), (m.xn, d["x"]))
            for target, source in pairs:
                sp.dma_start(target[:], source).then_inc(loaded, 16)
            sp.wait_ge(loaded, 16 * len(pairs))


def layer(nc, d):
    m = Tensors(d)
    with ExitStack() as stack:
        def sb(name, shape, dtype=F32):
            return stack.enter_context(nc.sbuf_tensor(name, shape, dtype))

        psum = stack.enter_context(nc.psum_tensor("banks", [P, 8 * 512], F32))
        m.bank = [psum[:, i * 512:(i + 1) * 512] for i in range(8)]
        m.pair = [psum[:, i * 1024:(i + 1) * 1024] for i in range(2)]
        m.turn_bank = m.bank[4:6]
        m.identity = sb("identity_sb", [P, P])
        m.mean_weights = sb("mean_weights_sb", [P, P])
        m.vectors = sb("vectors_sb", [P, V_COLS])
        m.lower = sb("lower_bound", [P, 20])
        m.intra_mask = sb("intra_mask_sb", [P, P])
        m.row_pick = sb("row_pick_sb", [DEC, DEC, P])
        m.table = sb("table", [1, DEC * PAGES], I32)
        m.xn = sb("xn", [P, KC, T])
        mixers(nc, m, d)
        m.h = sb("h", [P, KC, T])
        m.p_in = sb("p_in", [P, DPLE // P, T])
        load_residual(nc, m)
        add_linear(nc, m, "out", m.dram["w_out"], m.xn, KC)
        rms_norm_features(nc, m, "ffn", m.h, V_FFN, m.xn)
        with ExitStack() as ffn:
            m.hidden = ffn.enter_context(nc.sbuf_tensor("ffn_hidden", [P, FC, T], F32))
            feed_forward(nc, m)
            add_linear(nc, m, "down", m.dram["w_down"], m.hidden, FC)
        rms_norm_features(nc, m, "ple", m.h, V_PLE, m.xn)
        with ExitStack() as ple:
            m.embedded = ple.enter_context(nc.sbuf_tensor("embedded", [P, GROUPS, G], F32))
            gated_embedding(nc, m)
        rms_norm_features(nc, m, "final", m.h, V_FINAL, m.xn)
        store_result(nc, m)


def mixers(nc, m, d):
    with ExitStack() as stack:
        def sb(name, shape, dtype=F32):
            return stack.enter_context(nc.sbuf_tensor(name, shape, dtype))

        m.q_a = sb("q_a", [P, 4, T])
        m.k_slc = sb("k_slc_t", [P, T])
        m.k_win = sb("k_win_t", [P, T])
        m.kv_a = sb("kv_a", [P, 9, 512])
        m.kv_b = sb("kv_b", [P, 9, 280])
        m.v_hg = sb("v_hg", [P, 9, 512])
        m.gate_b = sb("gate_b", [P, 4, T])
        load_inputs(nc, m, d)
        lower_bound(nc, m)
        rms_norm_features(nc, m, "mix", m.xn, V_MIX, m.xn)
        with ExitStack() as recurrent:
            m.q_b = recurrent.enter_context(nc.sbuf_tensor("q_b", [P, 4, T], F32))
            m.forget = recurrent.enter_context(nc.sbuf_tensor("forget", [P, 4, T], F32))
            project_features(nc, m)
            project_tokens(nc, m)
            hgrn_prompt(nc, m)
            hgrn_decode(nc, m)
        m.kc_prompt, m.vc_prompt = sb("kc_prompt", [P, 64]), sb("vc_prompt", [64, P])
        m.kc_cache, m.vc_cache = sb("kc_cache", [P, DEC, P]), sb("vc_cache", [P, DEC, P])
        with ExitStack() as compression:
            def csb(name, shape):
                return compression.enter_context(nc.sbuf_tensor(name, shape, F32))

            m.w2_k, m.w2_v = csb("w2_k", [P, 2, KVH, P]), csb("w2_v", [P, 2, HEAD])
            m.pos, m.hidden_bias = csb("pos", [P, 2, 2, PAIRS]), csb("hidden_bias", [P, 4])
            compress(nc, m, True)
            compress(nc, m, False)
        m.o_nsa = sb("o_nsa", [P, 9, NSA])
        with ExitStack() as attention:
            m.gates = attention.enter_context(nc.sbuf_tensor("gates", [P, QT, 24], F32))
            gates_sigmoid(nc, m)
            prompt_attention(nc, m)
        decode_attention(nc, m)
        mix_features(nc, m)
        clear_semaphores(nc)


def constants():
    f = np.float32
    s, t = np.arange(P)[:, None], np.arange(P)[None, :]
    c = {}
    c["identity"] = np.eye(P, dtype=f)
    c["mean_weights"] = np.full((P, P), 1.0 / DM, f)
    c["intra_mask"] = ((s // BLOCK32 == t // BLOCK32) & (s <= t)).astype(f)
    c["row_pick"] = np.repeat(np.eye(DEC, dtype=f)[:, :, None], P, axis=2)
    q, k = s, t
    c["causal_add"] = np.where(k > q, f(NEG), f(0))
    c["window_add"] = np.where(k <= q, f(NEG), f(0))
    keep = HALF * (np.arange(119)[None, :] - 56) + 31 <= s
    c["cmp_keep"] = keep.astype(f)
    c["cmp_add"] = np.where(keep, f(0), f(NEG))
    r = np.arange(DEC * KVH * GQA)
    c["group_sum"] = (r[:, None] // GQA == r[None, :] // GQA).astype(f)
    c["own_column"] = (r[:, None] // 8 == np.arange(DEC)[None, :]).astype(f)
    b = np.arange(N_SEL)
    c["earlier"] = np.tile((b[None, :] < b[:, None]).astype(f).reshape(1, -1), (len(r), 1))
    return c


def columns(v):
    return v.reshape(-1, P).T


def weight_chunks(w, order=None):
    k, n = w.shape
    return np.ascontiguousarray(w.reshape(k // P, P, n // P, P).transpose(2, 1, 0, 3))


def laid_out(i):
    a = {}
    x = np.concatenate([i["x_prompt"][0], i["x_sample"][:, 0]])
    a["x"] = np.ascontiguousarray(x.T.reshape(KC, P, T).transpose(1, 0, 2))
    w = i["w_in"][0]
    start = np.cumsum([0, 512, 256, 256, 256, 24, 512, 512, 512, 512])
    qa, kvc, kvs, kvw, gate, qb, fb, vb, gb = (w[:, start[n]:start[n + 1]] for n in range(9))
    qa = qa.reshape(DM, KVH, GQA, HEAD).transpose(0, 2, 1, 3).reshape(DM, NSA)
    a["w_feature"] = weight_chunks(np.concatenate([qa, qb, gb, fb], axis=1))
    gate = gate.reshape(DM, 3, KVH * GQA).transpose(0, 2, 1).reshape(DM, 24)
    token = np.concatenate([kvc, kvs, kvw, gate, vb], axis=1)
    a["w_token"] = np.ascontiguousarray(token.reshape(KC, P, -1).transpose(1, 0, 2))
    v = [i["norm_mix"][0], i["norm_nsa_out"][0], i["norm_hg_out"][0], i["norm_ffn"][0], i["norm_ple"][0],
         i["norm_final"], i["hg_lb"][0], i["hg_lb"][1]]
    extra = np.zeros((P, 3), np.float32)
    extra[:, 0] = 1e-6
    extra[:, 1] = np.arange(P) // 4 % 2 == 0
    extra[:, 2] = np.arange(P) // 4 % 2 == 1
    a["vectors"] = np.concatenate([np.ascontiguousarray(columns(x)) for x in v] + [extra], axis=1)
    a["window_rows"] = i["state_kv_win"][0].reshape(DEC, WINDOW, 256)
    a["state_hgrn"] = i["state_hgrn"][0]
    a["w_out"] = weight_chunks(i["w_out"][0])
    gate_up = i["w_gate_up"][0]
    a["w_gate_up"] = np.concatenate([weight_chunks(gate_up[:, :DFF]), weight_chunks(gate_up[:, DFF:])], axis=2)
    a["w_down"] = weight_chunks(i["w_down"][0])
    a["w_ple"] = np.concatenate([weight_chunks(i["w_ple_gate"][0]), weight_chunks(i["w_ple_proj"][0])], axis=2)
    p = np.concatenate([i["p_prompt"][0, 0], i["p_sample"][0, :, 0]])
    a["p"] = np.ascontiguousarray(p.T.reshape(DPLE // P, P, T).transpose(1, 0, 2))
    a["cmp_w1"] = np.ascontiguousarray(i["cmp_w1"][0].reshape(2, 2, PAIRS, P, HID).transpose(3, 0, 1, 2, 4))
    a["cmp_pos"] = np.ascontiguousarray(i["cmp_pos"][0].reshape(2, 2, PAIRS, P).transpose(3, 0, 1, 2))
    w2 = i["cmp_w2"][0].reshape(2, 2, P, HEAD)
    w2_k = np.zeros((P, 2, KVH, KVH, HEAD), np.float32)
    for k in range(KVH):
        w2_k[:, :, k, k] = w2[0].transpose(1, 0, 2)
    a["cmp_w2_k"] = w2_k.reshape(P, 2, KVH, P)
    a["cmp_w2_v"] = np.ascontiguousarray(w2[1].transpose(1, 0, 2))
    cache = i["cache_kv_cmp"][0].reshape(POOL, PAGE // HALF, PAIRS, 2, 2, KVH, HEAD)
    a["cache_cmp"] = np.ascontiguousarray(cache.transpose(0, 3, 6, 2, 4, 5, 1)).reshape(POOL, P, 256)
    cache = i["cache_kv_slc"][0].reshape(POOL, PAGE, 2, P)
    a["slc_k"] = np.ascontiguousarray(cache[:, :, 0].transpose(0, 2, 1))
    a["slc_v"] = np.ascontiguousarray(cache[:, :, 1])
    window = i["state_kv_win"][0].reshape(DEC, WINDOW, 2, P)
    a["win_k"] = np.ascontiguousarray(window[:, :, 0].transpose(0, 2, 1))
    a["win_v"] = np.ascontiguousarray(window[:, :, 1].reshape(DEC, 4, P, P).transpose(0, 2, 1, 3)).reshape(DEC, P, WINDOW)
    a["page_table"] = i["page_table"].reshape(1, -1)
    a.update(constants())
    return a


OUTPUTS = {
    "out_cmp_p": (SEQ, 256), "out_slc_p": (SEQ, 256), "out_win_p": (WINDOW, 256), "out_hgrn_p": (HGH, P, P),
    "out_cmp_s": (DEC, 256), "out_slc_s": (DEC, 256), "out_win_s": (DEC, WINDOW, 256),
    "out_hgrn_s": (DEC, HGH, P, P), "out_y": (P, KC, T),
}
SCRATCH = {"gate_rows": (DEC, 8, 3), "o_rows": (DEC * KVH * GQA, HEAD)}


def kernel(**inputs):
    import concourse.bacc as bacc
    from concourse.bass_utils import run_bass_kernel_spmd

    nc = bacc.Bacc("TRN2", target_bir_lowering=False, num_devices=1)
    arrays = {}
    handles = {}
    for name, a in laid_out({k: np.asarray(v) for k, v in inputs.items()}).items():
        arrays["in_" + name] = np.ascontiguousarray(a)
        handles[name] = nc.dram_tensor("in_" + name, a.shape, mybir.dt.from_np(a.dtype), kind="ExternalInput").ap()
    for name, shape in OUTPUTS.items():
        handles[name] = nc.dram_tensor(name, shape, F32, kind="ExternalOutput").ap()
    for name, shape in SCRATCH.items():
        handles[name] = nc.dram_tensor(name, shape, F32, kind="Internal").ap()
    layer(nc, handles)
    r = run_bass_kernel_spmd(nc, [arrays], core_ids=[0]).results[0]
    y = r["out_y"].transpose(1, 0, 2).reshape(DM, T).T
    kv = (2, KVH, HEAD)
    return (
        y[None, :SEQ], y[SEQ:, None],
        r["out_cmp_p"].reshape(1, 1, SEQ, *kv), r["out_slc_p"].reshape(1, 1, SEQ, *kv),
        r["out_win_p"].reshape(1, 1, WINDOW, *kv), r["out_hgrn_p"][None, None],
        r["out_cmp_s"].reshape(1, DEC, 1, *kv), r["out_slc_s"].reshape(1, DEC, 1, *kv),
        r["out_win_s"].reshape(1, DEC, WINDOW, *kv), r["out_hgrn_s"][None],
    )
```

```python
from contextlib import ExitStack

import concourse.bass as bass
import concourse.mybir as mybir
from concourse.alu_op_type import AluOpType as ALU
import numpy as np

ACT = mybir.ActivationFunctionType
F32 = mybir.dt.float32
I32 = mybir.dt.int32
F32R = mybir.dt.float32r
AX = mybir.AxisListType

P = 128
SEQ, DEC = 1024, 8
T = SEQ + DEC
GROUPS = 3
G = T // GROUPS
DM, DFF, DPLE = 1024, 2816, 256
KC = DM // P
FC = DFF // P
PAGES, PAGE, POOL = 16, 128, 160
HEAD, KVH, GQA = 64, 2, 4
NSA, HG, HGH = 512, 512, 4
WINDOW = 512
N_CMP_P, N_CMP_D = 63, 127
N_SEL = 33
TOPK = 16
SCALE = HEAD ** -0.5
NEG = -1e30
FORCED = 1e9
TILES = [(i * P, min(P, T - i * P)) for i in range(9)]
QT = SEQ // P
BLOCK32 = 32
TOK_GROUPS = ((0, 512), (512, 280), (792, 512))
V_MIX, V_NSA, V_HG, V_FFN, V_PLE, V_FINAL, V_LB, V_EPS = 0, 8, 12, 16, 24, 32, 40, 48
V_HEAD0, V_HEAD1, V_COLS = 49, 50, 51


class Chain:

    def __init__(self, engine, semaphore, count=0):
        self.engine, self.semaphore, self.count = engine, semaphore, count

    def __call__(self, instruction):
        instruction.then_inc(self.semaphore, 1)
        self.count = self.count + 1
        self.engine.wait_ge(self.semaphore, self.count)


class Tensors:

    def __init__(self, dram):
        self.dram = dram


class Overlay:

    def __init__(self, nc, start, size):
        self.nc, self.at, self.end = nc, start, start + size

    def __call__(self, name, shape, dtype=F32):
        tensor = self.nc.alloc_sbuf_tensor_at(name, shape, dtype, offset=self.at)
        self.at += 32 * -(-4 * int(np.prod(shape[1:])) // 32)
        assert self.at <= self.end
        return tensor


USED = []


def phase(nc, stack):
    def sem(name):
        USED.append(stack.enter_context(nc.semaphore(name)))
        return USED[-1]
    return sem


def clear_semaphores(nc):
    for semaphore in USED:
        nc.sync.sem_clear(semaphore)
    USED.clear()
    nc.all_engine_barrier()


def cols(group):
    return slice(group * G, (group + 1) * G)


def rms_norm_features(nc, m, name, source, gain, target, load=None):
    split = isinstance(target, tuple)
    with ExitStack() as stack:
        sem = phase(nc, stack)
        squares = stack.enter_context(nc.sbuf_tensor(f"{name}_squares", [P, 2, T], F32))
        total = stack.enter_context(nc.sbuf_tensor(f"{name}_total", [P, T], F32))
        scale = stack.enter_context(nc.sbuf_tensor(f"{name}_scale", [P, T], F32))
        squared = sem(f"{name}_squared")
        added = sem(f"{name}_added")
        mean_ready = sem(f"{name}_mean")
        root_ready = sem(f"{name}_root")
        inverted = sem(f"{name}_inverted")
        normed = sem(f"{name}_normed")
        high_ready = sem(f"{name}_high_ready")
        low_ready = sem(f"{name}_low_ready")
        block = stack.enter_context(nc.Block())

        @block.scalar
        def _(act):
            for c in range(KC):
                if c >= 2:
                    act.wait_ge(added, c - 1)
                nc.scalar.activation(squares[:, c % 2, :], source[:, c, :], ACT.Square).then_inc(squared, 1)
            for g in range(GROUPS):
                act.wait_ge(mean_ready, g + 1)
                nc.scalar.activation(scale[:, cols(g)], m.bank[g][:, 0:G], ACT.Sqrt,
                                     bias=m.vectors[:, V_EPS:V_EPS + 1]).then_inc(root_ready, 1)
            if split:
                for c in range(KC):
                    act.wait_ge(normed, c + 1)
                    nc.scalar.activation(target[0][:, c], squares[:, c % 2], ACT.Copy).then_inc(high_ready, 1)

        @block.vector
        def _(dve):
            for c in range(KC):
                dve.wait_ge(squared, c + 1)
                if c:
                    dve.wait_ge(added, c)
                    nc.vector.tensor_tensor(total[:], total[:], squares[:, c % 2, :], ALU.add).then_inc(added, 1)
                else:
                    nc.vector.tensor_copy(total[:], squares[:, 0, :]).then_inc(added, 1)
            for g in range(GROUPS):
                dve.wait_ge(root_ready, g + 1)
                nc.vector.reciprocal(scale[:, cols(g)], scale[:, cols(g)]).then_inc(inverted, 1)
            dve.wait_ge(inverted, GROUPS)
            dve.wait_ge(added, KC)

            def low(c):
                dve.wait_ge(high_ready, c + 1)
                nc.vector.tensor_tensor(target[1][:, c], squares[:, c % 2], target[0][:, c].bitcast(F32),
                                        ALU.subtract).then_inc(low_ready, 1)

            for c in range(KC):
                if split and c >= 2:
                    dve.wait_ge(low_ready, c - 1)
                nc.vector.scalar_tensor_tensor(out=squares[:, c % 2] if split else target[:, c], in0=source[:, c],
                                               scalar=m.vectors[:, gain + c:gain + c + 1],
                                               in1=scale[:], op0=ALU.mult, op1=ALU.mult).then_inc(normed, 1)
                if split and c:
                    low(c - 1)
            if split:
                low(KC - 1)

        @block.tensor
        def _(pe):
            pe.wait_ge(added, KC)
            for g in range(GROUPS):
                nc.tensor.matmul(m.bank[g][:, 0:G], m.mean_weights[:], total[:, cols(g)],
                                 start=True, stop=True).then_inc(mean_ready, 1)


class SplitWeights:

    def __init__(self, nc, stack, sem, name, weights, counts):
        self.nc, self.weights, self.counts = nc, weights, counts
        most = max(counts)
        self.raw = stack.enter_context(nc.sbuf_tensor(f"{name}_raw", [P, 2, most, P], F32))
        self.high = stack.enter_context(nc.sbuf_tensor(f"{name}_high", [P, 2, most, P], F32R))
        self.low = stack.enter_context(nc.sbuf_tensor(f"{name}_low", [P, 2, most, P], F32R))
        self.arrived = [sem(f"{name}_arrived{s}") for s in range(2)]
        self.high_ready = [sem(f"{name}_high_ready{s}") for s in range(2)]
        self.ready = [sem(f"{name}_split_ready{s}") for s in range(2)]
        self.done = [sem(f"{name}_product_done{s}") for s in range(2)]

    def load_all(self, sp, turns):
        for s in range(2):
            sp.dma_start(self.raw[:, s, 0:self.counts[s]], self.weights(0, s)).then_inc(self.arrived[s], 16)
        with sp.Fori(1, turns) as i:
            for s in range(2):
                sp.wait_ge(self.ready[s], i)
                sp.dma_start(self.raw[:, s, 0:self.counts[s]], self.weights(i, s)).then_inc(self.arrived[s], 16)

    def make_high(self, act, turn, s, first=False):
        n = self.counts[s]
        act.wait_ge(self.arrived[s], turn * 16 + 16)
        if not first:
            act.wait_ge(self.done[s], turn * GROUPS)
        self.nc.scalar.activation(self.high[:, s, 0:n], self.raw[:, s, 0:n], ACT.Copy).then_inc(self.high_ready[s], 1)

    def make_low(self, dve, turn, s):
        n = self.counts[s]
        dve.wait_ge(self.high_ready[s], turn + 1)
        self.nc.vector.tensor_tensor(self.low[:, s, 0:n], self.raw[:, s, 0:n], self.high[:, s, 0:n].bitcast(F32),
                                     ALU.subtract).then_inc(self.ready[s], 1)

    def product(self, out, s, source, g):
        high, low = source
        n = self.counts[s]
        for k in range(n):
            self.nc.tensor.matmul(out, self.high[:, s, k], high[:, k, cols(g)], start=k == 0, stop=False)
            self.nc.tensor.matmul(out, self.high[:, s, k], low[:, k, cols(g)], start=False, stop=False)
            last = self.nc.tensor.matmul(out, self.low[:, s, k], high[:, k, cols(g)], start=False, stop=k == n - 1)
        return last.then_inc(self.done[s], 1)


def turns_but_last(engine, turns, work):
    with engine.Fori(0, turns - 1) as i:
        work(i, False)
    work(turns - 1, True)


def project_features(nc, m, name, first, targets):
    with ExitStack() as stack:
        sem = phase(nc, stack)
        w = SplitWeights(nc, stack, sem, name, lambda i, s: m.dram["w_feature"][i * 2 + (first + s)], (KC, KC))
        banks_free = [sem(f"{name}_banks_free{s}") for s in range(2)]
        block = stack.enter_context(nc.Block())
        turns = 2 * len(targets)

        @block.sync
        def _(sp):
            w.load_all(sp, turns)

        @block.tensor
        def _(pe):
            with pe.Fori(0, turns) as i:
                for s in range(2):
                    pe.wait_ge(w.ready[s], i + 1)
                    for g in range(GROUPS):
                        pe.wait_ge(banks_free[s], i * GROUPS + (g + 1))
                        w.product(m.bank[3 * s + g][:, 0:G], s, m.xn, g)

        @block.scalar
        def _(act):
            for s in range(2):
                act.sem_inc(banks_free[s], GROUPS)
                w.make_high(act, 0, s, first=True)
            for c in range(4 * len(targets)):
                target, function = targets[c // 4]
                i, s = c // 2, c % 2
                for g in range(GROUPS):
                    act.wait_ge(w.done[s], i * GROUPS + g + 1)
                    nc.scalar.activation(target[:, c % 4, cols(g)], m.bank[3 * s + g][:, 0:G],
                                         function).then_inc(banks_free[s], 1)
                if i + 1 < turns:
                    w.make_high(act, i + 1, s)

        @block.vector
        def _(dve):
            with dve.Fori(0, turns) as i:
                for s in range(2):
                    w.make_low(dve, i, s)


def lower_bound(nc, m):
    with ExitStack() as stack:
        sem = phase(nc, stack)
        step_done = sem("lower_step")
        exp_ready = sem("lower_exp")
        block = stack.enter_context(nc.Block())
        a0, a1 = m.vectors[:, V_LB:V_LB + 4], m.vectors[:, V_LB + 4:V_LB + 8]
        lb, rest, top, shifted = m.lower[:, 0:4], m.lower[:, 4:8], m.lower[:, 8:12], m.lower[:, 12:20]

        @block.vector
        def _(dve):
            step = Chain(dve, step_done)
            step(nc.vector.tensor_tensor(top, a0, a1, ALU.max))
            step(nc.vector.tensor_tensor(shifted[:, 0:4], a0, top, ALU.subtract))
            step(nc.vector.tensor_tensor(shifted[:, 4:8], a1, top, ALU.subtract))
            dve.wait_ge(exp_ready, 1)
            step(nc.vector.tensor_tensor(top, shifted[:, 0:4], shifted[:, 4:8], ALU.add))
            step(nc.vector.reciprocal(top, top))
            step(nc.vector.tensor_tensor(lb, shifted[:, 0:4], top, ALU.mult))
            step(nc.vector.tensor_scalar(rest, lb, -1.0, 1.0, ALU.mult, ALU.add))

        @block.scalar
        def _(act):
            act.wait_ge(step_done, 3)
            nc.scalar.activation(shifted, shifted, ACT.Exp).then_inc(exp_ready, 1)


def project_tokens(nc, m, name, groups, keys=(), stores=None):
    with ExitStack() as stack:
        sem = phase(nc, stack)
        raw = stack.enter_context(nc.sbuf_tensor(f"{name}_raw", [P, 2, 512], F32))
        high = stack.enter_context(nc.sbuf_tensor(f"{name}_high", [P, KC, 512], F32R))
        low = stack.enter_context(nc.sbuf_tensor(f"{name}_low", [P, KC, 512], F32R))
        arrived = [sem(f"{name}_arrived{s}") for s in range(2)]
        high_ready = sem(f"{name}_high_ready")
        low_ready = sem(f"{name}_low_ready")
        tile_done = sem(f"{name}_tile_done")
        tile_kept = sem(f"{name}_tile_kept")
        turned = sem(f"{name}_turned")
        keys_kept = sem(f"{name}_keys_kept")
        stored = sem(f"{name}_stored")
        block = stack.enter_context(nc.Block())

        @block.sync
        def _(sp):
            n = 0
            for target, start, width in groups:
                for k in range(KC):
                    if n >= 2:
                        sp.wait_ge(low_ready, n - 1)
                    sp.dma_start(raw[:, n % 2, 0:width],
                                 m.dram["w_token"][:, k, start:start + width]).then_inc(arrived[n % 2], 16)
                    n += 1
            if stores is not None:
                stores(sp, tile_kept, stored)

        @block.tensor
        def _(pe):
            n = 0
            for group, (target, start, width) in enumerate(groups):
                for i, (first, count) in enumerate(TILES):
                    if n >= 6:
                        pe.wait_ge(tile_kept, n - 5)
                    out = m.bank[n % 6][0:count, 0:width]
                    tokens = slice(first, first + count)
                    for k in range(KC):
                        if i == 0:
                            pe.wait_ge(low_ready, group * KC + k + 1)
                        nc.tensor.matmul(out, m.xn[0][:, k, tokens], high[:, k, 0:width], start=k == 0, stop=False)
                        nc.tensor.matmul(out, m.xn[0][:, k, tokens], low[:, k, 0:width], start=False, stop=False)
                        last = nc.tensor.matmul(out, m.xn[1][:, k, tokens], high[:, k, 0:width],
                                                start=False, stop=k == KC - 1)
                    last.then_inc(tile_done, 1)
                    n += 1
            pe.wait_ge(tile_kept, n)
            step = 0
            for rows, _ in keys:
                for tiles in (range(0, 4), range(4, 8), range(8, 9)):
                    if step >= 2:
                        pe.wait_ge(keys_kept, step - 1)
                    for i in tiles:
                        count = TILES[i][1]
                        last = nc.tensor.transpose(m.bank[6 + step % 2][:, (i % 4) * P:(i % 4) * P + count],
                                                   rows[0:count, i], m.identity[0:count, 0:count])
                    last.then_inc(turned, 1)
                    step += 1

        @block.vector
        def _(dve):
            def make_low(group, k, width):
                n = group * KC + k
                dve.wait_ge(high_ready, n + 1)
                nc.vector.tensor_tensor(low[:, k, 0:width], raw[:, n % 2, 0:width], high[:, k, 0:width].bitcast(F32),
                                        ALU.subtract).then_inc(low_ready, 1)

            n = 0
            for group, (target, start, width) in enumerate(groups):
                for k in range(KC):
                    make_low(group, k, width)
                for i, (first, count) in enumerate(TILES):
                    dve.wait_ge(tile_done, n + 1)
                    nc.vector.tensor_copy(target[0:count, i, 0:width],
                                          m.bank[n % 6][0:count, 0:width]).then_inc(tile_kept, 1)
                    n += 1

        @block.scalar
        def _(act):
            n = 0
            for group, (target, start, width) in enumerate(groups):
                if group:
                    act.wait_ge(tile_done, 9 * group)
                for k in range(KC):
                    act.wait_ge(arrived[n % 2], 16 * (n // 2 + 1))
                    nc.scalar.activation(high[:, k, 0:width], raw[:, n % 2, 0:width], ACT.Copy).then_inc(high_ready, 1)
                    n += 1
            step = 0
            for _, keys_t in keys:
                for first, count in ((0, 512), (512, 512), (1024, DEC)):
                    act.wait_ge(turned, step + 1)
                    nc.scalar.activation(keys_t[:, first:first + count], m.bank[6 + step % 2][:, 0:count],
                                         ACT.Copy).then_inc(keys_kept, 1)
                    step += 1


def store_rows(m):
    def stores(sp, kept, stored):
        def store(target, source):
            sp.dma_start(target, source).then_inc(stored, 16)

        store(m.dram["out_win_s"][:, 0:WINDOW - 1], m.dram["window_rows"][:, 1:WINDOW])
        sp.wait_ge(kept, 9)
        store(m.dram["out_cmp_p"].rearrange("(i p) f -> p i f", p=P), m.kv_a[:, 0:8, 0:256])
        store(m.dram["out_slc_p"].rearrange("(i p) f -> p i f", p=P), m.kv_a[:, 0:8, 256:512])
        store(m.dram["out_cmp_s"], m.kv_a[0:DEC, 8, 0:256])
        store(m.dram["out_slc_s"], m.kv_a[0:DEC, 8, 256:512])
        sp.wait_ge(kept, 18)
        store(m.dram["out_win_p"].rearrange("(i p) f -> p i f", p=P), m.kv_b[:, 4:8, 0:256])
        store(m.dram["out_win_s"][:, WINDOW - 1], m.kv_b[0:DEC, 8, 0:256])
        store(m.dram["gate_rows"].rearrange("b h c -> b (h c)"), m.kv_b[0:DEC, 8, 256:280])
        sp.wait_ge(stored, 8 * 16)

    return stores


def hgrn_prompt(nc, m):
    with ExitStack() as stack:
        sem = phase(nc, stack)

        def sb(name, shape):
            return stack.enter_context(nc.sbuf_tensor(name, shape, F32))

        W = HGH * P
        reset = sb("chunk_reset", [P, W])
        logf, cum, diff = sb("log_f", [P, W]), sb("cum_log_f", [P, W]), sb("cum_to_last", [P, W])
        grow, shrink = sb("exp_cum", [P, W]), sb("exp_minus_cum", [P, W])
        decay = sb("chunk_decay", [P, HGH, 4])
        key = sb("hgrn_key", [P, W])
        q_dec, k_inv, k_last = sb("q_dec", [P, HGH, P]), sb("k_inv", [P, HGH, P]), sb("k_last", [P, HGH, P])
        k_rows, values = sb("k_last_rows", [P, HGH, P]), sb("hgrn_values", [P, HGH, P])
        weights = sb("intra_weights", [P, HGH, P])
        state = sb("hgrn_state", [P, 2, HGH, P])
        prepared = sem("hgrn_reset_ready")
        forget_done = sem("forget_done")
        log_ready = sem("log_f_ready")
        cum_ready = sem("cum_ready")
        diff_ready = sem("diff_ready")
        exps_ready = sem("exps_ready")
        last_ready = sem("exp_last_ready")
        factors_ready = sem("factors_ready")
        k_last_ready = sem("k_last_ready")
        values_ready = sem("values_ready")
        scores_done = sem("intra_scores_done")
        rows_turned = sem("k_rows_turned")
        rows_kept = sem("k_rows_kept")
        weights_ready = sem("intra_weights_ready")
        update_done = sem("state_update_done")
        state_ready = sem("state_ready")
        out_done = sem("hgrn_out_done")
        out_kept = sem("hgrn_out_kept")
        stored = sem("hgrn_state_stored")
        block = stack.enter_context(nc.Block())
        GROUPS8 = SEQ // P
        bank_scores, bank_rows, bank_out, bank_update = m.bank[0], m.bank[1], m.bank[2], (m.bank[3], m.bank[4])

        def heads(ap):
            return ap.rearrange("p (h t) -> p h t", h=HGH)

        def window(ap, n):
            return ap[:, :, bass.ds(n * P, P)]

        @block.scalar
        def _(act):
            act.sem_inc(out_kept, 1)
            act.wait_ge(forget_done, HGH)
            with act.Fori(0, GROUPS8) as n:
                nc.scalar.activation(heads(logf[:]), window(m.forget, n), ACT.Ln).then_inc(log_ready, 1)
                act.wait_ge(cum_ready, n + 1)
                nc.scalar.activation(grow[:], cum[:], ACT.Exp)
                nc.scalar.activation(shrink[:], cum[:], ACT.Exp, scale=-1.0).then_inc(exps_ready, 1)
                act.wait_ge(diff_ready, n + 1)
                nc.scalar.activation(decay[:], heads(cum[:]).rearrange("p h (c s) -> p h c s", s=BLOCK32)[:, :, :, BLOCK32 - 1],
                                     ACT.Exp)
                nc.scalar.activation(logf[:], diff[:], ACT.Exp).then_inc(last_ready, 1)
                act.wait_ge(rows_turned, n + 1)
                nc.scalar.activation(k_rows[:].rearrange("p h t -> p (h t)"), bank_rows[:], ACT.Copy).then_inc(rows_kept, 1)
                act.wait_ge(out_done, n + 1)
                nc.scalar.activation(m.v_hg[:, bass.ds(n, 1), :].rearrange("p a f -> p (a f)"), bank_out[:],
                                     ACT.Copy).then_inc(out_kept, 1)
                act.wait_ge(k_last_ready, n + 1)

        @block.gpsimd
        def _(pool):
            with pool.Fori(0, GROUPS8) as n:
                pool.wait_ge(out_kept, n + 1)
                nc.gpsimd.tensor_copy(values[:].rearrange("p h t -> p (h t)"),
                                      m.v_hg[:, bass.ds(n, 1), :].rearrange("p a f -> p (a f)")).then_inc(values_ready, 1)

        @block.vector
        def _(dve):
            nc.vector.memset(state[:, 0], 0.0).then_inc(prepared, 1)
            nc.vector.memset(reset[:], 1.0).then_inc(prepared, 1)
            dve.wait_ge(prepared, 2)
            nc.vector.memset(reset[:].rearrange("p (c s) -> p c s", s=BLOCK32)[:, :, 0], 0.0).then_inc(prepared, 1)
            for h in range(HGH):
                nc.vector.tensor_scalar(m.forget[:, h], m.forget[:, h], m.lower[:, 4 + h:5 + h],
                                        m.lower[:, h:h + 1], ALU.mult, ALU.add).then_inc(forget_done, 1)
            dve.wait_ge(forget_done, HGH)
            dve.wait_ge(prepared, 3)
            with dve.Fori(0, GROUPS8) as n:
                nc.vector.tensor_scalar(heads(key[:]), window(m.forget, n), -1.0, 1.0, ALU.mult, ALU.add)
                dve.wait_ge(log_ready, n + 1)
                nc.vector.tensor_tensor_scan(cum[:], reset[:], logf[:], 0.0, ALU.mult, ALU.add).then_inc(cum_ready, 1)
                dve.wait_ge(cum_ready, n + 1)
                c4 = cum[:].rearrange("p (c s) -> p c s", s=BLOCK32)
                nc.vector.tensor_tensor(diff[:].rearrange("p (c s) -> p c s", s=BLOCK32),
                                        c4[:, :, BLOCK32 - 1:BLOCK32].to_broadcast([P, W // BLOCK32, BLOCK32]), c4,
                                        ALU.subtract).then_inc(diff_ready, 1)
                dve.wait_ge(exps_ready, n + 1)
                nc.vector.tensor_tensor(q_dec[:], window(m.q_b, n), heads(grow[:]), ALU.mult)
                nc.vector.tensor_tensor(k_inv[:], heads(key[:]), heads(shrink[:]), ALU.mult).then_inc(factors_ready, 1)
                dve.wait_ge(last_ready, n + 1)
                nc.vector.tensor_tensor(k_last[:], heads(key[:]), heads(logf[:]), ALU.mult).then_inc(k_last_ready, 1)
                dve.wait_ge(scores_done, n + 1)
                nc.vector.tensor_tensor(weights[:], bank_scores[:].rearrange("p (h t) -> p h t", h=HGH),
                                        m.intra_mask[:].rearrange("p (a t) -> p a t", a=1).to_broadcast([P, HGH, P]),
                                        ALU.mult).then_inc(weights_ready, 1)
                for j in range(4):
                    dve.wait_ge(update_done, n * 4 + (j + 1))
                    if j:
                        dve.wait_ge(state_ready, n * 4 + j)
                    for h in range(HGH):
                        last = nc.vector.scalar_tensor_tensor(
                            out=state[:, (j + 1) % 2, h], in0=state[:, j % 2, h], scalar=decay[:, h, j:j + 1],
                            in1=bank_update[j % 2][:, h * P:(h + 1) * P], op0=ALU.mult, op1=ALU.add)
                    last.then_inc(state_ready, 1)
                dve.wait_ge(state_ready, n * 4 + 4)

        @block.tensor
        def _(pe):
            pe.wait_ge(prepared, 1)
            with pe.Fori(0, GROUPS8) as n:
                pe.wait_ge(factors_ready, n + 1)
                for h in range(HGH):
                    last = nc.tensor.matmul(bank_scores[:, h * P:(h + 1) * P], k_inv[:, h], q_dec[:, h],
                                            start=True, stop=True)
                last.then_inc(scores_done, 1)
                pe.wait_ge(k_last_ready, n + 1)
                for h in range(HGH):
                    last = nc.tensor.transpose(bank_rows[:, h * P:(h + 1) * P], k_last[:, h], m.identity[:])
                last.then_inc(rows_turned, 1)
                pe.wait_ge(weights_ready, n + 1)
                pe.wait_ge(values_ready, n + 1)
                pe.wait_ge(out_kept, n + 1)
                for h in range(HGH):
                    nc.tensor.matmul(bank_out[:, h * P:(h + 1) * P], weights[:, h], values[:, h],
                                     start=h == 0, stop=False, skip_group_check=True)
                pe.wait_ge(rows_kept, n + 1)
                for j in range(4):
                    rows = slice(j * BLOCK32, (j + 1) * BLOCK32)
                    if j >= 2:
                        pe.wait_ge(state_ready, n * 4 + (j - 1))
                    for h in range(HGH):
                        last = nc.tensor.matmul(bank_update[j % 2][:, h * P:(h + 1) * P], k_rows[rows, h],
                                                values[rows, h], start=True, stop=True)
                    last.then_inc(update_done, 1)
                    if j:
                        pe.wait_ge(state_ready, n * 4 + j)
                    for h in range(HGH):
                        last = nc.tensor.matmul(bank_out[rows, h * P:(h + 1) * P], q_dec[:, h, rows],
                                                state[:, j % 2, h], start=False, stop=h == HGH - 1,
                                                skip_group_check=True)
                last.then_inc(out_done, 1)

        @block.sync
        def _(sp):
            sp.wait_ge(state_ready, GROUPS8 * 4)
            sp.dma_start(m.dram["out_hgrn_p"].rearrange("h k v -> k h v"), state[:, 0]).then_inc(stored, 16)
            sp.wait_ge(stored, 16)


def hgrn_decode(nc, m):
    with ExitStack() as stack:
        sem = phase(nc, stack)

        def sb(name, shape):
            return stack.enter_context(nc.sbuf_tensor(name, shape, F32))

        state = sb("decode_state", [P, 2, HGH, P])
        outer = sb("decode_outer", [P, HGH, P])
        key = sb("decode_key", [P, HGH, DEC])
        query = sb("decode_query", [P, HGH, DEC, DEC])
        loaded = [sem(f"decode_state_loaded{s}") for s in range(2)]
        query_ready = sem("decode_query_ready")
        spread = sem("decode_values_spread")
        outer_ready = sem("decode_outer_ready")
        updated = sem("decode_state_updated")
        read_out = sem("decode_state_read")
        stored = [sem(f"decode_state_stored{s}") for s in range(2)]
        kept = sem("decode_out_kept")
        block = stack.enter_context(nc.Block())
        bank_out = m.bank[2]

        @block.sync
        def _(sp):
            for b in range(DEC):
                if b >= 2:
                    sp.wait_ge(stored[b % 2], 16 * (b // 2))
                    sp.wait_ge(read_out, b - 1)
                sp.dma_start(state[:, b % 2], m.dram["state_hgrn"][b].rearrange("h k v -> k h v")).then_inc(loaded[b % 2], 16)

        @block.vector
        def _(dve):
            nc.vector.memset(query[:], 0.0).then_inc(query_ready, 1)
            nc.vector.tensor_scalar(key[:], m.forget[:, :, SEQ:T], -1.0, 1.0, ALU.mult, ALU.add).then_inc(query_ready, 1)
            dve.wait_ge(query_ready, 2)
            nc.vector.tensor_copy(query[:].rearrange("p h b c -> p h (b c)")[:, :, 0:DEC * DEC:DEC + 1],
                                  m.q_b[:, :, SEQ:T]).then_inc(query_ready, 1)
            for b in range(DEC):
                dve.wait_ge(spread, b + 1)
                for h in range(HGH):
                    last = nc.vector.tensor_scalar(outer[:, h], m.bank[b % 2][:, h * P:(h + 1) * P],
                                                   key[:, h, b:b + 1], None, ALU.mult)
                last.then_inc(outer_ready, 1)
                dve.wait_ge(outer_ready, b + 1)
                dve.wait_ge(loaded[b % 2], 16 * (b // 2 + 1))
                for h in range(HGH):
                    nc.vector.scalar_tensor_tensor(out=state[:, b % 2, h], in0=state[:, b % 2, h],
                                                   scalar=m.forget[:, h, SEQ + b:SEQ + b + 1], in1=outer[:, h],
                                                   op0=ALU.mult, op1=ALU.add).then_inc(updated, 1)
                dve.wait_ge(updated, 4 * (b + 1))

        @block.tensor
        def _(pe):
            pe.wait_ge(query_ready, 3)
            for b in range(DEC):
                if b >= 2:
                    pe.wait_ge(outer_ready, b - 1)
                nc.tensor.matmul(m.bank[b % 2][:], m.row_pick[0:DEC, b], m.v_hg[0:DEC, 8],
                                 start=True, stop=True).then_inc(spread, 1)
                pe.wait_ge(updated, 4 * (b + 1))
                for h in range(HGH):
                    last = nc.tensor.matmul(bank_out[0:DEC, h * P:(h + 1) * P], query[:, h, b], state[:, b % 2, h],
                                            start=b == 0 and h == 0, stop=b == DEC - 1, skip_group_check=True)
                last.then_inc(read_out, 1)

        @block.scalar
        def _(act):
            for b in range(DEC):
                act.wait_ge(updated, 4 * (b + 1))
                act.dma_start(m.dram["out_hgrn_s"][b].rearrange("h k v -> k h v"), state[:, b % 2]).then_inc(stored[b % 2], 16)
            for s in range(2):
                act.wait_ge(stored[s], 16 * (DEC // 2))
            act.wait_ge(read_out, DEC)
            nc.scalar.activation(m.v_hg[0:DEC, 8], bank_out[0:DEC], ACT.Copy).then_inc(kept, 1)


HALF = 16
PAIRS = HALF // 2
HID = 256


def compress(nc, m, prompt):
    with ExitStack() as stack:
        sem = phase(nc, stack)
        n_half = SEQ // HALF if prompt else PAGES * PAGE // HALF
        per_page = n_half if prompt else PAGE // HALF
        pages = n_half // per_page
        count = 1 if prompt else DEC
        slots = 1 if prompt else 2
        tag = "prompt" if prompt else "cache"
        width = KVH * n_half

        def sb(name, shape):
            return stack.enter_context(nc.sbuf_tensor(f"{tag}_{name}", shape, F32))

        rows = sb("rows", [P, slots, pages, PAIRS, 2, KVH, per_page])
        high = sb("high_half", [P, KVH, n_half + 1])
        before = sb("hidden_before", [P, 2, KVH, n_half])
        hidden = sb("hidden", [P, 2, 2, KVH, n_half])
        row_halves = sb("row_halves", [SEQ // HALF, 2 * KVH, HALF, HEAD]) if prompt else None
        weights_in = sem("compress_weights_in")
        bias_done = sem("compress_bias_done")
        bias_kept = sem("compress_bias_kept")
        halves_in = sem("prompt_halves_in")
        turned = sem("prompt_halves_turned")
        rows_kept = sem("prompt_rows_kept")
        page_in = [sem(f"compress_page_in{s}") for s in range(slots)]
        table_in = sem("compress_table_in")
        product_done = sem("half_products_done")
        high_kept = sem("high_half_kept")
        sum_ready = sem("hidden_sum_ready")
        hidden_ready = sem("hidden_ready")
        blocks_done = sem("kv_blocks_done")
        blocks_kept = sem("kv_blocks_kept")
        zeroed = sem("high_half_zeroed")
        block = stack.enter_context(nc.Block())
        w1 = m.w1[:]
        UNITS = 4

        def over_sequences(engine, work):
            if prompt:
                work(0, 0)
            else:
                with engine.Fori(0, DEC // 2) as i:
                    for s in range(2):
                        work(i * 2 + s, s)

        @block.sync
        def _(sp):
            if prompt:
                sp.dma_start(w1, m.dram["cmp_w1"]).then_inc(weights_in, 16)
                sp.dma_start(m.w2_k[:], m.dram["cmp_w2_k"]).then_inc(weights_in, 16)
                sp.dma_start(m.w2_v[:], m.dram["cmp_w2_v"]).then_inc(weights_in, 16)
                sp.dma_start(m.pos[:], m.dram["cmp_pos"]).then_inc(weights_in, 16)
                for a in range(2 * KVH):
                    sp.dma_start(row_halves[:, a], m.dram["out_cmp_p"][:, a * HEAD:(a + 1) * HEAD]
                                 .rearrange("(n s) d -> n s d", s=HALF)).then_inc(halves_in, 16)
            else:
                sp.dma_start(m.table[:], m.dram["page_table"]).then_inc(table_in, 16)
                sp.wait_ge(table_in, 16)

                def load_page(b, p, s, freed=None):
                    page = sp.value_load(m.table[0:1, bass.ds(b * PAGES + p, 1)], min_val=0, max_val=POOL - 1)
                    if freed is not None:
                        sp.wait_ge(product_done, freed)
                    sp.dma_start(rows[:, s, bass.ds(p, 1)].rearrange("p a s c k n -> p a (s c k n)"),
                                 m.dram["cache_cmp"][bass.ds(page, 1)].rearrange("a p f -> p a f")).then_inc(page_in[s], 16)

                for s in range(2):
                    with sp.Fori(0, PAGES) as p:
                        load_page(s, p, s)
                with sp.Fori(1, DEC // 2) as i:
                    for s in range(2):
                        load_page(i * 2 + s, 0, s, freed=(i * 2 + (s - 1)) * UNITS)
                        with sp.Fori(1, PAGES) as p:
                            load_page(i * 2 + s, p, s)

        @block.tensor
        def _(pe):
            if prompt:
                pe.wait_ge(weights_in, 4 * 16)
                for c in range(2):
                    for f in range(2):
                        for l in range(2):
                            for s in range(PAIRS):
                                last = nc.tensor.matmul(m.bank[7][:, 2 * c + f:2 * c + f + 1],
                                                        w1[:, c, l, s, f * P:(f + 1) * P], m.pos[:, c, l, s:s + 1],
                                                        start=l == 0 and s == 0, stop=l == 1 and s == PAIRS - 1)
                last.then_inc(bias_done, 1)
                pe.wait_ge(halves_in, 4 * 16)
                for c in range(2):
                    for k in range(KVH):
                        for s in range(PAIRS):
                            last = nc.tensor.transpose(m.bank[2 * c + k][:, s * n_half:(s + 1) * n_half],
                                                       row_halves[:, 2 * c + k, 2 * s:2 * s + 2].rearrange("n s d -> n (s d)"),
                                                       m.identity[0:n_half, 0:n_half])
                        last.then_inc(turned, 1)
                pe.wait_ge(rows_kept, 4)

            def work(n, slot):
                if not prompt:
                    pe.wait_ge(page_in[slot], (n - slot + 2) * (8 * PAGES))
                for c in range(2):
                    for f in range(2):
                        u = 2 * c + f
                        for l in range(2):
                            for s in range(PAIRS):
                                if prompt:
                                    out = m.bank[u][:, l * 256:l * 256 + width]
                                    moving = rows[:, slot, 0, s, c]
                                else:
                                    out = m.bank[u][:, l * 256:l * 256 + width].rearrange("p (a x) -> p a x", a=pages)
                                    moving = rows[:, slot, :, s, c].rearrange("p a k n -> p a (k n)")
                                last = nc.tensor.matmul(out, w1[:, c, l, s, f * P:(f + 1) * P], moving,
                                                        start=s == 0, stop=s == PAIRS - 1)
                        last.then_inc(product_done, 1)
                for c in range(2):
                    pe.wait_ge(hidden_ready, n * UNITS + 2 * (c + 1))
                    pe.wait_ge(blocks_kept, n * 2 + (c + 1))
                    for k in range(KVH):
                        for f in range(2):
                            if c == 0:
                                last = nc.tensor.matmul(m.bank[4][:, 0:n_half], m.w2_k[:, f, k],
                                                        hidden[:, 0, f, k], start=k == 0 and f == 0,
                                                        stop=k == 1 and f == 1)
                            else:
                                last = nc.tensor.matmul(m.bank[5][0:n_half, k * HEAD:(k + 1) * HEAD],
                                                        hidden[:, 1, f, k], m.w2_v[:, f],
                                                        start=f == 0, stop=f == 1)
                    last.then_inc(blocks_done, 1)

            over_sequences(pe, work)

        @block.vector
        def _(dve):
            nc.vector.memset(high[:], 0.0).then_inc(zeroed, 1)
            if prompt:
                nc.vector.memset(m.kc_prompt[:], 0.0).then_inc(zeroed, 1)
                nc.vector.memset(m.vc_prompt[:], 0.0).then_inc(zeroed, 1)
            if prompt:
                dve.wait_ge(bias_done, 1)
                nc.vector.tensor_copy(m.hidden_bias[:], m.bank[7][:, 0:4]).then_inc(bias_kept, 1)
                for c in range(2):
                    for k in range(KVH):
                        dve.wait_ge(turned, 2 * c + k + 1)
                        nc.vector.tensor_copy(rows[:, 0, 0, :, c, k],
                                              m.bank[2 * c + k][:].rearrange("p (s n) -> p s n", s=PAIRS)).then_inc(rows_kept, 1)

            def work(n, slot):
                for u in range(UNITS):
                    dve.wait_ge(high_kept, n * UNITS + u + 1)
                    for k in range(KVH):
                        low = m.bank[u][:, 0:width].rearrange("p (a k n) -> p a k n", a=pages, k=KVH)[:, :, k]
                        last = nc.vector.tensor_tensor(
                            before[:, u % 2, k].rearrange("p (a n) -> p a n", a=pages), low,
                            high[:, k, 1:n_half + 1].rearrange("p (a n) -> p a n", a=pages), ALU.add)
                    last.then_inc(sum_ready, 1)

            over_sequences(dve, work)

        @block.scalar
        def _(act):
            act.sem_inc(blocks_kept, 2)
            act.wait_ge(zeroed, 3 if prompt else 1)
            if prompt:
                act.wait_ge(bias_kept, 1)

            def work(n, slot):
                for u in range(UNITS):
                    act.wait_ge(product_done, n * UNITS + u + 1)
                    for k in range(KVH):
                        part = m.bank[u][:, 256:256 + width].rearrange("p (a k n) -> p a k n", a=pages, k=KVH)[:, :, k]
                        last = nc.scalar.activation(high[:, k, 0:n_half].rearrange("p (a n) -> p a n", a=pages), part,
                                                    ACT.Copy)
                    last.then_inc(high_kept, 1)
                    act.wait_ge(sum_ready, n * UNITS + u + 1)
                    nc.scalar.activation(hidden[:, u // 2, u % 2], before[:, u % 2], ACT.Silu,
                                         bias=m.hidden_bias[:, u:u + 1]).then_inc(hidden_ready, 1)
                act.wait_ge(blocks_done, n * 2 + 1)
                target = m.kc_prompt[:, 0:n_half] if prompt else m.kc_cache[:, bass.ds(n, 1)].rearrange("p a n -> p (a n)")
                nc.scalar.activation(target, m.bank[4][:, 0:n_half], ACT.Copy).then_inc(blocks_kept, 1)
                act.wait_ge(blocks_done, n * 2 + 2)
                target = m.vc_prompt[0:n_half] if prompt else m.vc_cache[:, bass.ds(n, 1)].rearrange("p a n -> p (a n)")
                nc.scalar.activation(target, m.bank[5][0:n_half, 0:P], ACT.Copy).then_inc(blocks_kept, 1)

            over_sequences(act, work)


def gates_sigmoid(nc, m):
    with ExitStack() as stack:
        sem = phase(nc, stack)
        done = sem("gates_done")
        block = stack.enter_context(nc.Block())

        @block.scalar
        def _(act):
            nc.scalar.activation(m.gates[:], m.kv_b[:, 0:QT, 256:280], ACT.Sigmoid).then_inc(done, 1)


def prompt_items():
    items = []
    for k in range(KVH):
        for i in range(QT):
            items.append((k, i, "slc", 0, i + 1))
            o = QT - 1 - i
            first = max(0, o - WINDOW // P)
            items.append((k, o, "near", first, o + 1 - first))
    return items


def prompt_attention(nc, m):
    with ExitStack() as stack:
        sem = phase(nc, stack)

        def sb(name, shape):
            return stack.enter_context(nc.sbuf_tensor(name, shape, F32))

        items = prompt_items()
        N = len(items)
        over = m.over_xn()
        query = over("query_pair", [P, KVH, SEQ])
        probs = over("probs", [P, 2, SEQ])
        probs_t = over("probs_turned", [P, 2, QT, P])
        out = over("out_pair", [P, QT, KVH, HEAD])
        gate = sb("gate_pair", [P, QT, KVH, 3])
        top, bias, total = sb("score_max", [P, 2, 2]), sb("exp_bias", [P, 2, 2]), sb("exp_total", [P, 4, 2])
        coefficient = sb("branch_coefficient", [P, 4, 2])
        causal, beyond = sb("causal_add_sb", [P, P]), sb("window_add_sb", [P, P])
        cmp_add, cmp_keep = sb("cmp_add_sb", [P, 56 + P]), sb("cmp_keep_sb", [P, 56 + P])
        masks_in = sem("attention_masks_in")
        cleared = sem("queries_cleared")
        staged = sem("pair_staged")
        scores_done = sem("scores_done")
        masked = sem("scores_masked")
        max_ready = sem("max_ready")
        bias_ready = sem("exp_bias_ready")
        probs_ready = sem("probs_ready")
        probs_masked = sem("probs_masked")
        turned = sem("probs_turned_done")
        kept_act = sem("turned_kept_by_scalar")
        kept_dve = sem("turned_kept_by_vector")
        product_done = sem("value_product_done")
        inverse_ready = sem("inverse_total_ready")
        coefficient_ready = sem("coefficient_ready")
        added = sem("window_branch_added")
        combined = sem("branch_combined")
        written = sem("pair_written")
        block = stack.enter_context(nc.Block())

        def is_near(n):
            return items[n][2] == "near"

        def key_tiles(n):
            return items[n][4] + is_near(n)

        def nears(n):
            return sum(is_near(x) for x in range(n))

        NEARS = nears(N)
        PARTS_OF = N + NEARS

        @block.sync
        def _(sp):
            for target, source in ((causal, m.dram["causal_add"]), (beyond, m.dram["window_add"]),
                                   (cmp_add, m.dram["cmp_add"]), (cmp_keep, m.dram["cmp_keep"])):
                sp.dma_start(target[:], source).then_inc(masks_in, 16)

        @block.tensor
        def _(pe):
            def scores(j, n):
                k, i, kind, first, tiles = items[n]
                if n >= 2:
                    pe.wait_ge(probs_ready, j * N + (n - 1))
                lhs = query[:, k, i * P:(i + 1) * P]
                pair = m.pair[n % 2]
                keys = m.k_win if is_near(n) else m.k_slc
                for a in range(0, tiles * P, 512):
                    b = min(a + 512, tiles * P)
                    last = nc.tensor.matmul(pair[:, a:b], lhs, keys[:, first * P + a:first * P + b],
                                            start=True, stop=True)
                if is_near(n):
                    last = nc.tensor.matmul(pair[:, tiles * P:(tiles + 1) * P], lhs, m.kc_prompt[:],
                                            start=True, stop=True)
                last.then_inc(scores_done, 1)

            def turn(j, n):
                if is_near(n):
                    pe.wait_ge(probs_masked, j * NEARS + (nears(n) + 1))
                pe.wait_ge(probs_ready, j * N + (n + 1))
                if n >= 1:
                    pe.wait_ge(kept_act, j * N + n)
                    pe.wait_ge(kept_dve, j * N + n)
                for t in range(key_tiles(n)):
                    last = nc.tensor.transpose(m.turn_bank[t // 4][:, (t % 4) * P:(t % 4) * P + P],
                                               probs[:, n % 2, t * P:(t + 1) * P], m.identity[:])
                last.then_inc(turned, 1)

            def product(j, n):
                k, i, kind, first, tiles = items[n]
                pe.wait_ge(kept_act, j * N + (n + 1))
                pe.wait_ge(kept_dve, j * N + (n + 1))
                if n >= 2:
                    pe.wait_ge(combined, j * N + (n - 1))
                o = m.bank[6 + n % 2]
                v, at = (m.kv_b, 128) if is_near(n) else (m.kv_a, 384)
                for t in range(tiles):
                    last = nc.tensor.matmul(o[:, 0:P], probs_t[:, n % 2, t], v[:, first + t, at:at + P],
                                            start=t == 0, stop=t == tiles - 1)
                if is_near(n):
                    last = nc.tensor.matmul(o[:, P:2 * P], probs_t[:, n % 2, tiles], m.vc_prompt[:],
                                            start=True, stop=True)
                last.then_inc(product_done, 1)

            with pe.Fori(0, GQA) as j:
                pe.wait_ge(staged, j * 3 + 3)
                scores(j, 0)
                for n in range(N + 1):
                    if n + 1 < N:
                        scores(j, n + 1)
                    if n < N:
                        turn(j, n)
                    if n >= 1:
                        product(j, n - 1)

        def keep_turned(copy, n, b):
            t0, t1 = 4 * b, min(key_tiles(n), 4 * b + 4)
            if t0 < t1:
                return copy(probs_t[:, n % 2, t0:t1],
                            m.turn_bank[b][:, 0:(t1 - t0) * P].rearrange("p (t q) -> p t q", q=P))
            return None

        @block.scalar
        def _(act):
            def copy(to, source):
                return nc.scalar.activation(to, source, ACT.Copy)

            with act.Fori(0, GQA) as j:
                for n in range(N + 1):
                    if n < N:
                        act.wait_ge(bias_ready, j * N + (n + 1))
                        if n >= 2:
                            act.wait_ge(turned, j * N + (n - 1))
                        w = items[n][4] * P
                        if is_near(n):
                            nc.scalar.activation(probs[:, n % 2, w:w + P], m.pair[n % 2][:, w:w + P], ACT.Exp,
                                                 scale=SCALE, bias=bias[:, n % 2, 1:2],
                                                 accum_out=total[:, n % 4, 1:2])
                        nc.scalar.activation(probs[:, n % 2, 0:w], m.pair[n % 2][:, 0:w], ACT.Exp, scale=SCALE,
                                             bias=bias[:, n % 2, 0:1],
                                             accum_out=total[:, n % 4, 0:1]).then_inc(probs_ready, 1)
                    if n >= 1:
                        act.wait_ge(turned, j * N + n)
                        if n >= 3:
                            act.wait_ge(product_done, j * N + (n - 2))
                        last = keep_turned(copy, n - 1, 1)
                        if last is not None:
                            last.then_inc(kept_act, 1)
                        else:
                            act.sem_inc(kept_act, 1)

        @block.vector
        def _(dve):
            nc.vector.memset(query[:], 0.0).then_inc(cleared, 1)
            dve.wait_ge(cleared, 1)
            dve.wait_ge(masks_in, 4 * 16)

            def mask_steps(n):
                return 1 if not is_near(n) else 3 if items[n][4] == 5 else 2

            MASKS = sum(mask_steps(n) for n in range(N))

            def maximum(j, n):
                k, i, kind, first, tiles = items[n]
                dve.wait_ge(scores_done, j * N + (n + 1))
                pair, w = m.pair[n % 2], tiles * P

                def add(a, mask):
                    nc.vector.tensor_tensor(pair[:, a:a + P], pair[:, a:a + P], mask, ALU.add).then_inc(masked, 1)

                if is_near(n):
                    add(w, cmp_add[:, 56 - 8 * i:56 - 8 * i + P])
                    if tiles == 5:
                        add(0, beyond[:])
                add(w - P, causal[:])
                dve.wait_ge(masked, j * MASKS + sum(mask_steps(x) for x in range(n + 1)))
                if is_near(n):
                    nc.vector.tensor_reduce(top[:, n % 2, 1:2], pair[:, w:w + P], AX.X, ALU.max)
                nc.vector.tensor_reduce(top[:, n % 2, 0:1], pair[:, 0:w], AX.X, ALU.max).then_inc(max_ready, 1)
                dve.wait_ge(max_ready, j * N + (n + 1))
                if n >= 2:
                    dve.wait_ge(probs_ready, j * N + (n - 1))
                c = 1 + is_near(n)
                nc.vector.tensor_scalar(bias[:, n % 2, 0:c], top[:, n % 2, 0:c], -SCALE, None,
                                        ALU.mult).then_inc(bias_ready, 1)

            def mask_blocks(j, n):
                w, i = items[n][4] * P, items[n][1]
                dve.wait_ge(probs_ready, j * N + (n + 1))
                nc.vector.tensor_tensor(probs[:, n % 2, w:w + P], probs[:, n % 2, w:w + P],
                                        cmp_keep[:, 56 - 8 * i:56 - 8 * i + P], ALU.mult).then_inc(probs_masked, 1)

            def keep(j, n):
                dve.wait_ge(turned, j * N + (n + 1))
                if n >= 2:
                    dve.wait_ge(product_done, j * N + (n - 1))
                keep_turned(nc.vector.tensor_copy, n, 0).then_inc(kept_dve, 1)

            def combine(j, n, seen):
                k, i, kind, first, tiles = items[n]
                parts = ((1, 0), (2, 1)) if is_near(n) else ((0, 0),)
                c = len(parts)
                r = parts[0][0]
                nc.vector.reciprocal(coefficient[:, n % 4, 0:c], total[:, n % 4, 0:c]).then_inc(inverse_ready, 1)
                dve.wait_ge(inverse_ready, j * N + (n + 1))
                nc.vector.tensor_tensor(coefficient[:, n % 4, 0:c], coefficient[:, n % 4, 0:c], gate[:, i, k, r:r + c],
                                        ALU.mult).then_inc(coefficient_ready, 1)
                dve.wait_ge(coefficient_ready, j * N + (n + 1))
                dve.wait_ge(product_done, j * N + (n + 1))
                for x, (_, part) in enumerate(parts):
                    o = m.bank[6 + n % 2][:, part * P + k * HEAD:part * P + (k + 1) * HEAD]
                    scalar = coefficient[:, n % 4, part:part + 1]
                    if (k, i) in seen:
                        if x:
                            dve.wait_ge(added, j * NEARS + (nears(n) + 1))
                        elif n:
                            dve.wait_ge(combined, j * N + n)
                        last = nc.vector.scalar_tensor_tensor(out=out[:, i, k], in0=o, scalar=scalar, in1=out[:, i, k],
                                                              op0=ALU.mult, op1=ALU.add)
                    else:
                        last = nc.vector.tensor_scalar(out[:, i, k], o, scalar, None, ALU.mult)
                    seen.add((k, i))
                    last.then_inc(combined if x == c - 1 else added, 1)

            with dve.Fori(0, GQA) as j:
                for k in range(KVH):
                    half = slice(k * HEAD, (k + 1) * HEAD)
                    nc.vector.tensor_copy(query[half, k], m.q_a[half, bass.ds(j, 1), 0:SEQ]
                                          .rearrange("p a t -> p (a t)")).then_inc(staged, 1)
                nc.vector.tensor_copy(gate[:].rearrange("p i k c -> p (i k) c"),
                                      m.gates[:].rearrange("p i (k g c) -> p (i k) g c", k=KVH, g=GQA)
                                      [:, :, bass.ds(j, 1), :].rearrange("p i a c -> p i (a c)")).then_inc(staged, 1)
                dve.wait_ge(staged, j * 3 + 3)
                seen = set()
                for n in range(N + 2):
                    if n < N:
                        maximum(j, n)
                    if n < N and is_near(n):
                        mask_blocks(j, n)
                    if 1 <= n <= N:
                        keep(j, n - 1)
                    if n >= 2:
                        combine(j, n - 2, seen)
                dve.wait_ge(combined, j * N + N)
                for k in range(KVH):
                    last = nc.vector.tensor_copy(
                        m.o_nsa[:, 0:QT].rearrange("p i (h d) -> p i h d", d=HEAD)[:, :, bass.ds(j + k * GQA, 1), :]
                        .rearrange("p i a d -> p i (a d)"), out[:, :, k])
                last.then_inc(written, 1)
                dve.wait_ge(written, j + 1)


def decode_attention(nc, m):
    with ExitStack() as stack:
        sem = phase(nc, stack)

        def sb(name, shape, dtype=F32):
            return stack.enter_context(nc.sbuf_tensor(name, shape, dtype))

        R = DEC * KVH * GQA
        KEYS = PAGES * PAGE
        KT = PAGES
        WT = WINDOW // P
        over = m.over_xn()
        query = sb("decode_q", [P, DEC, R])
        ring = over("decode_ring", [P, 2, KEYS + WINDOW])
        slc, win, cmp = sb("slc_scores", [R, KEYS + 1]), sb("win_scores", [R, WINDOW + 1]), sb("cmp_scores", [R, P])
        small = sb("decode_small", [R, 32])
        folded = sb("block_probs", [R, 136])
        importance, rank, barred = sb("importance", [R, N_SEL]), sb("rank", [R, N_SEL]), sb("barred", [R, N_SEL])
        new_probs = sb("new_probs", [R, 2, DEC])
        gate = sb("decode_gate", [R, 3])
        coefficient = sb("decode_coefficient", [R, 2, 3])
        group_sum, own = sb("group_sum_sb", [R, R]), sb("own_column_sb", [R, DEC])
        win_t, cmp_t = over("win_probs_turned", [P, WT, DEC, R]), sb("cmp_probs_turned", [P, DEC, R])
        new_t = sb("new_probs_turned", [DEC, 2, R])
        out = sb("decode_out", [R, HEAD])
        slc_t = over("slc_probs_turned", [P, KT, DEC, R])[:]
        spare = m.q_a[:].rearrange("p c t -> p (c t)")
        SS = N_SEL * N_SEL
        earlier, greater, equal = (spare[0:R, a * SS:(a + 1) * SS].rearrange("r (s u) -> r s u", s=N_SEL) for a in range(3))
        small_in = sem("decode_small_in")
        mask_in = sem("earlier_mask_in")
        cleared = sem("decode_cleared")
        query_ready = sem("decode_query_ready")
        k_in = [sem(f"decode_keys_in{s}") for s in range(2)]
        v_in = [sem(f"decode_values_in{s}") for s in range(2)]
        keys_read = sem("decode_keys_read")
        scores_done = sem("decode_scores_done")
        scores_kept = sem("decode_scores_kept")
        step_done = sem("decode_step")
        exp_done = sem("decode_exp_done")
        cmp_probs_ready = sem("cmp_probs_ready")
        imp_done = sem("importance_product_done")
        bars_ready = sem("bias_ready")
        probs_ready = sem("decode_probs_ready")
        turned = sem("decode_turned")
        turned_kept = sem("decode_turned_kept")
        values_read = sem("decode_values_read")
        products_done = sem("decode_products_done")
        stored, returned = sem("decode_out_stored"), sem("decode_out_returned")
        out_ready = sem("decode_out_ready")
        block = stack.enter_context(nc.Block())

        def load_pages(sp, cache, part, width, b, s, arrived):
            with sp.Fori(0, PAGES) as p:
                page = sp.value_load(m.table[0:1, bass.ds(p + b * PAGES, 1)], min_val=0, max_val=POOL - 1)
                sp.dma_start(ring[:, s, bass.ds(p * P, P)],
                             cache[bass.ds(page, 1)].rearrange("a p f -> p (a f)")).then_inc(arrived, 16)

        @block.sync
        def _(sp):
            sp.dma_start(gate[:], m.dram["gate_rows"].rearrange("b h c -> (b h) c")).then_inc(small_in, 16)
            sp.dma_start(group_sum[:], m.dram["group_sum"]).then_inc(small_in, 16)
            sp.dma_start(own[:], m.dram["own_column"]).then_inc(small_in, 16)
            for b in range(DEC):
                s = b % 2
                if b >= 2:
                    sp.wait_ge(keys_read, b - 1)
                load_pages(sp, m.dram["slc_k"], 0, P, b, s, k_in[s])
                sp.dma_start(ring[:, s, KEYS:], m.dram["win_k"][b]).then_inc(k_in[s], 16)
            sp.wait_ge(query_ready, 2)
            sp.dma_start(spare[0:R, 0:SS], m.dram["earlier"]).then_inc(mask_in, 16)
            for b in range(DEC):
                s = b % 2
                if b < 2:
                    sp.wait_ge(keys_read, DEC - 1 + s)
                else:
                    sp.wait_ge(values_read, b - 1)
                load_pages(sp, m.dram["slc_v"], 0, P, b, s, v_in[s])
                sp.dma_start(ring[:, s, KEYS:], m.dram["win_v"][b]).then_inc(v_in[s], 16)
            sp.wait_ge(out_ready, 1)
            sp.dma_start(m.dram["o_rows"], out[:]).then_inc(stored, 16)
            sp.wait_ge(stored, 16)
            sp.dma_start(m.o_nsa[0:DEC, 8], m.dram["o_rows"].rearrange("(b h) d -> b (h d)", b=DEC)).then_inc(returned, 16)
            sp.wait_ge(returned, 16)

        @block.gpsimd
        def _(pool):
            nc.gpsimd.memset(slc_t, 0.0).then_inc(cleared, 1)
            nc.gpsimd.memset(win_t[:], 0.0).then_inc(cleared, 1)
            nc.gpsimd.memset(cmp_t[:], 0.0).then_inc(cleared, 1)

        @block.tensor
        def _(pe):
            pe.wait_ge(query_ready, 2)
            for b in range(DEC):
                pe_last = nc.tensor.matmul(m.bank[5][0:R, 0:N_CMP_D], query[:, b], m.kc_cache[:, b, 0:N_CMP_D],
                                           start=b == 0, stop=b == DEC - 1)
            for n, keys in enumerate((m.k_slc, m.k_win)):
                for b in range(DEC):
                    pe_last = nc.tensor.matmul(m.bank[5][0:R, P + n:P + n + 1], query[:, b], keys[:, SEQ + b:SEQ + b + 1],
                                               start=b == 0, stop=b == DEC - 1)
            pe_last.then_inc(scores_done, 1)
            for b in range(DEC):
                s = b % 2
                pe.wait_ge(k_in[s], 16 * (PAGES + 1) * (b // 2 + 1))
                for a in range(5):
                    last = nc.tensor.matmul(m.bank[a][0:R, :], query[:, b], ring[:, s, a * 512:(a + 1) * 512],
                                            start=b == 0, stop=b == DEC - 1, skip_group_check=True)
                last.then_inc(keys_read, 1)
            pe.wait_ge(cmp_probs_ready, 1)
            nc.tensor.matmul(m.bank[6][0:R, 0:N_CMP_D], group_sum[:], cmp[:, 0:N_CMP_D],
                             start=True, stop=True).then_inc(imp_done, 1)
            pe.wait_ge(probs_ready, 1)
            for t in range(KT):
                nc.tensor.transpose(m.bank[t // 8][:, (t % 8) * R:(t % 8 + 1) * R], slc[:, t * P:(t + 1) * P],
                                    m.identity[0:R, 0:R])
            for t in range(WT):
                nc.tensor.transpose(m.bank[2][:, t * R:(t + 1) * R], win[:, t * P:(t + 1) * P], m.identity[0:R, 0:R])
            nc.tensor.transpose(m.bank[2][0:N_CMP_D, WT * R:(WT + 1) * R], cmp[:, 0:N_CMP_D], m.identity[0:R, 0:R])
            for n in range(2):
                last = nc.tensor.transpose(m.bank[3][0:DEC, n * R:(n + 1) * R], new_probs[:, n], m.identity[0:R, 0:R])
            last.then_inc(turned, 1)
            pe.wait_ge(turned_kept, 1)
            for b in range(DEC):
                nc.tensor.matmul(m.bank[5][0:R, 0:P], cmp_t[0:N_CMP_D, b], m.vc_cache[0:N_CMP_D, b],
                                 start=b == 0, stop=b == DEC - 1)
            nc.tensor.matmul(m.bank[6][0:R, 0:P], new_t[:, 0], m.kv_a[0:DEC, 8, 384:512], start=True, stop=False,
                             skip_group_check=True)
            nc.tensor.matmul(m.bank[7][0:R, 0:P], new_t[:, 1], m.kv_b[0:DEC, 8, 128:256], start=True, stop=False,
                             skip_group_check=True)
            for b in range(DEC):
                s = b % 2
                pe.wait_ge(v_in[s], 16 * (PAGES + 1) * (b // 2 + 1))
                for t in range(KT):
                    nc.tensor.matmul(m.bank[6][0:R, 0:P], slc_t[:, t, b], ring[:, s, t * P:(t + 1) * P],
                                     start=False, stop=b == DEC - 1 and t == KT - 1, skip_group_check=True)
                for t in range(WT):
                    last = nc.tensor.matmul(m.bank[7][0:R, 0:P], win_t[:, t, b],
                                            ring[:, s, KEYS + t * P:KEYS + (t + 1) * P],
                                            start=False, stop=b == DEC - 1 and t == WT - 1, skip_group_check=True)
                last.then_inc(values_read, 1)

        @block.scalar
        def _(act):
            act.wait_ge(small_in, 48)
            nc.scalar.activation(gate[:], gate[:], ACT.Sigmoid).then_inc(exp_done, 1)
            for n, scores in enumerate((cmp[:, 0:N_CMP_D], win[:], slc[:])):
                act.wait_ge(bars_ready, n + 1)
                nc.scalar.activation(scores, scores, ACT.Exp, scale=SCALE, bias=small[:, 3 + n:4 + n],
                                     accum_out=small[:, 6 + n:7 + n]).then_inc(exp_done, 1)

        @block.vector
        def _(dve):
            step = Chain(dve, step_done)
            step(nc.vector.memset(query[:], 0.0))
            for k in range(KVH):
                half = slice(k * HEAD, (k + 1) * HEAD)
                flat = query[half].rearrange("p b r -> p (b r)")
                for g in range(GQA):
                    at = k * GQA + g
                    last = nc.vector.tensor_copy(flat[:, at:at + (DEC - 1) * 72 + 1:72], m.q_a[half, g, SEQ:T])
                last.then_inc(query_ready, 1)
            dve.wait_ge(scores_done, 1)
            step(nc.vector.tensor_copy(cmp[:, 0:N_CMP_D], m.bank[5][0:R, 0:N_CMP_D]))
            step(nc.vector.tensor_copy(slc[:, KEYS:], m.bank[5][0:R, P:P + 1]))
            step(nc.vector.tensor_copy(win[:, WINDOW:], m.bank[5][0:R, P + 1:P + 2]))

            def exp_bias(n, scores):
                step(nc.vector.tensor_reduce(small[:, n:n + 1], scores, AX.X, ALU.max))
                nc.vector.tensor_scalar(small[:, 3 + n:4 + n], small[:, n:n + 1], -SCALE, None,
                                        ALU.mult).then_inc(bars_ready, 1)

            exp_bias(0, cmp[:, 0:N_CMP_D])
            dve.wait_ge(exp_done, 2)
            step(nc.vector.reciprocal(small[:, 9:10], small[:, 6:7]))
            nc.vector.tensor_scalar(cmp[:, 0:N_CMP_D], cmp[:, 0:N_CMP_D], small[:, 9:10], None,
                                    ALU.mult).then_inc(cmp_probs_ready, 1)
            step(nc.vector.memset(folded[:], 0.0))
            dve.wait_ge(imp_done, 1)
            step(nc.vector.tensor_copy(folded[:, 1:1 + N_CMP_D], m.bank[6][0:R, 0:N_CMP_D]))
            step(nc.vector.tensor_reduce(importance[:], folded[:, 0:4 * N_SEL].rearrange("r (s u) -> r s u", u=4),
                                         AX.X, ALU.add))
            step(nc.vector.tensor_tensor(importance[:], importance[:], folded[:, 4:4 * N_SEL + 1:4], ALU.add))
            step(nc.vector.memset(importance[:, 0:1], FORCED))
            step(nc.vector.memset(importance[:, N_SEL - 2:N_SEL], FORCED))
            dve.wait_ge(mask_in, 16)
            mine = importance[:].rearrange("r (s a) -> r s a", a=1).to_broadcast([R, N_SEL, N_SEL])
            other = importance[:].rearrange("r (a u) -> r a u", a=1).to_broadcast([R, N_SEL, N_SEL])
            step(nc.vector.tensor_tensor(greater, other, mine, ALU.is_gt))
            step(nc.vector.tensor_tensor(equal, other, mine, ALU.is_equal))
            step(nc.vector.tensor_tensor(equal, equal, earlier, ALU.mult))
            step(nc.vector.tensor_tensor(greater, greater, equal, ALU.add))
            step(nc.vector.tensor_reduce(rank[:], greater, AX.X, ALU.add))
            step(nc.vector.tensor_scalar(barred[:], rank[:], float(TOPK), None, ALU.is_ge))
            step(nc.vector.tensor_scalar(barred[:], barred[:], NEG, None, ALU.mult))
            dve.wait_ge(keys_read, DEC)
            step(nc.vector.tensor_copy(win[:, 0:WINDOW], m.bank[4][0:R, :]))
            step(nc.vector.tensor_scalar(win[:, 0:1], win[:, 0:1], NEG, None, ALU.add))
            exp_bias(1, win[:])
            for a in range(4):
                blocks = 512 // 64
                step(nc.vector.tensor_tensor(
                    slc[:, a * 512:(a + 1) * 512].rearrange("r (s u) -> r s u", u=64),
                    m.bank[a][0:R, :].rearrange("r (s u) -> r s u", u=64),
                    barred[:, a * blocks:(a + 1) * blocks].rearrange("r (s a) -> r s a", a=1).to_broadcast([R, blocks, 64]),
                    ALU.add))
            step(nc.vector.tensor_tensor(slc[:, KEYS:], slc[:, KEYS:], barred[:, N_SEL - 1:N_SEL], ALU.add))
            exp_bias(2, slc[:])
            dve.wait_ge(small_in, 48)
            dve.wait_ge(exp_done, 4)
            step(nc.vector.tensor_scalar(new_probs[:, 0], own[:], slc[:, KEYS:], None, ALU.mult))
            step(nc.vector.reciprocal(small[:, 10:12], small[:, 7:9]))
            nc.vector.tensor_scalar(new_probs[:, 1], own[:], win[:, WINDOW:], None, ALU.mult).then_inc(probs_ready, 1)
            for k in range(2):
                head = m.vectors[0:R, V_HEAD0 + k:V_HEAD0 + k + 1]
                step(nc.vector.tensor_scalar(coefficient[:, k], gate[:], head, None, ALU.mult))
                step(nc.vector.tensor_scalar(coefficient[:, k, 0:1], coefficient[:, k, 0:1], small[:, 11:12], None, ALU.mult))
                step(nc.vector.tensor_scalar(coefficient[:, k, 1:2], coefficient[:, k, 1:2], small[:, 10:11], None, ALU.mult))
            dve.wait_ge(turned, 1)
            dve.wait_ge(cleared, 3)

            for t in range(KT):
                flat = slc_t[:, t].rearrange("p b r -> p (b r)")
                nc.vector.tensor_copy(spread(flat, P), m.bank[t // 8][:, (t % 8) * R:(t % 8 + 1) * R]
                                      .rearrange("p (b h) -> p b h", b=DEC))
            for t in range(WT):
                nc.vector.tensor_copy(spread(win_t[:, t].rearrange("p b r -> p (b r)"), P),
                                      m.bank[2][:, t * R:(t + 1) * R].rearrange("p (b h) -> p b h", b=DEC))
            nc.vector.tensor_copy(spread(cmp_t[0:N_CMP_D].rearrange("p b r -> p (b r)"), N_CMP_D),
                                  m.bank[2][0:N_CMP_D, WT * R:(WT + 1) * R].rearrange("p (b h) -> p b h", b=DEC))
            nc.vector.tensor_copy(new_t[:].rearrange("b n r -> b (n r)"), m.bank[3][0:DEC, 0:2 * R]).then_inc(turned_kept, 1)
            dve.wait_ge(values_read, DEC)
            for n in range(3):
                for k in range(2):
                    source = m.bank[5 + n][0:R, k * HEAD:(k + 1) * HEAD]
                    c = coefficient[:, k, (2, 0, 1)[n]:(2, 0, 1)[n] + 1]
                    if n == 0 and k == 0:
                        step(nc.vector.tensor_scalar(out[:], source, c, None, ALU.mult))
                    else:
                        step(nc.vector.scalar_tensor_tensor(out=out[:], in0=source, scalar=c, in1=out[:],
                                                            op0=ALU.mult, op1=ALU.add))
            nc.vector.tensor_copy(out[:], out[:]).then_inc(out_ready, 1)


def spread(flat, partitions):
    R = DEC * KVH * GQA
    wide = flat.rearrange("p (b r) -> p b r", b=DEC)
    first = wide[:, 0:1, 0:8]
    return bass.AP(tensor=first.tensor, offset=first.offset, ap=[list(first.ap[0]), [R + 8, DEC], [1, 8]])


def mix_features(nc, m):
    with ExitStack() as stack:
        sem = phase(nc, stack)
        squares = stack.enter_context(nc.sbuf_tensor("row_squares", [P, 512], F32))
        sums = stack.enter_context(nc.sbuf_tensor("mix_sums", [P, 9, 5], F32))
        tile = stack.enter_context(nc.sbuf_tensor("mix_tile", [P, 2, KC, P], F32))
        high_ready, low_ready = sem("mix_high_ready"), sem("mix_low_ready")
        ready = sem("mix_sums_clear")
        summed = sem("mix_summed")
        rooted = sem("mix_rooted")
        inverted = sem("mix_inverted")
        scaled = sem("mix_scaled")
        turned = sem("mix_turned")
        kept_act, kept_dve = sem("mix_kept_by_scalar"), sem("mix_kept_by_vector")
        block = stack.enter_context(nc.Block())

        @block.scalar
        def _(act):
            act.wait_ge(ready, 1)
            for i, (first, count) in enumerate(TILES):
                act_step = 0
                nc.scalar.activation(squares[0:count], m.o_nsa[0:count, i], ACT.Square,
                                     accum_out=sums[0:count, i, 0:1]).then_inc(summed, 1)
                act.wait_ge(summed, 5 * i + 1)
                for h in range(HGH):
                    nc.scalar.activation(squares[0:count, h * P:(h + 1) * P], m.v_hg[0:count, i, h * P:(h + 1) * P],
                                         ACT.Square, accum_out=sums[0:count, i, 1 + h:2 + h]).then_inc(summed, 1)
                act.wait_ge(summed, 5 * i + 5)
            eps = m.vectors[:, V_EPS:V_EPS + 1]
            nc.scalar.activation(sums[:, :, 0], sums[:, :, 0], ACT.Sqrt, scale=1.0 / NSA, bias=eps).then_inc(rooted, 1)
            nc.scalar.activation(sums[:, :, 1:5], sums[:, :, 1:5], ACT.Sqrt, scale=1.0 / P, bias=eps).then_inc(rooted, 1)
            for i, (first, count) in enumerate(TILES):
                act.wait_ge(turned, 2 * i + 1)
                if i >= 2:
                    act.wait_ge(low_ready, i - 1)
                for c in range(4):
                    last = nc.scalar.activation(tile[:, i % 2, c, 0:count],
                                                m.bank[2 * (i % 2)][:, c * P:c * P + count], ACT.Copy,
                                                scale=m.vectors[:, V_NSA + c:V_NSA + c + 1])
                last.then_inc(kept_act, 1)
                act.wait_ge(kept_act, i + 1)
                act.wait_ge(kept_dve, i + 1)
                nc.scalar.activation(m.xn[0][:, :, first:first + count], tile[:, i % 2, :, 0:count],
                                     ACT.Copy).then_inc(high_ready, 1)

        @block.vector
        def _(dve):
            nc.vector.memset(sums[:], 1.0).then_inc(ready, 1)
            dve.wait_ge(rooted, 2)
            nc.vector.reciprocal(sums[:], sums[:]).then_inc(inverted, 1)
            dve.wait_ge(inverted, 1)

            def scale(i):
                count = TILES[i][1]
                nc.vector.tensor_scalar(m.o_nsa[0:count, i], m.o_nsa[0:count, i], sums[0:count, i, 0:1], None, ALU.mult)
                v = m.v_hg[0:count, i].rearrange("p (h d) -> p h d", h=HGH)
                nc.vector.tensor_tensor(v, v, sums[0:count, i, 1:5].rearrange("p (h a) -> p h a", a=1)
                                        .to_broadcast([count, HGH, P]), ALU.mult).then_inc(scaled, 1)

            scale(0)
            for i, (first, count) in enumerate(TILES):
                if i + 1 < 9:
                    scale(i + 1)
                dve.wait_ge(turned, 2 * i + 2)
                if i >= 2:
                    dve.wait_ge(low_ready, i - 1)
                for c in range(4):
                    last = nc.vector.scalar_tensor_tensor(
                        out=tile[:, i % 2, 4 + c, 0:count], in0=m.bank[2 * (i % 2) + 1][:, c * P:c * P + count],
                        scalar=m.vectors[:, V_HG + c:V_HG + c + 1], in1=m.gate_b[:, c, first:first + count],
                        op0=ALU.mult, op1=ALU.mult)
                last.then_inc(kept_dve, 1)
                dve.wait_ge(high_ready, i + 1)
                nc.vector.tensor_tensor(m.xn[1][:, :, first:first + count], tile[:, i % 2, :, 0:count],
                                        m.xn[0][:, :, first:first + count].bitcast(F32), ALU.subtract).then_inc(low_ready, 1)

        @block.tensor
        def _(pe):
            for i, (first, count) in enumerate(TILES):
                pe.wait_ge(scaled, i + 1)
                if i >= 2:
                    pe.wait_ge(kept_act, i - 1)
                    pe.wait_ge(kept_dve, i - 1)
                for n, source in enumerate((m.o_nsa, m.v_hg)):
                    for c in range(4):
                        last = nc.tensor.transpose(m.bank[2 * (i % 2) + n][:, c * P:c * P + count],
                                                   source[0:count, i, c * P:(c + 1) * P], m.identity[0:count, 0:count])
                    last.then_inc(turned, 1)


def add_linear(nc, m, name, weights, source, chunks_in):
    with ExitStack() as stack:
        sem = phase(nc, stack)
        w = SplitWeights(nc, stack, sem, name, lambda i, s: weights(i * 2 + s), (chunks_in, chunks_in))
        banks_free = [sem(f"{name}_banks_free{s}") for s in range(2)]
        block = stack.enter_context(nc.Block())
        turns = KC // 2

        @block.sync
        def _(sp):
            w.load_all(sp, turns)

        @block.tensor
        def _(pe):
            with pe.Fori(0, turns) as i:
                for s in range(2):
                    pe.wait_ge(w.ready[s], i + 1)
                    for g in range(GROUPS):
                        pe.wait_ge(banks_free[s], i * GROUPS + (g + 1))
                        w.product(m.bank[3 * s + g][:, 0:G], s, source, g)

        @block.scalar
        def _(act):
            for s in range(2):
                w.make_high(act, 0, s, first=True)
            with act.Fori(1, turns) as i:
                for s in range(2):
                    w.make_high(act, i, s)

        @block.vector
        def _(dve):
            for s in range(2):
                dve.sem_inc(banks_free[s], GROUPS)
                w.make_low(dve, 0, s)

            def work(i, last):
                for s in range(2):
                    for g in range(GROUPS):
                        dve.wait_ge(w.done[s], i * GROUPS + (g + 1))
                        h = m.h[:, bass.ds(i * 2 + s, 1), cols(g)].rearrange("p a t -> p (a t)")
                        nc.vector.tensor_tensor(h, m.bank[3 * s + g][:, 0:G], h, ALU.add).then_inc(banks_free[s], 1)
                    if not last:
                        w.make_low(dve, i + 1, s)

            turns_but_last(dve, turns, work)


def gated_pair(nc, m, name, weights, sources, counts, turns, function, finish):
    with ExitStack() as stack:
        sem = phase(nc, stack)
        w = SplitWeights(nc, stack, sem, name, weights, counts)
        active = stack.enter_context(nc.sbuf_tensor(f"{name}_active", [P, GROUPS, G], F32))
        result = stack.enter_context(nc.sbuf_tensor(f"{name}_result", [P, GROUPS, G], F32))
        active_ready = sem(f"{name}_active_ready")
        multiplied = sem(f"{name}_multiplied")
        finished = sem(f"{name}_finished")
        high_kept = sem(f"{name}_high_kept")
        block = stack.enter_context(nc.Block())

        @block.sync
        def _(sp):
            w.load_all(sp, turns)

        @block.tensor
        def _(pe):
            with pe.Fori(0, turns) as i:
                for s in range(2):
                    pe.wait_ge(w.ready[s], i + 1)
                    for g in range(GROUPS):
                        pe.wait_ge(multiplied, i * GROUPS + (g + 1))
                        w.product(m.bank[3 * s + g][:, 0:G], s, sources[s], g)

        @block.scalar
        def _(act):
            for s in range(2):
                w.make_high(act, 0, s, first=True)

            def work(i, last):
                if not last:
                    w.make_high(act, i + 1, 0)
                for g in range(GROUPS):
                    act.wait_ge(w.done[0], i * GROUPS + (g + 1))
                    act.wait_ge(multiplied, i * GROUPS + (g + 1))
                    nc.scalar.activation(active[:, g], m.bank[g][:, 0:G], function).then_inc(active_ready, 1)
                for g in range(GROUPS):
                    if finish.high is not None:
                        act.wait_ge(multiplied, (i + 1) * GROUPS + (g + 1))
                        nc.scalar.activation(finish.high(i, g), result[:, g], ACT.Copy).then_inc(high_kept, 1)
                if not last:
                    w.make_high(act, i + 1, 1)

            turns_but_last(act, turns, work)

        @block.vector
        def _(dve):
            dve.sem_inc(multiplied, GROUPS)
            for s in range(2):
                w.make_low(dve, 0, s)

            def work(i, last):
                if not last:
                    w.make_low(dve, i + 1, 0)
                for g in range(GROUPS):
                    dve.wait_ge(active_ready, i * GROUPS + (g + 1))
                    dve.wait_ge(w.done[1], i * GROUPS + (g + 1))
                    nc.vector.tensor_tensor(result[:, g], m.bank[3 + g][:, 0:G], active[:, g],
                                            ALU.mult).then_inc(multiplied, 1)
                    if finish.high is not None:
                        dve.wait_ge(high_kept, i * GROUPS + (g + 1))
                        nc.vector.tensor_tensor(finish.low(i, g), result[:, g], finish.high(i, g).bitcast(F32),
                                                ALU.subtract).then_inc(finished, 1)
                    else:
                        dve.wait_ge(multiplied, (i + 1) * GROUPS + (g + 1))
                        h = m.h[:, bass.ds(i, 1), cols(g)].rearrange("p a t -> p (a t)")
                        nc.vector.tensor_tensor(h, h, result[:, g], ALU.add).then_inc(finished, 1)
                if not last:
                    w.make_low(dve, i + 1, 1)

            turns_but_last(dve, turns, work)


class SplitInto:

    def __init__(self, high=None, low=None):
        self.high, self.low = high, low


PARTS = ((0, 8), (8, 8), (16, 6))


def feed_forward(nc, m):
    for n, (first, count) in enumerate(PARTS):
        def place(tensor):
            return lambda i, g: tensor[:, bass.ds(i, 1), cols(g)].rearrange("p a t -> p (a t)")

        def chunk(i, s, first=first):
            return m.dram["w_gate_up"][i + first, :, s * KC:(s + 1) * KC]

        gated_pair(nc, m, f"ffn{n}", chunk, (m.xn, m.xn), (KC, KC), count, ACT.Silu,
                   SplitInto(place(m.hidden[0]), place(m.hidden[1])))
        add_linear(nc, m, f"down{n}", lambda c, first=first, count=count: m.dram["w_down"][c, :, first:first + count],
                   m.hidden, count)
        clear_semaphores(nc)


def gated_embedding(nc, m):
    gated_pair(nc, m, "ple", lambda i, s: m.dram["w_ple"][i, :, s * KC:s * KC + (KC, DPLE // P)[s]],
               (m.xn, m.p_in), (KC, DPLE // P), KC, ACT.Sigmoid, SplitInto())


def load_residual(nc, m):
    with ExitStack() as stack:
        sem = phase(nc, stack)
        loaded = sem("residual_loaded")
        block = stack.enter_context(nc.Block())

        @block.sync
        def _(sp):
            sp.dma_start(m.h[:], m.dram["x"]).then_inc(loaded, 16)
            sp.wait_ge(loaded, 16)


def load_embedding(nc, m):
    with ExitStack() as stack:
        sem = phase(nc, stack)
        raw = stack.enter_context(nc.sbuf_tensor("p_raw", [P, DPLE // P, T], F32))
        loaded = sem("embedding_loaded")
        high_ready = sem("p_high_ready")
        block = stack.enter_context(nc.Block())

        @block.sync
        def _(sp):
            sp.dma_start(raw[:], m.dram["p"]).then_inc(loaded, 16)

        @block.scalar
        def _(act):
            act.wait_ge(loaded, 16)
            nc.scalar.activation(m.p_in[0][:], raw[:], ACT.Copy).then_inc(high_ready, 1)

        @block.vector
        def _(dve):
            dve.wait_ge(high_ready, 1)
            nc.vector.tensor_tensor(m.p_in[1][:], raw[:], m.p_in[0][:].bitcast(F32), ALU.subtract)


def store_result(nc, m):
    with ExitStack() as stack:
        sem = phase(nc, stack)
        stored = sem("result_stored")
        block = stack.enter_context(nc.Block())

        @block.sync
        def _(sp):
            sp.dma_start(m.dram["out_y"], m.result[:]).then_inc(stored, 16)
            sp.wait_ge(stored, 16)


def load_inputs(nc, m, d):
    with ExitStack() as stack:
        sem = phase(nc, stack)
        loaded = sem("inputs_loaded")
        block = stack.enter_context(nc.Block())

        @block.sync
        def _(sp):
            pairs = ((m.identity, d["identity"]), (m.mean_weights, d["mean_weights"]), (m.vectors, d["vectors"]),
                     (m.intra_mask, d["intra_mask"]), (m.row_pick, d["row_pick"]), (m.x_in, d["x"]))
            for target, source in pairs:
                sp.dma_start(target[:], source).then_inc(loaded, 16)
            sp.wait_ge(loaded, 16 * len(pairs))


def layer(nc, d):
    m = Tensors(d)
    with ExitStack() as stack:
        def sb(name, shape, dtype=F32):
            return stack.enter_context(nc.sbuf_tensor(name, shape, dtype))

        psum = stack.enter_context(nc.psum_tensor("banks", [P, 8 * 512], F32))
        m.bank = [psum[:, i * 512:(i + 1) * 512] for i in range(8)]
        m.pair = [psum[:, i * 1024:(i + 1) * 1024] for i in range(2)]
        m.turn_bank = m.bank[4:6]
        m.identity = sb("identity_sb", [P, P])
        m.mean_weights = sb("mean_weights_sb", [P, P])
        m.vectors = sb("vectors_sb", [P, V_COLS])
        m.lower = sb("lower_bound", [P, 20])
        m.intra_mask = sb("intra_mask_sb", [P, P])
        m.row_pick = sb("row_pick_sb", [DEC, DEC, P])
        m.table = sb("table", [1, DEC * PAGES], I32)
        start = -(-nc.sbuf_base // 32) * 32
        m.xn = (sb("xn_high", [P, KC, T], F32R), sb("xn_low", [P, KC, T], F32R))
        m.over_xn = lambda: Overlay(nc, start, 2 * 4 * KC * T)
        mixers(nc, m, d)
        m.h = sb("h", [P, KC, T])
        load_residual(nc, m)
        add_linear(nc, m, "out", lambda c: m.dram["w_out"][c], m.xn, KC)
        rms_norm_features(nc, m, "ffn", m.h, V_FFN, m.xn)
        with ExitStack() as ffn:
            m.hidden = tuple(ffn.enter_context(nc.sbuf_tensor(f"ffn_hidden_{part}", [P, KC, T], F32R))
                             for part in ("high", "low"))
            feed_forward(nc, m)
        rms_norm_features(nc, m, "ple", m.h, V_PLE, m.xn)
        m.p_in = (sb("p_high", [P, DPLE // P, T], F32R), sb("p_low", [P, DPLE // P, T], F32R))
        load_embedding(nc, m)
        gated_embedding(nc, m)
        m.result = sb("result", [P, KC, T])
        rms_norm_features(nc, m, "final", m.h, V_FINAL, m.result)
        store_result(nc, m)


def mixers(nc, m, d):
    with ExitStack() as stack:
        def sb(name, shape, dtype=F32):
            return stack.enter_context(nc.sbuf_tensor(name, shape, dtype))

        m.v_hg = sb("v_hg", [P, 9, 512])
        with ExitStack() as start:
            m.x_in = start.enter_context(nc.sbuf_tensor("x_in", [P, KC, T], F32))
            load_inputs(nc, m, d)
            lower_bound(nc, m)
            rms_norm_features(nc, m, "mix", m.x_in, V_MIX, m.xn)
        with ExitStack() as recurrent:
            m.q_b = recurrent.enter_context(nc.sbuf_tensor("q_b", [P, 4, T], F32))
            m.forget = recurrent.enter_context(nc.sbuf_tensor("forget", [P, 4, T], F32))
            project_features(nc, m, "recurrent", 0, ((m.q_b, ACT.Silu), (m.forget, ACT.Sigmoid)))
            project_tokens(nc, m, "values", ((m.v_hg, 792, 512),))
            hgrn_prompt(nc, m)
            hgrn_decode(nc, m)
        m.gate_b = sb("gate_b", [P, 4, T])
        m.q_a = sb("q_a", [P, 4, T])
        m.k_slc = sb("k_slc_t", [P, T])
        m.k_win = sb("k_win_t", [P, T])
        m.kv_a = sb("kv_a", [P, 9, 512])
        m.kv_b = sb("kv_b", [P, 9, 280])
        project_features(nc, m, "query", 8, ((m.q_a, ACT.Copy), (m.gate_b, ACT.Silu)))
        project_tokens(nc, m, "kv", ((m.kv_a, 0, 512), (m.kv_b, 512, 280)),
                       ((m.kv_a[:, :, 256:384], m.k_slc), (m.kv_b[:, :, 0:128], m.k_win)), store_rows(m))
        m.kc_prompt, m.vc_prompt = sb("kc_prompt", [P, P]), sb("vc_prompt", [P, P])
        m.kc_cache, m.vc_cache = sb("kc_cache", [P, DEC, P]), sb("vc_cache", [P, DEC, P])
        m.w1 = m.over_xn()("compress_w1", [P, 2, 2, PAIRS, HID])
        with ExitStack() as compression:
            def csb(name, shape):
                return compression.enter_context(nc.sbuf_tensor(name, shape, F32))

            m.w2_k, m.w2_v = csb("w2_k", [P, 2, KVH, P]), csb("w2_v", [P, 2, HEAD])
            m.pos, m.hidden_bias = csb("pos", [P, 2, 2, PAIRS]), csb("hidden_bias", [P, 4])
            compress(nc, m, True)
            compress(nc, m, False)
        m.o_nsa = sb("o_nsa", [P, 9, NSA])
        clear_semaphores(nc)
        with ExitStack() as attention:
            m.gates = attention.enter_context(nc.sbuf_tensor("gates", [P, QT, 24], F32))
            gates_sigmoid(nc, m)
            prompt_attention(nc, m)
        decode_attention(nc, m)
        mix_features(nc, m)
        clear_semaphores(nc)


def constants():
    f = np.float32
    s, t = np.arange(P)[:, None], np.arange(P)[None, :]
    c = {}
    c["identity"] = np.eye(P, dtype=f)
    c["mean_weights"] = np.full((P, P), 1.0 / DM, f)
    c["intra_mask"] = ((s // BLOCK32 == t // BLOCK32) & (s <= t)).astype(f)
    c["row_pick"] = np.repeat(np.eye(DEC, dtype=f)[:, :, None], P, axis=2)
    q, k = s, t
    c["causal_add"] = np.where(k > q, f(NEG), f(0))
    c["window_add"] = np.where(k <= q, f(NEG), f(0))
    keep = HALF * (np.arange(56 + P)[None, :] - 56) + 31 <= s
    c["cmp_keep"] = keep.astype(f)
    c["cmp_add"] = np.where(keep, f(0), f(NEG))
    r = np.arange(DEC * KVH * GQA)
    c["group_sum"] = (r[:, None] // GQA == r[None, :] // GQA).astype(f)
    c["own_column"] = (r[:, None] // 8 == np.arange(DEC)[None, :]).astype(f)
    b = np.arange(N_SEL)
    c["earlier"] = np.tile((b[None, :] < b[:, None]).astype(f).reshape(1, -1), (len(r), 1))
    return c


def columns(v):
    return v.reshape(-1, P).T


def weight_chunks(w, order=None):
    k, n = w.shape
    return np.ascontiguousarray(w.reshape(k // P, P, n // P, P).transpose(2, 1, 0, 3))


def laid_out(i):
    a = {}
    x = np.concatenate([i["x_prompt"][0], i["x_sample"][:, 0]])
    a["x"] = np.ascontiguousarray(x.T.reshape(KC, P, T).transpose(1, 0, 2))
    w = i["w_in"][0]
    start = np.cumsum([0, 512, 256, 256, 256, 24, 512, 512, 512, 512])
    qa, kvc, kvs, kvw, gate, qb, fb, vb, gb = (w[:, start[n]:start[n + 1]] for n in range(9))
    qa = qa.reshape(DM, KVH, GQA, HEAD).transpose(0, 2, 1, 3).reshape(DM, NSA)
    a["w_feature"] = weight_chunks(np.concatenate([qb, fb, qa, gb], axis=1))
    gate = gate.reshape(DM, 3, KVH * GQA)[:, [1, 2, 0]].transpose(0, 2, 1).reshape(DM, 24)
    token = np.concatenate([kvc, kvs, kvw, gate, vb], axis=1)
    a["w_token"] = np.ascontiguousarray(token.reshape(KC, P, -1).transpose(1, 0, 2))
    v = [i["norm_mix"][0], i["norm_nsa_out"][0], i["norm_hg_out"][0], i["norm_ffn"][0], i["norm_ple"][0],
         i["norm_final"], i["hg_lb"][0], i["hg_lb"][1]]
    extra = np.zeros((P, 3), np.float32)
    extra[:, 0] = 1e-6
    extra[:, 1] = np.arange(P) // 4 % 2 == 0
    extra[:, 2] = np.arange(P) // 4 % 2 == 1
    a["vectors"] = np.concatenate([np.ascontiguousarray(columns(x)) for x in v] + [extra], axis=1)
    a["window_rows"] = i["state_kv_win"][0].reshape(DEC, WINDOW, 256)
    a["state_hgrn"] = i["state_hgrn"][0]
    a["w_out"] = weight_chunks(i["w_out"][0])
    gate_up = i["w_gate_up"][0]
    a["w_gate_up"] = np.concatenate([weight_chunks(gate_up[:, :DFF]), weight_chunks(gate_up[:, DFF:])], axis=2)
    a["w_down"] = weight_chunks(i["w_down"][0])
    a["w_ple"] = np.concatenate([weight_chunks(i["w_ple_gate"][0]), weight_chunks(i["w_ple_proj"][0])], axis=2)
    p = np.concatenate([i["p_prompt"][0, 0], i["p_sample"][0, :, 0]])
    a["p"] = np.ascontiguousarray(p.T.reshape(DPLE // P, P, T).transpose(1, 0, 2))
    a["cmp_w1"] = np.ascontiguousarray(i["cmp_w1"][0].reshape(2, 2, PAIRS, P, HID).transpose(3, 0, 1, 2, 4))
    a["cmp_pos"] = np.ascontiguousarray(i["cmp_pos"][0].reshape(2, 2, PAIRS, P).transpose(3, 0, 1, 2))
    w2 = i["cmp_w2"][0].reshape(2, 2, P, HEAD)
    w2_k = np.zeros((P, 2, KVH, KVH, HEAD), np.float32)
    for k in range(KVH):
        w2_k[:, :, k, k] = w2[0].transpose(1, 0, 2)
    a["cmp_w2_k"] = w2_k.reshape(P, 2, KVH, P)
    a["cmp_w2_v"] = np.ascontiguousarray(w2[1].transpose(1, 0, 2))
    cache = i["cache_kv_cmp"][0].reshape(POOL, PAGE // HALF, PAIRS, 2, 2, KVH, HEAD)
    a["cache_cmp"] = np.ascontiguousarray(cache.transpose(0, 3, 6, 2, 4, 5, 1)).reshape(POOL, P, 256)
    cache = i["cache_kv_slc"][0].reshape(POOL, PAGE, 2, P)
    a["slc_k"] = np.ascontiguousarray(cache[:, :, 0].transpose(0, 2, 1))
    a["slc_v"] = np.ascontiguousarray(cache[:, :, 1])
    window = i["state_kv_win"][0].reshape(DEC, WINDOW, 2, P)
    a["win_k"] = np.ascontiguousarray(window[:, :, 0].transpose(0, 2, 1))
    a["win_v"] = np.ascontiguousarray(window[:, :, 1].reshape(DEC, 4, P, P).transpose(0, 2, 1, 3)).reshape(DEC, P, WINDOW)
    a["page_table"] = i["page_table"].reshape(1, -1)
    a.update(constants())
    return a


OUTPUTS = {
    "out_cmp_p": (SEQ, 256), "out_slc_p": (SEQ, 256), "out_win_p": (WINDOW, 256), "out_hgrn_p": (HGH, P, P),
    "out_cmp_s": (DEC, 256), "out_slc_s": (DEC, 256), "out_win_s": (DEC, WINDOW, 256),
    "out_hgrn_s": (DEC, HGH, P, P), "out_y": (P, KC, T),
}
SCRATCH = {"gate_rows": (DEC, 8, 3), "o_rows": (DEC * KVH * GQA, HEAD)}


def kernel(**inputs):
    import concourse.bacc as bacc
    from concourse.bass_utils import run_bass_kernel_spmd

    nc = bacc.Bacc("TRN2", target_bir_lowering=False, num_devices=1)
    arrays = {}
    handles = {}
    for name, a in laid_out({k: np.asarray(v) for k, v in inputs.items()}).items():
        arrays["in_" + name] = np.ascontiguousarray(a)
        handles[name] = nc.dram_tensor("in_" + name, a.shape, mybir.dt.from_np(a.dtype), kind="ExternalInput").ap()
    for name, shape in OUTPUTS.items():
        handles[name] = nc.dram_tensor(name, shape, F32, kind="ExternalOutput").ap()
    for name, shape in SCRATCH.items():
        handles[name] = nc.dram_tensor(name, shape, F32, kind="Internal").ap()
    layer(nc, handles)
    r = run_bass_kernel_spmd(nc, [arrays], core_ids=[0]).results[0]
    y = r["out_y"].transpose(1, 0, 2).reshape(DM, T).T
    kv = (2, KVH, HEAD)
    return (
        y[None, :SEQ], y[SEQ:, None],
        r["out_cmp_p"].reshape(1, 1, SEQ, *kv), r["out_slc_p"].reshape(1, 1, SEQ, *kv),
        r["out_win_p"].reshape(1, 1, WINDOW, *kv), r["out_hgrn_p"][None, None],
        r["out_cmp_s"].reshape(1, DEC, 1, *kv), r["out_slc_s"].reshape(1, DEC, 1, *kv),
        r["out_win_s"].reshape(1, DEC, WINDOW, *kv), r["out_hgrn_s"][None],
    )
```

```python
from contextlib import ExitStack

import concourse.bass as bass
import concourse.mybir as mybir
from concourse.alu_op_type import AluOpType as ALU
import numpy as np

ACT = mybir.ActivationFunctionType
F32 = mybir.dt.float32
I32 = mybir.dt.int32
F32R = mybir.dt.float32r
AX = mybir.AxisListType

P = 128
SEQ, DEC = 1024, 8
T = SEQ + DEC
GROUPS = 3
G = T // GROUPS
DM, DFF, DPLE = 1024, 2816, 256
KC = DM // P
PAGES, PAGE, POOL = 16, 128, 160
HEAD, KVH, GQA = 64, 2, 4
NSA, HGH = 512, 4
WINDOW = 512
N_CMP_D = 127
N_SEL = 33
SEL = 64
TOPK = 16
SCALE = HEAD ** -0.5
NEG = -1e30
FORCED = 1e9
TILES = [(i * P, min(P, T - i * P)) for i in range(9)]
QT = SEQ // P
BLOCK32 = 32
V_MIX, V_NSA, V_HG, V_FFN, V_PLE, V_FINAL, V_LB, V_EPS = 0, 8, 12, 16, 24, 32, 40, 48
V_HEAD0, V_HEAD1, V_COLS = 49, 50, 51


class Chain:

    def __init__(self, engine, semaphore, count=0):
        self.engine, self.semaphore, self.count = engine, semaphore, count

    def __call__(self, instruction):
        instruction.then_inc(self.semaphore, 1)
        self.count = self.count + 1
        self.engine.wait_ge(self.semaphore, self.count)


class Tensors:

    def __init__(self, dram):
        self.dram = dram


class Overlay:

    def __init__(self, nc, start, size):
        self.nc, self.at, self.end = nc, start, start + size

    def __call__(self, name, shape, dtype=F32):
        tensor = self.nc.alloc_sbuf_tensor_at(name, shape, dtype, offset=self.at)
        self.at += 32 * -(-4 * int(np.prod(shape[1:])) // 32)
        assert self.at <= self.end
        return tensor


USED = []


def phase(nc, stack):
    def sem(name):
        USED.append(stack.enter_context(nc.semaphore(name)))
        return USED[-1]
    return sem


def clear_semaphores(nc):
    for semaphore in USED:
        nc.sync.sem_clear(semaphore)
    USED.clear()
    nc.all_engine_barrier()


def cols(group):
    return slice(group * G, (group + 1) * G)


def load_and_split(nc, m):
    with ExitStack() as stack:
        sem = phase(nc, stack)
        SLOTS = 4
        x = stack.enter_context(nc.sbuf_tensor("x_chunk", [P, SLOTS, T], F32))
        squares = stack.enter_context(nc.sbuf_tensor("x_squares", [P, 2, T], F32))
        constants_in, vectors_in = sem("constants_in"), sem("vectors_in")
        arrived = [sem(f"x_arrived{s}") for s in range(SLOTS)]
        high_ready, squared = sem("x_high_ready"), sem("x_squared")
        low_ready = sem("x_low_ready")
        odd_total = stack.enter_context(nc.sbuf_tensor("x_odd_total", [P, T], F32))
        added = [sem("x_even_added"), sem("x_odd_added")]
        block = stack.enter_context(nc.Block())

        @block.sync
        def _(sp):
            sp.dma_start(m.vectors[:], m.dram["vectors"]).then_inc(vectors_in, 16)
            for c in range(KC):
                if c >= SLOTS:
                    sp.wait_ge(low_ready, c - SLOTS + 1)
                    sp.wait_ge(squared, c - SLOTS + 1)
                sp.dma_start(x[:, c % SLOTS], m.dram["x"][:, c]).then_inc(arrived[c % SLOTS], 16)
            pairs = ((m.identity, "identity"), (m.mean_weights, "mean_weights"), (m.intra_mask, "intra_mask"),
                     (m.row_pick, "row_pick"))
            for target, source in pairs:
                sp.dma_start(target[:], m.dram[source]).then_inc(constants_in, 16)
            sp.wait_ge(constants_in, 16 * len(pairs))

        @block.scalar
        def _(act):
            act.wait_ge(vectors_in, 16)
            for c in range(KC):
                act.wait_ge(arrived[c % SLOTS], 16 * (c // SLOTS + 1))
                nc.scalar.activation(m.xn[0][:, c], x[:, c % SLOTS], ACT.Copy,
                                     scale=m.vectors[:, V_MIX + c:V_MIX + c + 1]).then_inc(high_ready, 1)
                if c >= 2:
                    act.wait_ge(added[c % 2], c // 2 + 1)
                nc.scalar.activation(squares[:, c % 2], x[:, c % SLOTS], ACT.Square).then_inc(squared, 1)

        @block.vector
        def _(dve):
            nc.vector.memset(m.total[:], 0.0).then_inc(added[0], 1)
            for c in range(KC):
                dve.wait_ge(high_ready, c + 1)
                nc.vector.scalar_tensor_tensor(out=m.xn[1][:, c], in0=x[:, c % SLOTS],
                                               scalar=m.vectors[:, V_MIX + c:V_MIX + c + 1],
                                               in1=m.xn[0][:, c].bitcast(F32), op0=ALU.mult,
                                               op1=ALU.subtract).then_inc(low_ready, 1)
                if c % 2 == 0:
                    dve.wait_ge(squared, c + 1)
                    dve.wait_ge(added[0], c // 2 + 1)
                    nc.vector.tensor_tensor(m.total[:], m.total[:], squares[:, 0], ALU.add).then_inc(added[0], 1)
            dve.wait_ge(added[0], KC // 2 + 1)
            dve.wait_ge(added[1], KC // 2 + 1)
            nc.vector.tensor_tensor(m.total[:], m.total[:], odd_total[:], ALU.add)

        @block.gpsimd
        def _(pool):
            nc.gpsimd.memset(odd_total[:], 0.0).then_inc(added[1], 1)
            for c in range(1, KC, 2):
                pool.wait_ge(squared, c + 1)
                pool.wait_ge(added[1], c // 2 + 1)
                nc.gpsimd.tensor_tensor(odd_total[:], odd_total[:], squares[:, 1], ALU.add).then_inc(added[1], 1)


class NormFactor:

    def __init__(self, nc, m, sem, name, banks):
        self.nc, self.m, self.banks = nc, m, banks
        self.mean_ready = sem(f"{name}_mean_ready")
        self.root_ready = sem(f"{name}_root_ready")
        self.ready = sem(f"{name}_factor_ready")

    def mean(self, pe):
        for g in range(GROUPS):
            self.nc.tensor.matmul(self.banks[g][:, 0:G], self.m.mean_weights[:], self.m.total[:, cols(g)],
                                  start=True, stop=True).then_inc(self.mean_ready, 1)

    def root(self, act):
        for g in range(GROUPS):
            act.wait_ge(self.mean_ready, g + 1)
            self.nc.scalar.activation(self.m.scale[:, cols(g)], self.banks[g][:, 0:G], ACT.Sqrt,
                                      bias=self.m.vectors[:, V_EPS:V_EPS + 1]).then_inc(self.root_ready, 1)

    def invert(self, dve):
        for g in range(GROUPS):
            dve.wait_ge(self.root_ready, g + 1)
            scale = self.m.scale[:, cols(g)]
            self.nc.vector.reciprocal(scale, scale).then_inc(self.ready, 1)
        dve.wait_ge(self.ready, GROUPS)


def final_norm(nc, m):
    with ExitStack() as stack:
        sem = phase(nc, stack)
        result = stack.enter_context(nc.sbuf_tensor("result", [P, KC, T], F32))
        factor = NormFactor(nc, m, sem, "final", m.bank[0:3])
        normed, stored = sem("final_normed"), sem("result_stored")
        block = stack.enter_context(nc.Block())

        @block.tensor
        def _(pe):
            factor.mean(pe)

        @block.scalar
        def _(act):
            factor.root(act)

        @block.vector
        def _(dve):
            factor.invert(dve)
            for c in range(KC):
                nc.vector.scalar_tensor_tensor(out=result[:, c], in0=m.h[:, c],
                                               scalar=m.vectors[:, V_FINAL + c:V_FINAL + c + 1],
                                               in1=m.scale[:], op0=ALU.mult, op1=ALU.mult).then_inc(normed, 1)

        @block.sync
        def _(sp):
            for c in range(KC):
                sp.wait_ge(normed, c + 1)
                sp.dma_start(m.dram["out_y"][:, c], result[:, c]).then_inc(stored, 16)
            sp.wait_ge(stored, 16 * KC)


class SplitBuffers:

    def __init__(self, nc, stack, name, most):
        self.raw = stack.enter_context(nc.sbuf_tensor(f"{name}_raw", [P, 2, most, P], F32))
        self.high = stack.enter_context(nc.sbuf_tensor(f"{name}_high", [P, 2, most, P], F32R))
        self.low = stack.enter_context(nc.sbuf_tensor(f"{name}_low", [P, 2, most, P], F32R))


class Weights:

    def __init__(self, source, counts):
        self.source, self.counts = source, counts


class SplitWeights:

    def __init__(self, nc, sem, name, buffers, weights, primed=False, following=None):
        self.nc, self.weights, self.primed, self.following = nc, weights, primed, following
        self.raw, self.high, self.low = buffers.raw, buffers.high, buffers.low
        self.arrived = [sem(f"{name}_arrived{s}") for s in range(2)]
        self.high_ready = [sem(f"{name}_high_ready{s}") for s in range(2)]
        self.ready = [sem(f"{name}_split_ready{s}") for s in range(2)]
        self.done = [sem(f"{name}_product_done{s}") for s in range(2)]

    def load_all(self, sp, turns):
        def load(weights, turn, s):
            sp.dma_start(self.raw[:, s, 0:weights.counts[s]], weights.source(turn, s)).then_inc(self.arrived[s], 16)

        for s in range(2):
            if self.primed:
                sp.sem_inc(self.arrived[s], 16)
            else:
                load(self.weights, 0, s)
        with sp.Fori(1, turns) as i:
            for s in range(2):
                sp.wait_ge(self.ready[s], i)
                load(self.weights, i, s)
        if self.following:
            for s in range(2):
                sp.wait_ge(self.ready[s], turns)
                load(self.following, 0, s)
            sp.wait_ge(self.arrived[1], 16 * (turns + 1))

    def make_high(self, act, turn, s, first=False, last=False):
        if first and self.primed and s == 0:
            act.sem_inc(self.high_ready[s], 1)
            return
        if last and (s == 1 or not self.following):
            return
        n = (self.following if last else self.weights).counts[s]
        act.wait_ge(self.arrived[s], turn * 16 + 16)
        if not first:
            act.wait_ge(self.done[s], turn * GROUPS)
        self.nc.scalar.activation(self.high[:, s, 0:n], self.raw[:, s, 0:n], ACT.Copy).then_inc(self.high_ready[s], 1)

    def make_low(self, dve, turn, s, first=False, last=False):
        if first and self.primed and s == 0:
            dve.sem_inc(self.ready[s], 1)
            return
        if last and (s == 1 or not self.following):
            return
        n = (self.following if last else self.weights).counts[s]
        dve.wait_ge(self.high_ready[s], turn + 1)
        self.nc.vector.tensor_tensor(self.low[:, s, 0:n], self.raw[:, s, 0:n], self.high[:, s, 0:n].bitcast(F32),
                                     ALU.subtract).then_inc(self.ready[s], 1)

    def product(self, out, s, source, g):
        high, low = source
        n = self.weights.counts[s]
        for k in range(n):
            self.nc.tensor.matmul(out, self.high[:, s, k], high[:, k, cols(g)], start=k == 0, stop=False)
            self.nc.tensor.matmul(out, self.high[:, s, k], low[:, k, cols(g)], start=False, stop=False)
            last = self.nc.tensor.matmul(out, self.low[:, s, k], high[:, k, cols(g)], start=False, stop=k == n - 1)
        return last.then_inc(self.done[s], 1)


def turns_but_last(engine, turns, work):
    with engine.Fori(0, turns - 1) as i:
        work(i, False)
    work(turns - 1, True)


def project_features(nc, m, name, first, targets, norm=False, decode=False):
    with ExitStack() as stack:
        sem = phase(nc, stack)
        w = SplitWeights(nc, sem, name, SplitBuffers(nc, stack, name, KC),
                         Weights(lambda i, s: m.dram["w_feature"][i * 2 + (first + s)], (KC, KC)))
        banks_free = [sem(f"{name}_banks_free{s}") for s in range(2)]
        factor = NormFactor(nc, m, sem, name, (m.bank[6], m.bank[7], m.bank[5]))
        tokens_mean, tokens_root = sem(f"{name}_tokens_mean"), sem(f"{name}_tokens_root")
        tokens_ready = sem(f"{name}_tokens_ready")
        finished = sem(f"{name}_finished")
        recurrence = DecodeRecurrence(nc, m, stack, sem) if decode else None
        block = stack.enter_context(nc.Block())
        turns = 2 * len(targets)

        @block.sync
        def _(sp):
            w.load_all(sp, turns)

        @block.tensor
        def _(pe):
            if norm:
                factor.mean(pe)
                pe.wait_ge(factor.root_ready, 1)
                for i, (start, count) in enumerate(TILES):
                    last = nc.tensor.matmul(m.bank[6][0:count, i:i + 1], m.total[:, start:start + count],
                                            m.mean_weights[:, 0:1], start=True, stop=True)
                last.then_inc(tokens_mean, 1)
                pe.wait_ge(factor.root_ready, GROUPS)
            if decode:
                recurrence.add_nothing(pe, first=True)
            with pe.Fori(0, turns) as i:
                for s in range(2):
                    pe.wait_ge(w.ready[s], i + 1)
                    for g in range(GROUPS):
                        pe.wait_ge(banks_free[s], i * GROUPS + (g + 1))
                        w.product(m.bank[3 * s + g][:, 0:G], s, m.xn, g)
                        if decode and g == 0:
                            recurrence.spread(pe, i * 2 + s, s)
                    if decode:
                        recurrence.read(pe, i * 2 + s, s)
            if decode:
                recurrence.add_nothing(pe, first=False)

        @block.scalar
        def _(act):
            if norm:
                factor.root(act)
                act.wait_ge(tokens_mean, 1)
                eps = m.vectors[:, V_EPS:V_EPS + 1]
                nc.scalar.activation(m.token_scale[:, 0:8], m.bank[6][:, 0:8], ACT.Sqrt, bias=eps)
                nc.scalar.activation(m.token_scale[0:DEC, 8:9], m.bank[6][0:DEC, 8:9], ACT.Sqrt,
                                     bias=eps[0:DEC]).then_inc(tokens_root, 1)
            for s in range(2):
                w.make_high(act, 0, s, first=True)
            if decode:
                for b in range(2):
                    recurrence.load(act, b)
            for c in range(4 * len(targets)):
                target, function = targets[c // 4]
                i, s = c // 2, c % 2
                if i + 1 < turns:
                    w.make_high(act, i + 1, s)
                if function is not None:
                    for g in range(GROUPS):
                        act.wait_ge(banks_free[s], (i + 1) * GROUPS + g + 1)
                        nc.scalar.activation(target[:, c % 4, cols(g)], target[:, c % 4, cols(g)],
                                             function).then_inc(finished, 1)
                if decode:
                    recurrence.store(act, c)
                    if 1 <= c < DEC - 1:
                        recurrence.load(act, c + 1)
            if decode:
                recurrence.finish(act)

        @block.vector
        def _(dve):
            for s in range(2):
                dve.sem_inc(banks_free[s], GROUPS)
                w.make_low(dve, 0, s, first=True)
            if norm:
                factor.invert(dve)
                dve.wait_ge(tokens_root, 1)
                nc.vector.reciprocal(m.token_scale[:, 0:8], m.token_scale[:, 0:8])
                nc.vector.reciprocal(m.token_scale[0:DEC, 8:9], m.token_scale[0:DEC, 8:9]).then_inc(tokens_ready, 1)
            if decode:
                recurrence.prepare(dve)
            for c in range(4 * len(targets)):
                target, i, s = targets[c // 4][0], c // 2, c % 2
                if decode:
                    recurrence.stage(dve, c)
                for g in range(GROUPS):
                    dve.wait_ge(w.done[s], i * GROUPS + g + 1)
                    nc.vector.tensor_tensor(target[:, c % 4, cols(g)], m.bank[3 * s + g][:, 0:G], m.scale[:, cols(g)],
                                            ALU.mult).then_inc(banks_free[s], 1)
                    if decode and g == 0:
                        recurrence.update(dve, c)
                if i + 1 < turns:
                    w.make_low(dve, i + 1, s)


def lower_bound(nc, m):
    with ExitStack() as stack:
        sem = phase(nc, stack)
        step_done = sem("lower_step")
        exp_ready = sem("lower_exp")
        block = stack.enter_context(nc.Block())
        a0, a1 = m.vectors[:, V_LB:V_LB + 4], m.vectors[:, V_LB + 4:V_LB + 8]
        lb, rest, top, shifted = m.lower[:, 0:4], m.lower[:, 4:8], m.lower[:, 8:12], m.lower[:, 12:20]

        @block.vector
        def _(dve):
            step = Chain(dve, step_done)
            step(nc.vector.tensor_tensor(top, a0, a1, ALU.max))
            step(nc.vector.tensor_tensor(shifted[:, 0:4], a0, top, ALU.subtract))
            step(nc.vector.tensor_tensor(shifted[:, 4:8], a1, top, ALU.subtract))
            dve.wait_ge(exp_ready, 1)
            step(nc.vector.tensor_tensor(top, shifted[:, 0:4], shifted[:, 4:8], ALU.add))
            step(nc.vector.reciprocal(top, top))
            step(nc.vector.tensor_tensor(lb, shifted[:, 0:4], top, ALU.mult))
            step(nc.vector.tensor_scalar(rest, lb, -1.0, 1.0, ALU.mult, ALU.add))

        @block.scalar
        def _(act):
            act.wait_ge(step_done, 3)
            nc.scalar.activation(shifted, shifted, ACT.Exp).then_inc(exp_ready, 1)


class HeadRoots:

    def __init__(self, nc, m, stack, sem):
        self.nc, self.m = nc, m
        self.squares = stack.enter_context(nc.sbuf_tensor("head_squares", [P, 2, 512], F32))
        self.summed = sem("head_summed")

    def __call__(self, act):
        nc, m = self.nc, self.m
        for i, (first, count) in enumerate(TILES):
            if i >= 2:
                act.wait_ge(self.summed, i - 1)
            for h in range(HGH):
                last = nc.scalar.activation(self.squares[0:count, i % 2, h * P:(h + 1) * P],
                                            m.v_hg[0:count, i, h * P:(h + 1) * P], ACT.Square,
                                            accum_out=m.head_roots[0:count, i, h:h + 1])
            last.then_inc(self.summed, 1)
        act.wait_ge(self.summed, len(TILES))
        for roots in (m.head_roots[:, 0:QT], m.head_roots[0:DEC, QT]):
            nc.scalar.activation(roots, roots, ACT.Sqrt, scale=1.0 / P,
                                 bias=m.vectors[0:roots.shape[0], V_EPS:V_EPS + 1])


def project_tokens(nc, m, name, groups, keys=(), stores=None):
    with ExitStack() as stack:
        sem = phase(nc, stack)
        raw = stack.enter_context(nc.sbuf_tensor(f"{name}_raw", [P, 2, 512], F32))
        high = stack.enter_context(nc.sbuf_tensor(f"{name}_high", [P, KC, 512], F32R))
        low = stack.enter_context(nc.sbuf_tensor(f"{name}_low", [P, KC, 512], F32R))
        arrived = [sem(f"{name}_arrived{s}") for s in range(2)]
        high_ready = sem(f"{name}_high_ready")
        low_ready = sem(f"{name}_low_ready")
        tile_done = sem(f"{name}_tile_done")
        tile_kept = sem(f"{name}_tile_kept")
        turned = sem(f"{name}_turned")
        keys_kept = sem(f"{name}_keys_kept")
        head_roots = HeadRoots(nc, m, stack, sem) if keys else None
        block = stack.enter_context(nc.Block())

        @block.sync
        def _(sp):
            n = 0
            for target, start, width in groups:
                for k in range(KC):
                    if n >= 2:
                        sp.wait_ge(low_ready, n - 1)
                    sp.dma_start(raw[:, n % 2, 0:width],
                                 m.dram["w_token"][:, k, start:start + width]).then_inc(arrived[n % 2], 16)
                    n += 1
                if stores is not None and target is groups[0][0]:
                    sp.dma_start(m.dram["out_win_s"][:, 0:WINDOW - 1],
                                 m.dram["window_rows"][:, 1:WINDOW]).then_inc(m.rows_stored, 16)
            if stores is not None:
                stores(sp, tile_kept)

        @block.tensor
        def _(pe):
            n = 0
            for group, (target, start, width) in enumerate(groups):
                for i, (first, count) in enumerate(TILES):
                    if n >= 6:
                        pe.wait_ge(tile_kept, n - 5)
                    out = m.bank[n % 6][0:count, 0:width]
                    tokens = slice(first, first + count)
                    for k in range(KC):
                        if i == 0:
                            pe.wait_ge(low_ready, group * KC + k + 1)
                        nc.tensor.matmul(out, m.xn[0][:, k, tokens], high[:, k, 0:width], start=k == 0, stop=False)
                        nc.tensor.matmul(out, m.xn[0][:, k, tokens], low[:, k, 0:width], start=False, stop=False)
                        last = nc.tensor.matmul(out, m.xn[1][:, k, tokens], high[:, k, 0:width],
                                                start=False, stop=k == KC - 1)
                    last.then_inc(tile_done, 1)
                    n += 1
            pe.wait_ge(tile_kept, n)
            step = 0
            for rows, _ in keys:
                for tiles in (range(0, 4), range(4, 8), range(8, 9)):
                    if step >= 2:
                        pe.wait_ge(keys_kept, step - 1)
                    for i in tiles:
                        count = TILES[i][1]
                        last = nc.tensor.transpose(m.bank[6 + step % 2][:, (i % 4) * P:(i % 4) * P + count],
                                                   rows[0:count, i], m.identity[0:count, 0:count])
                    last.then_inc(turned, 1)
                    step += 1

        @block.vector
        def _(dve):
            def make_low(group, k, width):
                n = group * KC + k
                dve.wait_ge(high_ready, n + 1)
                nc.vector.tensor_tensor(low[:, k, 0:width], raw[:, n % 2, 0:width], high[:, k, 0:width].bitcast(F32),
                                        ALU.subtract).then_inc(low_ready, 1)

            n = 0
            for group, (target, start, width) in enumerate(groups):
                for k in range(KC):
                    make_low(group, k, width)
                for i, (first, count) in enumerate(TILES):
                    dve.wait_ge(tile_done, n + 1)
                    nc.vector.tensor_scalar(target[0:count, i, 0:width], m.bank[n % 6][0:count, 0:width],
                                            m.token_scale[0:count, i:i + 1], None, ALU.mult).then_inc(tile_kept, 1)
                    n += 1

        @block.scalar
        def _(act):
            n = 0
            for group, (target, start, width) in enumerate(groups):
                if group:
                    act.wait_ge(tile_done, 9 * group)
                for k in range(KC):
                    act.wait_ge(arrived[n % 2], 16 * (n // 2 + 1))
                    nc.scalar.activation(high[:, k, 0:width], raw[:, n % 2, 0:width], ACT.Copy).then_inc(high_ready, 1)
                    n += 1
                if keys and group == 0:
                    head_roots(act)
            step = 0
            for _, keys_t in keys:
                for first, count in ((0, 512), (512, 512), (1024, DEC)):
                    act.wait_ge(turned, step + 1)
                    nc.scalar.activation(keys_t[:, first:first + count], m.bank[6 + step % 2][:, 0:count],
                                         ACT.Copy).then_inc(keys_kept, 1)
                    step += 1


def store_rows(m):
    def stores(sp, kept):
        def store(target, source):
            sp.dma_start(target, source).then_inc(m.rows_stored, 16)

        sp.wait_ge(kept, 9)
        store(m.dram["out_cmp_p"].rearrange("(i p) f -> p i f", p=P), m.kv_a[:, 0:8, 0:256])
        store(m.dram["out_slc_p"].rearrange("(i p) f -> p i f", p=P), m.kv_a[:, 0:8, 256:512])
        store(m.dram["out_cmp_s"], m.kv_a[0:DEC, 8, 0:256])
        store(m.dram["out_slc_s"], m.kv_a[0:DEC, 8, 256:512])
        sp.wait_ge(kept, 18)
        store(m.dram["out_win_p"].rearrange("(i p) f -> p i f", p=P), m.kv_b[:, 4:8, 0:256])
        store(m.dram["out_win_s"][:, WINDOW - 1], m.kv_b[0:DEC, 8, 0:256])
        store(m.dram["gate_rows"].rearrange("b h c -> b (h c)"), m.kv_b[0:DEC, 8, 256:280])

    return stores


def hgrn_prompt(nc, m):
    with ExitStack() as stack:
        sem = phase(nc, stack)

        def sb(name, shape):
            return stack.enter_context(nc.sbuf_tensor(name, shape, F32))

        W = HGH * P
        reset = sb("chunk_reset", [P, W])
        logf, cum, diff = sb("log_f", [P, W]), sb("cum_log_f", [P, W]), sb("cum_to_last", [P, W])
        grow, shrink = sb("exp_cum", [P, W]), sb("exp_minus_cum", [P, W])
        decay = sb("chunk_decay", [P, 2, HGH, 4])
        key = sb("hgrn_key", [P, W])
        q_dec, k_inv, k_last = sb("q_dec", [P, 2, HGH, P]), sb("k_inv", [P, HGH, P]), sb("k_last", [P, HGH, P])
        k_rows, values = sb("k_last_rows", [P, 2, HGH, P]), sb("hgrn_values", [P, 2, HGH, P])
        weights = sb("intra_weights", [P, 2, HGH, P])
        state = sb("hgrn_state", [P, 2, HGH, P])
        prepared = sem("hgrn_reset_ready")
        forget_done = sem("forget_done")
        log_ready = sem("log_f_ready")
        cum_ready = sem("cum_ready")
        diff_ready = sem("diff_ready")
        exps_ready = sem("exps_ready")
        last_ready = sem("exp_last_ready")
        factors_ready = sem("factors_ready")
        k_last_ready = sem("k_last_ready")
        values_ready = sem("values_ready")
        scores_done = sem("intra_scores_done")
        rows_turned = sem("k_rows_turned")
        rows_kept = sem("k_rows_kept")
        weights_ready = sem("intra_weights_ready")
        update_done = sem("state_update_done")
        state_ready = sem("state_ready")
        out_done = sem("hgrn_out_done")
        out_kept = sem("hgrn_out_kept")
        stored = sem("hgrn_state_stored")
        block = stack.enter_context(nc.Block())
        bank_scores, bank_rows, bank_out, bank_update = m.bank[0], m.bank[1], (m.bank[2], m.bank[5]), (m.bank[3], m.bank[4])

        def heads(ap):
            return ap.rearrange("p (h t) -> p h t", h=HGH)

        def window(ap, n):
            return ap[:, :, bass.ds(n * P, P)]

        def over_tiles(engine, work):
            with engine.Fori(0, QT // 2 - 1) as i:
                work(i * 2, 0, 2)
                work(i * 2 + 1, 1, 2)
            work(QT - 2, 0, 1)
            work(QT - 1, 1, 0)

        @block.scalar
        def _(act):
            act.sem_inc(out_kept, 2)
            act.wait_ge(forget_done, HGH)

            def log(n):
                nc.scalar.activation(heads(logf[:]), window(m.forget, n), ACT.Ln).then_inc(log_ready, 1)

            def factors(n, q, more):
                act.wait_ge(cum_ready, n + 1)
                nc.scalar.activation(grow[:], cum[:], ACT.Exp)
                nc.scalar.activation(shrink[:], cum[:], ACT.Exp, scale=-1.0).then_inc(exps_ready, 1)
                act.wait_ge(diff_ready, n + 1)
                nc.scalar.activation(decay[:, q], heads(cum[:]).rearrange("p h (c s) -> p h c s", s=BLOCK32)[:, :, :, BLOCK32 - 1],
                                     ACT.Exp)
                nc.scalar.activation(logf[:], diff[:], ACT.Exp).then_inc(last_ready, 1)
                act.wait_ge(rows_turned, n + 2)
                nc.scalar.activation(k_rows[:, q].rearrange("p h t -> p (h t)"), bank_rows[:], ACT.Copy).then_inc(rows_kept, 1)
                if more:
                    act.wait_ge(k_last_ready, n + 1)
                    log(n + 1)

            def work(n, q, more):
                if more:
                    factors(n + 1, 1 - q, more > 1)
                act.wait_ge(out_done, n + 3)
                nc.scalar.activation(m.v_hg[:, bass.ds(n, 1), :].rearrange("p a f -> p (a f)"), bank_out[q][:],
                                     ACT.Copy).then_inc(out_kept, 1)

            log(0)
            factors(0, 0, True)
            over_tiles(act, work)

        @block.gpsimd
        def _(pool):
            def work(n, q, more):
                pool.wait_ge(out_done, n + 1)
                nc.gpsimd.tensor_copy(values[:, q].rearrange("p h t -> p (h t)"),
                                      m.v_hg[:, bass.ds(n, 1), :].rearrange("p a f -> p (a f)")).then_inc(values_ready, 1)

            over_tiles(pool, work)

        @block.vector
        def _(dve):
            nc.vector.memset(state[:, 0], 0.0).then_inc(state_ready, 1)
            nc.vector.memset(reset[:], 1.0).then_inc(prepared, 1)
            dve.wait_ge(prepared, 1)
            nc.vector.memset(reset[:].rearrange("p (c s) -> p c s", s=BLOCK32)[:, :, 0], 0.0).then_inc(prepared, 1)
            for h in range(HGH):
                nc.vector.tensor_scalar(m.forget[:, h], m.forget[:, h], m.lower[:, 4 + h:5 + h],
                                        m.lower[:, h:h + 1], ALU.mult, ALU.add).then_inc(forget_done, 1)
            dve.wait_ge(forget_done, HGH)
            dve.wait_ge(prepared, 2)
            nc.vector.tensor_copy(m.decode_forget[:], m.forget[:, :, SEQ:T])
            nc.vector.tensor_copy(m.decode_q[:], m.q_b[:, :, SEQ:T])

            def cumulate(n):
                dve.wait_ge(log_ready, n + 1)
                nc.vector.tensor_scalar(heads(key[:]), window(m.forget, n), -1.0, 1.0, ALU.mult, ALU.add)
                nc.vector.tensor_tensor_scan(cum[:], reset[:], logf[:], 0.0, ALU.mult, ALU.add).then_inc(cum_ready, 1)
                dve.wait_ge(cum_ready, n + 1)
                c4 = cum[:].rearrange("p (c s) -> p c s", s=BLOCK32)
                nc.vector.tensor_tensor(diff[:].rearrange("p (c s) -> p c s", s=BLOCK32),
                                        c4[:, :, BLOCK32 - 1:BLOCK32].to_broadcast([P, W // BLOCK32, BLOCK32]), c4,
                                        ALU.subtract).then_inc(diff_ready, 1)

            def multiply(n, q):
                dve.wait_ge(exps_ready, n + 1)
                dve.wait_ge(out_done, n + 1)
                nc.vector.tensor_tensor(q_dec[:, q], window(m.q_b, n), heads(grow[:]), ALU.mult)
                nc.vector.tensor_tensor(k_inv[:], heads(key[:]), heads(shrink[:]), ALU.mult).then_inc(factors_ready, 1)
                dve.wait_ge(last_ready, n + 1)
                dve.wait_ge(rows_turned, n + 1)
                nc.vector.tensor_tensor(k_last[:], heads(key[:]), heads(logf[:]), ALU.mult).then_inc(k_last_ready, 1)

            def mask(n, q):
                dve.wait_ge(scores_done, n + 1)
                nc.vector.tensor_tensor(weights[:, q], bank_scores[:].rearrange("p (h t) -> p h t", h=HGH),
                                        m.intra_mask[:].rearrange("p (a t) -> p a t", a=1).to_broadcast([P, HGH, P]),
                                        ALU.mult).then_inc(weights_ready, 1)

            def step(n, q, j):
                dve.wait_ge(update_done, n * 4 + (j + 1))
                dve.wait_ge(state_ready, n * 4 + (j + 1))
                for h in range(HGH):
                    last = nc.vector.scalar_tensor_tensor(
                        out=state[:, (j + 1) % 2, h], in0=state[:, j % 2, h], scalar=decay[:, q, h, j:j + 1],
                        in1=bank_update[j % 2][:, h * P:(h + 1) * P], op0=ALU.mult, op1=ALU.add)
                last.then_inc(state_ready, 1)

            def work(n, q, more):
                if more:
                    cumulate(n + 1)
                step(n, q, 0)
                if more:
                    multiply(n + 1, 1 - q)
                step(n, q, 1)
                step(n, q, 2)
                if more:
                    mask(n + 1, 1 - q)
                step(n, q, 3)

            cumulate(0)
            multiply(0, 0)
            mask(0, 0)
            over_tiles(dve, work)

        @block.tensor
        def _(pe):
            pe.sem_inc(out_done, 2)
            pe.sem_inc(rows_turned, 1)

            def scores(n, q):
                pe.wait_ge(factors_ready, n + 1)
                for h in range(HGH):
                    last = nc.tensor.matmul(bank_scores[:, h * P:(h + 1) * P], k_inv[:, h], q_dec[:, q, h],
                                            start=True, stop=True)
                last.then_inc(scores_done, 1)

            def turn(n):
                pe.wait_ge(k_last_ready, n + 1)
                for h in range(HGH):
                    last = nc.tensor.transpose(bank_rows[:, h * P:(h + 1) * P], k_last[:, h], m.identity[:])
                last.then_inc(rows_turned, 1)

            def inside(n, q):
                pe.wait_ge(weights_ready, n + 1)
                pe.wait_ge(values_ready, n + 1)
                pe.wait_ge(out_kept, n + 1)
                for h in range(HGH):
                    nc.tensor.matmul(bank_out[q][:, h * P:(h + 1) * P], weights[:, q, h], values[:, q, h],
                                     start=h == 0, stop=False, skip_group_check=True)
                pe.wait_ge(rows_kept, n + 1)

            def step(n, q, j):
                rows = slice(j * BLOCK32, (j + 1) * BLOCK32)
                pe.wait_ge(state_ready, n * 4 + max(j, 1))
                for h in range(HGH):
                    last = nc.tensor.matmul(bank_update[j % 2][:, h * P:(h + 1) * P], k_rows[rows, q, h],
                                            values[rows, q, h], start=True, stop=True)
                last.then_inc(update_done, 1)
                pe.wait_ge(state_ready, n * 4 + (j + 1))
                for h in range(HGH):
                    last = nc.tensor.matmul(bank_out[q][rows, h * P:(h + 1) * P], q_dec[:, q, h, rows],
                                            state[:, j % 2, h], start=False, stop=h == HGH - 1,
                                            skip_group_check=True)
                return last

            def work(n, q, more):
                inside(n, q)
                step(n, q, 0)
                step(n, q, 1)
                if more:
                    scores(n + 1, 1 - q)
                step(n, q, 2)
                if more:
                    turn(n + 1)
                step(n, q, 3).then_inc(out_done, 1)

            scores(0, 0)
            turn(0)
            over_tiles(pe, work)

        @block.sync
        def _(sp):
            sp.wait_ge(state_ready, QT * 4 + 1)
            sp.dma_start(m.dram["out_hgrn_p"].rearrange("h k v -> k h v"), state[:, 0]).then_inc(stored, 16)
            sp.wait_ge(stored, 16)


class DecodeRecurrence:

    def __init__(self, nc, m, stack, sem):
        def sb(name, shape):
            return stack.enter_context(nc.sbuf_tensor(name, shape, F32))

        self.nc, self.m = nc, m
        self.state = sb("decode_state", [P, 2, HGH, P])
        self.outer = sb("decode_outer", [P, HGH, P])
        self.key = sb("decode_key", [P, HGH, DEC])
        self.queries = sb("decode_queries", [P, HGH, DEC, DEC])
        self.query, self.pick = sb("decode_query", [P, 2, HGH, DEC]), sb("decode_pick", [DEC, 2, P])
        self.zeros = sb("decode_zeros", [P, DEC])
        self.loaded = [sem(f"decode_state_loaded{s}") for s in range(2)]
        self.stored = [sem(f"decode_state_stored{s}") for s in range(2)]
        self.prepared = sem("decode_prepared")
        self.staged = sem("decode_staged")
        self.values_spread = sem("decode_values_spread")
        self.outer_ready = sem("decode_outer_ready")
        self.updated = sem("decode_state_updated")
        self.state_read = sem("decode_state_read")
        self.out_done = sem("decode_recurrence_out_done")
        self.kept = sem("decode_out_kept")
        self.bank_values, self.bank_out = m.bank[6], m.bank[7]

    def load(self, act, b):
        if b >= 2:
            act.wait_ge(self.stored[b % 2], 16 * (b // 2))
            act.wait_ge(self.state_read, b - 1)
        act.dma_start(self.state[:, b % 2],
                      self.m.dram["state_hgrn"][b].rearrange("h k v -> k h v")).then_inc(self.loaded[b % 2], 16)

    def store(self, act, b):
        act.wait_ge(self.updated, b + 1)
        act.dma_start(self.m.dram["out_hgrn_s"][b].rearrange("h k v -> k h v"),
                      self.state[:, b % 2]).then_inc(self.stored[b % 2], 16)

    def finish(self, act):
        for s in range(2):
            act.wait_ge(self.stored[s], 16 * (DEC // 2))
        act.wait_ge(self.out_done, 1)
        self.nc.scalar.activation(self.m.v_hg[0:DEC, 8], self.bank_out[0:DEC], ACT.Copy).then_inc(self.kept, 1)

    def prepare(self, dve):
        nc, m = self.nc, self.m
        nc.vector.memset(self.zeros[:], 0.0).then_inc(self.prepared, 1)
        nc.vector.memset(self.queries[:], 0.0).then_inc(self.prepared, 1)
        nc.vector.tensor_scalar(self.key[:], m.decode_forget[:], -1.0, 1.0, ALU.mult, ALU.add).then_inc(self.prepared, 1)
        dve.wait_ge(self.prepared, 3)
        nc.vector.tensor_copy(self.queries[:].rearrange("p h b c -> p h (b c)")[:, :, 0:DEC * DEC:DEC + 1],
                              m.decode_q[:]).then_inc(self.prepared, 1)
        dve.wait_ge(self.prepared, 4)

    def stage(self, dve, b):
        if b >= 2:
            dve.wait_ge(self.state_read, b - 1)
        self.nc.vector.tensor_copy(self.pick[:, b % 2], self.m.row_pick[:, b])
        self.nc.vector.tensor_copy(self.query[:, b % 2], self.queries[:, :, b]).then_inc(self.staged, 1)

    def update(self, dve, b):
        nc, m = self.nc, self.m
        dve.wait_ge(self.values_spread, b + 1)
        if b:
            dve.wait_ge(self.updated, b)
        for h in range(HGH):
            last = nc.vector.tensor_scalar(self.outer[:, h], self.bank_values[:, h * P:(h + 1) * P],
                                           self.key[:, h, b:b + 1], None, ALU.mult)
        last.then_inc(self.outer_ready, 1)
        dve.wait_ge(self.outer_ready, b + 1)
        dve.wait_ge(self.loaded[b % 2], 16 * (b // 2 + 1))
        for h in range(HGH):
            state = self.state[:, b % 2, h]
            last = nc.vector.scalar_tensor_tensor(out=state, in0=state, scalar=m.decode_forget[:, h, b:b + 1],
                                                  in1=self.outer[:, h], op0=ALU.mult, op1=ALU.add)
        last.then_inc(self.updated, 1)

    def add_nothing(self, pe, first):
        pe.wait_ge(self.prepared, 1)
        for h in range(HGH):
            last = self.nc.tensor.matmul(self.bank_out[0:DEC, h * P:(h + 1) * P], self.zeros[:], self.m.identity[:],
                                         start=first and h == 0, stop=not first, skip_group_check=True)
        if not first:
            last.then_inc(self.out_done, 1)

    def spread(self, pe, b, s):
        pe.wait_ge(self.staged, b + 1)
        self.nc.tensor.matmul(self.bank_values[:], self.pick[:, s], self.m.v_hg[0:DEC, 8],
                              start=True, stop=True).then_inc(self.values_spread, 1)

    def read(self, pe, b, s):
        pe.wait_ge(self.updated, b + 1)
        for h in range(HGH):
            last = self.nc.tensor.matmul(self.bank_out[0:DEC, h * P:(h + 1) * P], self.query[:, s, h],
                                         self.state[:, s, h], start=False, stop=False, skip_group_check=True)
        last.then_inc(self.state_read, 1)


HALF = 16
PAIRS = HALF // 2
HID = 256


def compress(nc, m, prompt):
    with ExitStack() as stack:
        sem = phase(nc, stack)
        n_half = SEQ // HALF if prompt else PAGES * PAGE // HALF
        per_page = n_half if prompt else PAGE // HALF
        pages = n_half // per_page
        tag = "prompt" if prompt else "cache"
        width = KVH * n_half

        def sb(name, shape):
            return stack.enter_context(nc.sbuf_tensor(f"{tag}_{name}", shape, F32))

        if prompt:
            rows = m.v_hg[:].rearrange("p i f -> p (i f)")[:, 0:PAIRS * 2 * width].rearrange(
                "p (s c k n) -> p s c k n", s=PAIRS, c=2, k=KVH)
        else:
            rows = m.cache_rows
        high = sb("high_half", [P, KVH, n_half + 1])
        before = sb("hidden_before", [P, 2, KVH, n_half])
        hidden = sb("hidden", [P, 2, 2, KVH, n_half])
        row_halves, page_in = m.row_halves, m.page_in
        turned = sem("prompt_halves_turned")
        rows_kept = sem("prompt_rows_kept")
        product_done = sem("half_products_done")
        high_kept = sem("high_half_kept")
        sum_ready = sem("hidden_sum_ready")
        hidden_ready = sem("hidden_ready")
        blocks_done = sem("kv_blocks_done")
        blocks_kept = sem("kv_blocks_kept")
        zeroed = sem("high_half_zeroed")
        block = stack.enter_context(nc.Block())
        w1 = m.w1[:]
        UNITS = 4

        def over_sequences(engine, work):
            if prompt:
                work(0, 0)
            else:
                with engine.Fori(0, DEC // 2) as i:
                    for s in range(2):
                        work(i * 2 + s, s)

        @block.sync
        def _(sp):
            def load_page(b, p, s, freed=None):
                page = sp.value_load(m.table[0:1, bass.ds(b * PAGES + p, 1)], min_val=0, max_val=POOL - 1)
                if freed is not None:
                    sp.wait_ge(product_done, freed)
                sp.dma_start(m.cache_rows[:, s, bass.ds(p, 1)].rearrange("p a s c k n -> p a (s c k n)"),
                             m.dram["cache_cmp"][bass.ds(page, 1)].rearrange("a p f -> p a f")).then_inc(page_in[s], 16)

            first = 0 if prompt else 1
            with sp.Fori(0, PAGES) as p:
                load_page(first, p, first)
            if not prompt:
                with sp.Fori(1, DEC // 2) as i:
                    for s in range(2):
                        load_page(i * 2 + s, 0, s, freed=(i * 2 + (s - 1)) * UNITS)
                        with sp.Fori(0, (PAGES - 1) // 3) as p:
                            for k in range(1, 4):
                                load_page(i * 2 + s, p * 3 + k, s)

        @block.tensor
        def _(pe):
            if prompt:
                pe.wait_ge(m.weights_in, 2 * 16)
                for l in range(2):
                    pe.wait_ge(m.w1_in[l], 16)
                pe.wait_ge(m.halves_in, 4 * 16)
                for c in range(2):
                    for k in range(KVH):
                        for s in range(PAIRS):
                            last = nc.tensor.transpose(m.bank[2 * c + k][:, s * n_half:(s + 1) * n_half],
                                                       row_halves[:, 2 * c + k, 2 * s:2 * s + 2].rearrange("n s d -> n (s d)"),
                                                       m.identity[0:n_half, 0:n_half])
                        last.then_inc(turned, 1)
                pe.wait_ge(rows_kept, 4)

            def unit(n, slot, u):
                c, f = u // 2, u % 2
                if u == 0 and not prompt:
                    pe.wait_ge(page_in[slot], (n - slot + 2) * (8 * PAGES))
                for l in range(2):
                    for s in range(PAIRS):
                        if prompt:
                            out = m.bank[u][:, l * 256:l * 256 + width]
                            moving = rows[:, s, c]
                        else:
                            out = m.bank[u][:, l * 256:l * 256 + width].rearrange("p (a x) -> p a x", a=pages)
                            moving = rows[:, slot, :, s, c].rearrange("p a k n -> p a (k n)")
                        last = nc.tensor.matmul(out, w1[:, c, l, s, f * P:(f + 1) * P], moving,
                                                start=s == 0, stop=s == PAIRS - 1)
                last.then_inc(product_done, 1)

            def blocks(n, c):
                pe.wait_ge(hidden_ready, n * UNITS + 2 * (c + 1))
                pe.wait_ge(blocks_kept, n * 2 + (c + 1))
                for k in range(KVH):
                    for f in range(2):
                        if c == 0:
                            last = nc.tensor.matmul(m.bank[4][:, 0:n_half], m.w2_k[:, f, k], hidden[:, 0, f, k],
                                                    start=k == 0 and f == 0, stop=k == 1 and f == 1)
                        else:
                            last = nc.tensor.matmul(m.bank[5][0:n_half, k * HEAD:(k + 1) * HEAD],
                                                    hidden[:, 1, f, k], m.w2_v[:, f], start=f == 0, stop=f == 1)
                last.then_inc(blocks_done, 1)

            def rest(n, slot, following):
                for u in range(1, UNITS):
                    unit(n, slot, u)
                blocks(n, 0)
                if following:
                    unit(n + 1, 1 - slot, 0)
                blocks(n, 1)

            unit(0, 0, 0)
            if prompt:
                rest(0, 0, False)
            else:
                with pe.Fori(0, DEC // 2 - 1) as i:
                    rest(i * 2, 0, True)
                    rest(i * 2 + 1, 1, True)
                rest(DEC - 2, 0, True)
                rest(DEC - 1, 1, False)

        @block.vector
        def _(dve):
            nc.vector.memset(high[:], 0.0).then_inc(zeroed, 1)
            if prompt:
                nc.vector.memset(m.kc_prompt[:], 0.0).then_inc(zeroed, 1)
                nc.vector.memset(m.vc_prompt[:], 0.0).then_inc(zeroed, 1)
            if prompt:
                for c in range(2):
                    for k in range(KVH):
                        dve.wait_ge(turned, 2 * c + k + 1)
                        nc.vector.tensor_copy(rows[:, :, c, k],
                                              m.bank[2 * c + k][:].rearrange("p (s n) -> p s n", s=PAIRS)).then_inc(rows_kept, 1)

            def work(n, slot):
                for u in range(UNITS):
                    dve.wait_ge(high_kept, n * UNITS + u + 1)
                    for k in range(KVH):
                        low = m.bank[u][:, 0:width].rearrange("p (a k n) -> p a k n", a=pages, k=KVH)[:, :, k]
                        last = nc.vector.tensor_tensor(
                            before[:, u % 2, k].rearrange("p (a n) -> p a n", a=pages), low,
                            high[:, k, 1:n_half + 1].rearrange("p (a n) -> p a n", a=pages), ALU.add)
                    last.then_inc(sum_ready, 1)

            over_sequences(dve, work)

        @block.scalar
        def _(act):
            act.sem_inc(blocks_kept, 2)
            act.wait_ge(zeroed, 3 if prompt else 1)

            def work(n, slot):
                for u in range(UNITS):
                    act.wait_ge(product_done, n * UNITS + u + 1)
                    for k in range(KVH):
                        part = m.bank[u][:, 256:256 + width].rearrange("p (a k n) -> p a k n", a=pages, k=KVH)[:, :, k]
                        last = nc.scalar.activation(high[:, k, 0:n_half].rearrange("p (a n) -> p a n", a=pages), part,
                                                    ACT.Copy)
                    last.then_inc(high_kept, 1)
                    act.wait_ge(sum_ready, n * UNITS + u + 1)
                    nc.scalar.activation(hidden[:, u // 2, u % 2], before[:, u % 2], ACT.Silu,
                                         bias=m.hidden_bias[:, u:u + 1]).then_inc(hidden_ready, 1)
                act.wait_ge(blocks_done, n * 2 + 1)
                target = m.kc_prompt[:, 0:n_half] if prompt else m.kc_cache[:, bass.ds(n, 1)].rearrange("p a n -> p (a n)")
                nc.scalar.activation(target, m.bank[4][:, 0:n_half], ACT.Copy).then_inc(blocks_kept, 1)
                act.wait_ge(blocks_done, n * 2 + 2)
                target = m.vc_prompt[0:n_half] if prompt else m.vc_cache[:, bass.ds(n, 1)].rearrange("p a n -> p (a n)")
                nc.scalar.activation(target, m.bank[5][0:n_half, 0:P], ACT.Copy).then_inc(blocks_kept, 1)

            over_sequences(act, work)


def prepare_attention(nc, m):
    with ExitStack() as stack:
        sem = phase(nc, stack)
        done = sem("gates_done")
        masks_in = sem("attention_masks_in")
        block = stack.enter_context(nc.Block())

        @block.sync
        def _(sp):
            for target, source in zip(m.masks, ("causal_add", "window_add", "cmp_add", "cmp_keep")):
                sp.dma_start(target[:], m.dram[source]).then_inc(masks_in, 16)
            sp.wait_ge(masks_in, 16 * len(m.masks))

        @block.scalar
        def _(act):
            nc.scalar.activation(m.gates[:], m.kv_b[:, 0:QT, 256:280], ACT.Sigmoid).then_inc(done, 1)


def prompt_items():
    items = []
    for k in range(KVH):
        for i in range(QT):
            items.append((k, i, "slc", 0, i + 1))
            o = QT - 1 - i
            first = max(0, o - WINDOW // P)
            items.append((k, o, "near", first, o + 1 - first))
    return items


def load_pages(sp, m, cache, b, slot, arrived):
    with sp.Fori(0, PAGES // 2) as p:
        for h in range(2):
            page = sp.value_load(m.table[0:1, bass.ds(2 * p + (b * PAGES + h), 1)], min_val=0, max_val=POOL - 1)
            sp.dma_start(slot[:, bass.ds(p, 1), h * P:(h + 1) * P].rearrange("p a f -> p (a f)"),
                         cache[bass.ds(page, 1)].rearrange("a p f -> p (a f)")).then_inc(arrived, 16)


def prompt_attention(nc, m, part, cache):
    with ExitStack() as stack:
        make = phase(nc, stack)

        def sem(name):
            return make(f"{name}{part}")

        def sb(name, shape):
            return stack.enter_context(nc.sbuf_tensor(f"{name}{part}", shape, F32))

        def over(name, shape):
            return work(f"{name}{part}", shape)

        items = prompt_items()
        N = len(items)
        work = m.over_work()
        TURNS = GQA // 2
        query = over("query_pair", [P, KVH, SEQ])
        probs = over("probs", [P, 2, SEQ])
        probs_t = over("probs_turned", [P, 2, QT, P])
        out = over("out_pair", [P, QT, KVH, HEAD])
        gate = sb("gate_pair", [P, QT, KVH, 3])
        top, bias, total = sb("score_max", [P, 2, 2]), sb("exp_bias", [P, 2, 2]), sb("exp_total", [P, 4, 2])
        coefficient = sb("branch_coefficient", [P, 4, 2])
        causal, beyond, cmp_add, cmp_keep = m.masks
        pages_in = sem("pages_in")
        cleared = sem("queries_cleared")
        staged = sem("pair_staged")
        scores_done = sem("scores_done")
        masked = sem("scores_masked")
        max_ready = sem("max_ready")
        bias_ready = sem("exp_bias_ready")
        probs_ready = sem("probs_ready")
        probs_masked = sem("probs_masked")
        turned = sem("probs_turned_done")
        kept_act = sem("turned_kept_by_scalar")
        kept_dve = sem("turned_kept_by_vector")
        product_done = sem("value_product_done")
        inverse_ready = sem("inverse_total_ready")
        coefficient_ready = sem("coefficient_ready")
        added = sem("window_branch_added")
        combined = sem("branch_combined")
        written = sem("pair_written")
        block = stack.enter_context(nc.Block())

        def is_near(n):
            return items[n][2] == "near"

        def key_tiles(n):
            return items[n][4] + is_near(n)

        def nears(n):
            return sum(is_near(x) for x in range(n))

        NEARS = nears(N)

        @block.sync
        def _(sp):
            for b in range(DEC - 1):
                load_pages(sp, m, cache, b, m.slots[b], pages_in)
            sp.wait_ge(pages_in, 16 * PAGES * (DEC - 1))

        @block.tensor
        def _(pe):
            def scores(j, n):
                k, i, kind, first, tiles = items[n]
                if n >= 2:
                    pe.wait_ge(probs_ready, j * N + (n - 1))
                lhs = query[:, k, i * P:(i + 1) * P]
                pair = m.pair[n % 2]
                keys = m.k_win if is_near(n) else m.k_slc
                for a in range(0, tiles * P, 512):
                    b = min(a + 512, tiles * P)
                    last = nc.tensor.matmul(pair[:, a:b], lhs, keys[:, first * P + a:first * P + b],
                                            start=True, stop=True)
                if is_near(n):
                    last = nc.tensor.matmul(pair[:, tiles * P:(tiles + 1) * P], lhs, m.kc_prompt[:],
                                            start=True, stop=True)
                last.then_inc(scores_done, 1)

            def turn(j, n):
                if is_near(n):
                    pe.wait_ge(probs_masked, j * NEARS + (nears(n) + 1))
                pe.wait_ge(probs_ready, j * N + (n + 1))
                if n >= 1:
                    pe.wait_ge(kept_act, j * N + n)
                    pe.wait_ge(kept_dve, j * N + n)
                for t in range(key_tiles(n)):
                    last = nc.tensor.transpose(m.turn_bank[t // 4][:, (t % 4) * P:(t % 4) * P + P],
                                               probs[:, n % 2, t * P:(t + 1) * P], m.identity[:])
                last.then_inc(turned, 1)

            def product(j, n):
                k, i, kind, first, tiles = items[n]
                pe.wait_ge(kept_act, j * N + (n + 1))
                pe.wait_ge(kept_dve, j * N + (n + 1))
                if n >= 2:
                    pe.wait_ge(combined, j * N + (n - 1))
                o = m.bank[6 + n % 2]
                v, at = (m.kv_b, 128) if is_near(n) else (m.kv_a, 384)
                for t in range(tiles):
                    last = nc.tensor.matmul(o[:, 0:P], probs_t[:, n % 2, t], v[:, first + t, at:at + P],
                                            start=t == 0, stop=t == tiles - 1)
                if is_near(n):
                    last = nc.tensor.matmul(o[:, P:2 * P], probs_t[:, n % 2, tiles], m.vc_prompt[:],
                                            start=True, stop=True)
                last.then_inc(product_done, 1)

            with pe.Fori(0, TURNS) as j:
                pe.wait_ge(staged, j * 3 + 3)
                scores(j, 0)
                for n in range(N + 1):
                    if n + 1 < N:
                        scores(j, n + 1)
                    if n >= 1:
                        product(j, n - 1)
                    if n < N:
                        turn(j, n)

        def keep_turned(copy, n, b):
            t0, t1 = 4 * b, min(key_tiles(n), 4 * b + 4)
            if t0 < t1:
                return copy(probs_t[:, n % 2, t0:t1],
                            m.turn_bank[b][:, 0:(t1 - t0) * P].rearrange("p (t q) -> p t q", q=P))
            return None

        @block.scalar
        def _(act):
            def copy(to, source):
                return nc.scalar.activation(to, source, ACT.Copy)

            with act.Fori(0, TURNS) as j:
                for n in range(N + 1):
                    if n < N:
                        act.wait_ge(bias_ready, j * N + (n + 1))
                        if n >= 2:
                            act.wait_ge(turned, j * N + (n - 1))
                        w = items[n][4] * P
                        if is_near(n):
                            nc.scalar.activation(probs[:, n % 2, w:w + P], m.pair[n % 2][:, w:w + P], ACT.Exp,
                                                 scale=SCALE, bias=bias[:, n % 2, 1:2],
                                                 accum_out=total[:, n % 4, 1:2])
                        nc.scalar.activation(probs[:, n % 2, 0:w], m.pair[n % 2][:, 0:w], ACT.Exp, scale=SCALE,
                                             bias=bias[:, n % 2, 0:1],
                                             accum_out=total[:, n % 4, 0:1]).then_inc(probs_ready, 1)
                    if n >= 1:
                        act.wait_ge(turned, j * N + n)
                        if n >= 3:
                            act.wait_ge(product_done, j * N + (n - 2))
                        last = keep_turned(copy, n - 1, 1)
                        if last is not None:
                            last.then_inc(kept_act, 1)
                        else:
                            act.sem_inc(kept_act, 1)

        @block.gpsimd
        def _(pool):
            def mask_blocks(j, n):
                w, i = items[n][4] * P, items[n][1]
                pool.wait_ge(probs_ready, j * N + (n + 1))
                nc.gpsimd.tensor_tensor(probs[:, n % 2, w:w + P], probs[:, n % 2, w:w + P],
                                        cmp_keep[:, 56 - 8 * i:56 - 8 * i + P], ALU.mult).then_inc(probs_masked, 1)

            with pool.Fori(0, TURNS) as j:
                for n in range(N):
                    if is_near(n):
                        mask_blocks(j, n)

        @block.vector
        def _(dve):
            nc.vector.memset(query[:], 0.0).then_inc(cleared, 1)
            dve.wait_ge(cleared, 1)

            def mask_steps(n):
                return 1 if not is_near(n) else 3 if items[n][4] == 5 else 2

            MASKS = sum(mask_steps(n) for n in range(N))

            def maximum(j, n):
                k, i, kind, first, tiles = items[n]
                dve.wait_ge(scores_done, j * N + (n + 1))
                pair, w = m.pair[n % 2], tiles * P

                def add(a, mask):
                    nc.vector.tensor_tensor(pair[:, a:a + P], pair[:, a:a + P], mask, ALU.add).then_inc(masked, 1)

                if is_near(n):
                    add(w, cmp_add[:, 56 - 8 * i:56 - 8 * i + P])
                    if tiles == 5:
                        add(0, beyond[:])
                add(w - P, causal[:])
                dve.wait_ge(masked, j * MASKS + sum(mask_steps(x) for x in range(n + 1)))
                if is_near(n):
                    nc.vector.tensor_reduce(top[:, n % 2, 1:2], pair[:, w:w + P], AX.X, ALU.max)
                nc.vector.tensor_reduce(top[:, n % 2, 0:1], pair[:, 0:w], AX.X, ALU.max).then_inc(max_ready, 1)
                dve.wait_ge(max_ready, j * N + (n + 1))
                if n >= 2:
                    dve.wait_ge(probs_ready, j * N + (n - 1))
                c = 1 + is_near(n)
                nc.vector.tensor_scalar(bias[:, n % 2, 0:c], top[:, n % 2, 0:c], -SCALE, None,
                                        ALU.mult).then_inc(bias_ready, 1)

            def keep(j, n):
                dve.wait_ge(turned, j * N + (n + 1))
                if n >= 2:
                    dve.wait_ge(product_done, j * N + (n - 1))
                keep_turned(nc.vector.tensor_copy, n, 0).then_inc(kept_dve, 1)

            def combine(j, n, seen):
                k, i, kind, first, tiles = items[n]
                parts = ((1, 0), (2, 1)) if is_near(n) else ((0, 0),)
                c = len(parts)
                r = parts[0][0]
                nc.vector.reciprocal(coefficient[:, n % 4, 0:c], total[:, n % 4, 0:c]).then_inc(inverse_ready, 1)
                dve.wait_ge(inverse_ready, j * N + (n + 1))
                nc.vector.tensor_tensor(coefficient[:, n % 4, 0:c], coefficient[:, n % 4, 0:c], gate[:, i, k, r:r + c],
                                        ALU.mult).then_inc(coefficient_ready, 1)
                dve.wait_ge(coefficient_ready, j * N + (n + 1))
                dve.wait_ge(product_done, j * N + (n + 1))
                for x, (_, part) in enumerate(parts):
                    o = m.bank[6 + n % 2][:, part * P + k * HEAD:part * P + (k + 1) * HEAD]
                    scalar = coefficient[:, n % 4, part:part + 1]
                    if (k, i) in seen:
                        if x:
                            dve.wait_ge(added, j * NEARS + (nears(n) + 1))
                        elif n:
                            dve.wait_ge(combined, j * N + n)
                        last = nc.vector.scalar_tensor_tensor(out=out[:, i, k], in0=o, scalar=scalar, in1=out[:, i, k],
                                                              op0=ALU.mult, op1=ALU.add)
                    else:
                        last = nc.vector.tensor_scalar(out[:, i, k], o, scalar, None, ALU.mult)
                    seen.add((k, i))
                    last.then_inc(combined if x == c - 1 else added, 1)

            with dve.Fori(0, TURNS) as j:
                for k in range(KVH):
                    half = slice(k * HEAD, (k + 1) * HEAD)
                    nc.vector.tensor_copy(query[half, k], m.q_a[half, bass.ds(j + part * TURNS, 1), 0:SEQ]
                                          .rearrange("p a t -> p (a t)")).then_inc(staged, 1)
                nc.vector.tensor_copy(gate[:].rearrange("p i k c -> p (i k) c"),
                                      m.gates[:].rearrange("p i (k g c) -> p (i k) g c", k=KVH, g=GQA)
                                      [:, :, bass.ds(j + part * TURNS, 1), :].rearrange("p i a c -> p i (a c)")).then_inc(staged, 1)
                dve.wait_ge(staged, j * 3 + 3)
                seen = set()
                for n in range(N + 2):
                    if n < N:
                        maximum(j, n)
                    if 1 <= n <= N:
                        keep(j, n - 1)
                    if n >= 2:
                        combine(j, n - 2, seen)
                dve.wait_ge(combined, j * N + N)
                for k in range(KVH):
                    last = nc.vector.tensor_copy(
                        m.o_nsa[:, 0:QT].rearrange("p i (h d) -> p i h d", d=HEAD)[:, :, bass.ds(j + (part * TURNS + k * GQA), 1), :]
                        .rearrange("p i a d -> p i (a d)"), out[:, :, k])
                last.then_inc(written, 1)
                dve.wait_ge(written, j + 1)


ROWS = DEC * KVH * GQA
KEYS = PAGES * PAGE
WINDOW_TILES = WINDOW // P


def decode_scores(nc, m):
    with ExitStack() as stack:
        sem = phase(nc, stack)

        def sb(name, shape, dtype=F32):
            return stack.enter_context(nc.sbuf_tensor(name, shape, dtype))

        R = ROWS
        WINDOW_SLOTS = 4
        over = m.over_work()
        last_slot = over("last_key_slot", [P, PAGES // 2, 2 * P])
        window = over("window_keys", [P, WINDOW_SLOTS, WINDOW])
        slc, win = over("slc_scores", [R, KEYS + 1]), over("win_scores", [R, WINDOW + 1])
        query = sb("decode_q", [P, DEC, R])
        cmp = sb("cmp_scores", [R, P])
        small = sb("decode_small", [R, 32])
        folded = sb("block_probs", [R, 136])
        importance, rank, barred = sb("importance", [R, N_SEL]), sb("rank", [R, N_SEL]), sb("barred", [R, N_SEL])
        new_probs = sb("new_probs", [R, 2, DEC])
        gate = sb("decode_gate", [R, 3])
        group_sum, own = sb("group_sum_sb", [R, R]), sb("own_column_sb", [R, DEC])
        spare = m.v_hg[:].rearrange("p i f -> p (i f)")
        SS = N_SEL * N_SEL
        earlier, greater, equal = (spare[0:R, a * SS:(a + 1) * SS].rearrange("r (s u) -> r s u", s=N_SEL) for a in range(3))
        small_in = sem("decode_small_in")
        mask_in = sem("earlier_mask_in")
        query_ready = sem("decode_query_ready")
        window_in = [sem(f"window_keys_in{s}") for s in range(WINDOW_SLOTS)]
        last_in = sem("last_keys_in")
        keys_read = sem("decode_keys_read")
        scores_done = sem("decode_scores_done")
        step_done = sem("decode_step")
        exp_done = sem("decode_exp_done")
        cmp_probs_ready = sem("cmp_probs_ready")
        imp_done = sem("importance_product_done")
        bias_ready = sem("decode_exp_bias_ready")
        probs_ready = sem("decode_probs_ready")
        turned = sem("decode_turned")
        turned_kept = sem("decode_turned_kept")
        block = stack.enter_context(nc.Block())

        @block.sync
        def _(sp):
            sp.dma_start(gate[:], m.dram["gate_rows"].rearrange("b h c -> (b h) c")).then_inc(small_in, 16)
            sp.dma_start(group_sum[:], m.dram["group_sum"]).then_inc(small_in, 16)
            sp.dma_start(own[:], m.dram["own_column"]).then_inc(small_in, 16)
            for b in range(DEC):
                s = b % WINDOW_SLOTS
                if b == WINDOW_SLOTS:
                    load_pages(sp, m, m.dram["slc_k"], DEC - 1, last_slot, last_in)
                    sp.wait_ge(keys_read, 2)
                    sp.dma_start(spare[0:R, 0:SS], m.dram["earlier"]).then_inc(mask_in, 16)
                if b >= WINDOW_SLOTS:
                    sp.wait_ge(keys_read, b - WINDOW_SLOTS + 1)
                sp.dma_start(window[:, s], m.dram["win_k"][b]).then_inc(window_in[s], 16)

        @block.tensor
        def _(pe):
            pe.wait_ge(query_ready, 2)
            for b in range(DEC):
                nc.tensor.matmul(m.bank[5][0:R, 0:N_CMP_D], query[:, b], m.kc_cache[:, b, 0:N_CMP_D],
                                 start=b == 0, stop=b == DEC - 1)
            for n, keys in enumerate((m.k_slc, m.k_win)):
                for b in range(DEC):
                    last = nc.tensor.matmul(m.bank[5][0:R, P + n:P + n + 1], query[:, b], keys[:, SEQ + b:SEQ + b + 1],
                                            start=b == 0, stop=b == DEC - 1)
            last.then_inc(scores_done, 1)
            for b in range(DEC):
                if b == DEC // 2:
                    pe.wait_ge(cmp_probs_ready, 1)
                    nc.tensor.matmul(m.bank[6][0:R, 0:N_CMP_D], group_sum[:], cmp[:, 0:N_CMP_D],
                                     start=True, stop=True).then_inc(imp_done, 1)
                slot = m.slots[b] if b < DEC - 1 else last_slot
                if b == DEC - 1:
                    pe.wait_ge(last_in, 16 * PAGES)
                for a in range(4):
                    nc.tensor.matmul(m.bank[a][0:R, :], query[:, b], slot[:, 2 * a:2 * a + 2],
                                     start=b == 0, stop=b == DEC - 1, skip_group_check=True)
                pe.wait_ge(window_in[b % WINDOW_SLOTS], 16 * (b // WINDOW_SLOTS + 1))
                nc.tensor.matmul(m.bank[4][0:R, :], query[:, b], window[:, b % WINDOW_SLOTS],
                                 start=b == 0, stop=b == DEC - 1, skip_group_check=True).then_inc(keys_read, 1)
            pe.wait_ge(probs_ready, 1)
            for t in range(WINDOW_TILES):
                nc.tensor.transpose(m.bank[2][:, t * R:(t + 1) * R], win[:, t * P:(t + 1) * P], m.identity[0:R, 0:R])
            nc.tensor.transpose(m.bank[2][0:N_CMP_D, WINDOW_TILES * R:(WINDOW_TILES + 1) * R], cmp[:, 0:N_CMP_D],
                                m.identity[0:R, 0:R])
            for n in range(2):
                last = nc.tensor.transpose(m.bank[3][0:DEC, n * R:(n + 1) * R], new_probs[:, n], m.identity[0:R, 0:R])
            last.then_inc(turned, 1)
            for t in range(PAGES):
                last = nc.tensor.transpose(m.bank[t // 8][:, (t % 8) * R:(t % 8 + 1) * R], slc[:, t * P:(t + 1) * P],
                                           m.identity[0:R, 0:R])
                if t % 8 == 7:
                    last.then_inc(turned, 1)

        @block.scalar
        def _(act):
            act.wait_ge(small_in, 48)
            nc.scalar.activation(gate[:], gate[:], ACT.Sigmoid).then_inc(exp_done, 1)
            for n, scores in enumerate((cmp[:, 0:N_CMP_D], win[:], slc[:])):
                act.wait_ge(bias_ready, n + 1)
                nc.scalar.activation(scores, scores, ACT.Exp, scale=SCALE, bias=small[:, 3 + n:4 + n],
                                     accum_out=small[:, 6 + n:7 + n]).then_inc(exp_done, 1)
            act.wait_ge(turned, 2)
            nc.scalar.activation(m.slc_t[:, 0:8].rearrange("p t r -> p (t r)"), m.bank[0], ACT.Copy).then_inc(turned_kept, 1)

        @block.vector
        def _(dve):
            step = Chain(dve, step_done)
            step(nc.vector.memset(query[:], 0.0))
            for k in range(KVH):
                half = slice(k * HEAD, (k + 1) * HEAD)
                flat = query[half].rearrange("p b r -> p (b r)")
                for g in range(GQA):
                    at = k * GQA + g
                    last = nc.vector.tensor_copy(flat[:, at:at + (DEC - 1) * 72 + 1:72], m.q_a[half, g, SEQ:T])
                last.then_inc(query_ready, 1)
            dve.wait_ge(scores_done, 1)
            step(nc.vector.tensor_copy(cmp[:, 0:N_CMP_D], m.bank[5][0:R, 0:N_CMP_D]))
            step(nc.vector.tensor_copy(slc[:, KEYS:], m.bank[5][0:R, P:P + 1]))
            step(nc.vector.tensor_copy(win[:, WINDOW:], m.bank[5][0:R, P + 1:P + 2]))

            def exp_bias(n, scores):
                step(nc.vector.tensor_reduce(small[:, n:n + 1], scores, AX.X, ALU.max))
                nc.vector.tensor_scalar(small[:, 3 + n:4 + n], small[:, n:n + 1], -SCALE, None,
                                        ALU.mult).then_inc(bias_ready, 1)

            exp_bias(0, cmp[:, 0:N_CMP_D])
            dve.wait_ge(exp_done, 2)
            step(nc.vector.reciprocal(small[:, 9:10], small[:, 6:7]))
            nc.vector.tensor_scalar(cmp[:, 0:N_CMP_D], cmp[:, 0:N_CMP_D], small[:, 9:10], None,
                                    ALU.mult).then_inc(cmp_probs_ready, 1)
            step(nc.vector.memset(folded[:], 0.0))
            dve.wait_ge(imp_done, 1)
            step(nc.vector.tensor_scalar(cmp[:, 0:N_CMP_D], cmp[:, 0:N_CMP_D], gate[:, 2:3], None, ALU.mult))
            step(nc.vector.tensor_copy(folded[:, 1:1 + N_CMP_D], m.bank[6][0:R, 0:N_CMP_D]))
            step(nc.vector.tensor_reduce(importance[:], folded[:, 0:4 * N_SEL].rearrange("r (s u) -> r s u", u=4),
                                         AX.X, ALU.add))
            step(nc.vector.tensor_tensor(importance[:], importance[:], folded[:, 4:4 * N_SEL + 1:4], ALU.add))
            step(nc.vector.memset(importance[:, 0:1], FORCED))
            step(nc.vector.memset(importance[:, N_SEL - 2:N_SEL], FORCED))
            dve.wait_ge(keys_read, 2)
            dve.wait_ge(mask_in, 16)
            mine = importance[:].rearrange("r (s a) -> r s a", a=1).to_broadcast([R, N_SEL, N_SEL])
            other = importance[:].rearrange("r (a u) -> r a u", a=1).to_broadcast([R, N_SEL, N_SEL])
            step(nc.vector.tensor_tensor(greater, other, mine, ALU.is_gt))
            step(nc.vector.tensor_tensor(equal, other, mine, ALU.is_equal))
            step(nc.vector.tensor_tensor(equal, equal, earlier, ALU.mult))
            step(nc.vector.tensor_tensor(greater, greater, equal, ALU.add))
            step(nc.vector.tensor_reduce(rank[:], greater, AX.X, ALU.add))
            step(nc.vector.tensor_scalar(barred[:], rank[:], float(TOPK), None, ALU.is_ge))
            step(nc.vector.tensor_scalar(barred[:], barred[:], NEG, None, ALU.mult))
            dve.wait_ge(keys_read, DEC)
            step(nc.vector.tensor_copy(win[:, 0:WINDOW], m.bank[4][0:R, :]))
            step(nc.vector.tensor_scalar(win[:, 0:1], win[:, 0:1], NEG, None, ALU.add))
            exp_bias(1, win[:])
            for a in range(4):
                blocks = 512 // SEL
                last = nc.vector.tensor_tensor(
                    slc[:, a * 512:(a + 1) * 512].rearrange("r (s u) -> r s u", u=SEL),
                    m.bank[a][0:R, :].rearrange("r (s u) -> r s u", u=SEL),
                    barred[:, a * blocks:(a + 1) * blocks].rearrange("r (s a) -> r s a", a=1).to_broadcast([R, blocks, SEL]),
                    ALU.add)
            step(last)
            step(nc.vector.tensor_tensor(slc[:, KEYS:], slc[:, KEYS:], barred[:, N_SEL - 1:N_SEL], ALU.add))
            exp_bias(2, slc[:])
            dve.wait_ge(exp_done, 4)
            step(nc.vector.reciprocal(small[:, 10:12], small[:, 7:9]))
            for n, (scores, branch) in enumerate(((win, 1), (slc, 0))):
                step(nc.vector.tensor_scalar(scores[:], scores[:], small[:, 10 + n:11 + n], gate[:, branch:branch + 1],
                                             ALU.mult, ALU.mult))
            step(nc.vector.tensor_scalar(new_probs[:, 0], own[:], slc[:, KEYS:], None, ALU.mult))
            nc.vector.tensor_scalar(new_probs[:, 1], own[:], win[:, WINDOW:], None, ALU.mult).then_inc(probs_ready, 1)
            dve.wait_ge(turned, 1)
            nc.vector.tensor_copy(m.rest_t[:, 0:WINDOW_TILES].rearrange("p t r -> p (t r)"), m.bank[2][:, 0:WINDOW_TILES * R])
            nc.vector.tensor_copy(m.rest_t[0:N_CMP_D, WINDOW_TILES], m.bank[2][0:N_CMP_D, WINDOW_TILES * R:(WINDOW_TILES + 1) * R])
            nc.vector.tensor_copy(m.new_t[:].rearrange("b n r -> b (n r)"), m.bank[3][0:DEC, 0:2 * R])
            dve.wait_ge(turned, 3)
            nc.vector.tensor_copy(m.slc_t[:, 8:16].rearrange("p t r -> p (t r)"), m.bank[1]).then_inc(turned_kept, 1)


def decode_values(nc, m):
    with ExitStack() as stack:
        sem = phase(nc, stack)
        over = m.over_work()
        last_slot = over("last_value_slot", [P, PAGES // 2, 2 * P])
        window = over("window_values", [P, DEC, WINDOW])
        HEADS = KVH * GQA
        out = stack.enter_context(nc.sbuf_tensor("decode_out", [HEADS, DEC, HEAD], F32))
        window_in = [sem(f"window_values_in{s}") for s in range(DEC // 2)]
        last_in = sem("last_values_in")
        values_done = sem("decode_values_done")
        half_done = sem("first_half_kept")
        squares = stack.enter_context(nc.sbuf_tensor("prompt_row_squares", [P, 2, 512], F32))
        squared, rooted, inverted = sem("prompt_squared"), sem("prompt_rooted"), sem("prompt_inverted")
        stored, returned = sem("decode_out_stored"), sem("decode_out_returned")
        out_ready = sem("decode_out_ready")
        block = stack.enter_context(nc.Block())

        @block.sync
        def _(sp):
            for s in range(DEC // 2):
                sp.dma_start(window[:, 2 * s:2 * s + 2], m.dram["win_v"][2 * s:2 * s + 2]
                             .rearrange("b p f -> p b f")).then_inc(window_in[s], 16)
            load_pages(sp, m, m.dram["slc_v"], DEC - 1, last_slot, last_in)
            sp.wait_ge(out_ready, 2)
            sp.dma_start(m.dram["o_rows"], out[:].rearrange("h b d -> h (b d)")).then_inc(stored, 16)
            sp.wait_ge(stored, 16)
            sp.dma_start(m.o_nsa[0:DEC, 8].rearrange("b (h d) -> b h d", d=HEAD),
                         m.dram["o_rows"].rearrange("h (b d) -> b h d", d=HEAD)).then_inc(returned, 16)
            sp.wait_ge(returned, 16)

        @block.tensor
        def _(pe):
            for b in range(DEC):
                rows = slice(b * HEADS, (b + 1) * HEADS)
                o = m.bank[6 + b // 4][0:HEADS, (b % 4) * P:(b % 4 + 1) * P]
                if b == DEC - 1:
                    pe.wait_ge(last_in, 16 * PAGES)
                slot = m.slots[b] if b < DEC - 1 else last_slot
                nc.tensor.matmul(o, m.rest_t[0:N_CMP_D, WINDOW_TILES, rows], m.vc_cache[0:N_CMP_D, b],
                                 start=True, stop=False)
                nc.tensor.matmul(o, m.new_t[:, 0, rows], m.kv_a[0:DEC, 8, 384:512], start=False, stop=False)
                nc.tensor.matmul(o, m.new_t[:, 1, rows], m.kv_b[0:DEC, 8, 128:256], start=False, stop=False)
                for t in range(PAGES):
                    nc.tensor.matmul(o, m.slc_t[:, t, rows], slot[:, t // 2, (t % 2) * P:(t % 2 + 1) * P],
                                     start=False, stop=False)
                pe.wait_ge(window_in[b // 2], 16)
                for t in range(WINDOW_TILES):
                    last = nc.tensor.matmul(o, m.rest_t[:, t, rows], window[:, b, t * P:(t + 1) * P],
                                            start=False, stop=t == WINDOW_TILES - 1)
                if b % 4 == 3:
                    last.then_inc(values_done, 1)

        @block.scalar
        def _(act):
            for i in range(QT):
                if i >= 2:
                    act.wait_ge(squared, i - 1)
                nc.scalar.activation(squares[:, i % 2], m.o_nsa[:, i], ACT.Square,
                                     accum_out=m.row_sums[:, i:i + 1]).then_inc(squared, 1)
            act.wait_ge(squared, QT)
            nc.scalar.activation(m.row_sums[:, 0:QT], m.row_sums[:, 0:QT], ACT.Sqrt, scale=1.0 / NSA,
                                 bias=m.vectors[:, V_EPS:V_EPS + 1]).then_inc(rooted, 1)

        @block.vector
        def _(dve):
            dve.wait_ge(rooted, 1)
            nc.vector.reciprocal(m.row_sums[:, 0:QT], m.row_sums[:, 0:QT]).then_inc(inverted, 1)
            dve.wait_ge(inverted, 1)
            for i in range(QT):
                nc.vector.tensor_scalar(m.o_nsa[:, i], m.o_nsa[:, i], m.row_sums[:, i:i + 1], None, ALU.mult)
            for n in range(2):
                dve.wait_ge(values_done, n + 1)
                o = m.bank[6 + n][0:HEADS, :].rearrange("h (b f) -> h b f", f=P)
                mine = out[:, 4 * n:4 * n + 4]
                nc.vector.tensor_scalar(mine, o[:, :, 0:HEAD], m.vectors[0:HEADS, V_HEAD0:V_HEAD0 + 1], None,
                                        ALU.mult).then_inc(half_done, 1)
                dve.wait_ge(half_done, n + 1)
                nc.vector.scalar_tensor_tensor(out=mine, in0=o[:, :, HEAD:P], scalar=m.vectors[0:HEADS, V_HEAD1:V_HEAD1 + 1],
                                               in1=mine, op0=ALU.mult, op1=ALU.add).then_inc(out_ready, 1)


def norm_recurrent(nc, m):
    with ExitStack() as stack:
        sem = phase(nc, stack)
        sums = m.head_roots
        inverted = sem("head_inverted")
        scaled = sem("head_scaled")
        turned = sem("recurrent_turned")
        kept = sem("recurrent_kept")
        position = stack.enter_context(nc.sbuf_tensor("position_products", [P, 2, HID], F32))
        weighted, bias_done = sem("position_weighted"), sem("compress_bias_done")
        block = stack.enter_context(nc.Block())

        @block.sync
        def _(sp):
            sp.dma_start(m.table[:], m.dram["page_table"]).then_inc(m.table_in, 16)
            sp.dma_start(m.pos[:], m.dram["cmp_pos"]).then_inc(m.pos_in, 16)
            for l in range(2):
                sp.dma_start(m.w1[:, :, l], m.dram["cmp_w1"][:, :, l]).then_inc(m.w1_in[l], 16)
            for target, source in ((m.w2_k, "cmp_w2_k"), (m.w2_v, "cmp_w2_v")):
                sp.dma_start(target[:], m.dram[source]).then_inc(m.weights_in, 16)
            sp.wait_ge(m.rows_stored, 8 * 16)
            for a in range(2 * KVH):
                sp.dma_start(m.row_halves[:, a], m.dram["out_cmp_p"][:, a * HEAD:(a + 1) * HEAD]
                             .rearrange("(n s) d -> n s d", s=HALF)).then_inc(m.halves_in, 16)
            sp.wait_ge(m.table_in, 16)

        @block.vector
        def _(dve):
            def weigh_position(l):
                dve.wait_ge(m.w1_in[l], 16)
                for s in range(PAIRS):
                    n = l * PAIRS + s
                    for c in range(2):
                        w1, pos = m.w1[:, c, l, s], m.pos[:, c, l, s:s + 1]
                        if n == 0:
                            last = nc.vector.tensor_scalar(position[:, c], w1, pos, None, ALU.mult)
                        else:
                            dve.wait_ge(weighted, 2 * n + c - 1)
                            last = nc.vector.scalar_tensor_tensor(out=position[:, c], in0=w1, scalar=pos,
                                                                  in1=position[:, c], op0=ALU.mult, op1=ALU.add)
                        last.then_inc(weighted, 1)

            nc.vector.reciprocal(sums[:, 0:QT], sums[:, 0:QT])
            nc.vector.reciprocal(sums[0:DEC, QT], sums[0:DEC, QT]).then_inc(inverted, 1)
            dve.wait_ge(inverted, 1)

            def scale(i):
                count = TILES[i][1]
                v = m.v_hg[0:count, i].rearrange("p (h d) -> p h d", h=HGH)
                nc.vector.tensor_tensor(v, v, sums[0:count, i].rearrange("p (h a) -> p h a", a=1)
                                        .to_broadcast([count, HGH, P]), ALU.mult).then_inc(scaled, 1)

            scale(0)
            for i, (first, count) in enumerate(TILES):
                if i + 1 < 9:
                    scale(i + 1)
                dve.wait_ge(turned, i + 1)
                for c in range(4):
                    last = nc.vector.scalar_tensor_tensor(
                        out=m.gate_b[:, c, first:first + count], in0=m.bank[i % 2][:, c * P:c * P + count],
                        scalar=m.vectors[:, V_HG + c:V_HG + c + 1], in1=m.gate_b[:, c, first:first + count],
                        op0=ALU.mult, op1=ALU.mult)
                last.then_inc(kept, 1)
            dve.wait_ge(m.pos_in, 16)
            weigh_position(0)
            weigh_position(1)
            dve.wait_ge(bias_done, 1)
            nc.vector.tensor_scalar(m.hidden_bias[:], m.bank[7][:, 0:4], float(DM), None, ALU.mult)

        @block.tensor
        def _(pe):
            for i, (first, count) in enumerate(TILES):
                pe.wait_ge(scaled, i + 1)
                if i >= 2:
                    pe.wait_ge(kept, i - 1)
                for c in range(4):
                    last = nc.tensor.transpose(m.bank[i % 2][:, c * P:c * P + count],
                                               m.v_hg[0:count, i, c * P:(c + 1) * P], m.identity[0:count, 0:count])
                last.then_inc(turned, 1)
            pe.wait_ge(weighted, 2 * 2 * PAIRS)
            for u in range(4):
                last = nc.tensor.matmul(m.bank[7][:, u:u + 1], position[:, u // 2, (u % 2) * P:(u % 2 + 1) * P],
                                        m.mean_weights[:, 0:1], start=True, stop=True)
            last.then_inc(bias_done, 1)


def mix_features(nc, m):
    with ExitStack() as stack:
        sem = phase(nc, stack)
        squares = stack.enter_context(nc.sbuf_tensor("row_squares", [DEC, 512], F32))
        sums = m.row_sums[0:DEC, QT:QT + 1]
        tile = stack.enter_context(nc.sbuf_tensor("mix_tile", [P, 3, 4, P], F32))
        high_ready, low_ready = sem("mix_high_ready"), sem("mix_low_ready")
        gated_high, gated_low = sem("mix_gated_high"), sem("mix_gated_low")
        summed = sem("mix_summed")
        rooted = sem("mix_rooted")
        inverted = sem("mix_inverted")
        scaled = sem("mix_scaled")
        turned = sem("mix_turned")
        kept = sem("mix_kept")
        block = stack.enter_context(nc.Block())

        @block.scalar
        def _(act):
            nc.scalar.activation(squares[:], m.o_nsa[0:DEC, QT], ACT.Square, accum_out=sums).then_inc(summed, 1)
            act.wait_ge(summed, 1)
            nc.scalar.activation(sums, sums, ACT.Sqrt, scale=1.0 / NSA,
                                 bias=m.vectors[0:DEC, V_EPS:V_EPS + 1]).then_inc(rooted, 1)

            def high(i):
                first, count = TILES[i]
                act.wait_ge(kept, i + 1)
                nc.scalar.activation(m.xn[0][:, 0:4, first:first + count], tile[:, i % 3, :, 0:count],
                                     ACT.Copy).then_inc(high_ready, 1)

            nc.scalar.activation(m.xn[0][:, 4, :], m.gate_b[:, 0], ACT.Copy).then_inc(gated_high, 1)
            for i, (first, count) in enumerate(TILES):
                act.wait_ge(turned, i + 1)
                if i >= 3:
                    act.wait_ge(low_ready, i - 2)
                for c in range(4):
                    last = nc.scalar.activation(tile[:, i % 3, c, 0:count], m.bank[i % 2][:, c * P:c * P + count],
                                                ACT.Copy, scale=m.vectors[:, V_NSA + c:V_NSA + c + 1])
                last.then_inc(kept, 1)
                if i >= 1:
                    high(i - 1)
                if i in (2, 4, 6):
                    c = i // 2
                    nc.scalar.activation(m.xn[0][:, 4 + c, :], m.gate_b[:, c], ACT.Copy).then_inc(gated_high, 1)
            high(8)

        @block.vector
        def _(dve):
            dve.wait_ge(rooted, 1)
            nc.vector.reciprocal(sums, sums).then_inc(inverted, 1)
            dve.wait_ge(inverted, 1)
            nc.vector.tensor_scalar(m.o_nsa[0:DEC, QT], m.o_nsa[0:DEC, QT], sums, None, ALU.mult).then_inc(scaled, 1)
            for i, (first, count) in enumerate(TILES):
                dve.wait_ge(high_ready, i + 1)
                nc.vector.tensor_tensor(m.xn[1][:, 0:4, first:first + count], tile[:, i % 3, :, 0:count],
                                        m.xn[0][:, 0:4, first:first + count].bitcast(F32), ALU.subtract).then_inc(low_ready, 1)
                if i in (1, 3, 5, 7):
                    c = i // 2
                    dve.wait_ge(gated_high, c + 1)
                    nc.vector.tensor_tensor(m.xn[1][:, 4 + c, :], m.gate_b[:, c], m.xn[0][:, 4 + c, :].bitcast(F32),
                                            ALU.subtract).then_inc(gated_low, 1)

        @block.tensor
        def _(pe):
            for i, (first, count) in enumerate(TILES):
                if i == QT:
                    pe.wait_ge(scaled, 1)
                if i >= 2:
                    pe.wait_ge(kept, i - 1)
                for c in range(4):
                    last = nc.tensor.transpose(m.bank[i % 2][:, c * P:c * P + count],
                                               m.o_nsa[0:count, i, c * P:(c + 1) * P], m.identity[0:count, 0:count])
                last.then_inc(turned, 1)


class NextNorm:

    def __init__(self, nc, m, squares, sem, name, gain=None, target=None):
        self.nc, self.m, self.gain, self.target = nc, m, gain, target
        self.squares = squares
        self.high_ready, self.low_ready = sem(f"{name}_next_high_ready"), sem(f"{name}_next_low_ready")
        self.squared, self.added = sem(f"{name}_squared"), sem(f"{name}_added")

    def clear(self, dve):
        self.nc.vector.memset(self.m.total[:], 0.0).then_inc(self.added, 1)
        dve.wait_ge(self.added, 1)

    def at(self, tensor, c, g):
        return tensor[:, bass.ds(c, 1), cols(g)].rearrange("p a t -> p (a t)")

    def on_scalar(self, act, c, g):
        h = self.at(self.m.h, c, g)
        if self.target:
            self.nc.scalar.activation(self.at(self.target[0], c, g), h, ACT.Copy,
                                      scale=self.m.vectors[:, bass.ds(c + self.gain, 1)]).then_inc(self.high_ready, 1)
        self.nc.scalar.activation(self.squares[:, g], h, ACT.Square).then_inc(self.squared, 1)

    def on_vector(self, dve, c, g):
        done = c * GROUPS + (g + 1)
        if self.target:
            dve.wait_ge(self.high_ready, done)
            self.nc.vector.scalar_tensor_tensor(
                out=self.at(self.target[1], c, g), in0=self.at(self.m.h, c, g),
                scalar=self.m.vectors[:, bass.ds(c + self.gain, 1)],
                in1=self.at(self.target[0], c, g).bitcast(F32), op0=ALU.mult,
                op1=ALU.subtract).then_inc(self.low_ready, 1)
        dve.wait_ge(self.squared, done)
        total = self.m.total[:, cols(g)]
        self.nc.vector.tensor_tensor(total, total, self.squares[:, g], ALU.add).then_inc(self.added, 1)


def add_linear(nc, m, name, weights, source, primed=False, following=None, load=False, norm=None):
    with ExitStack() as stack:
        sem = phase(nc, stack)
        w = SplitWeights(nc, sem, name, m.buffers, weights, primed, following)
        following_norm = None
        if norm:
            squares = stack.enter_context(nc.sbuf_tensor(f"{name}_squares", [P, GROUPS, G], F32))
            following_norm = NextNorm(nc, m, squares, sem, name, *norm)
        residual_in = sem(f"{name}_residual_in")
        banks_free = [sem(f"{name}_banks_free{s}") for s in range(2)]
        block = stack.enter_context(nc.Block())
        turns = KC // 2

        @block.sync
        def _(sp):
            w.load_all(sp, turns)

        @block.tensor
        def _(pe):
            with pe.Fori(0, turns) as i:
                for s in range(2):
                    pe.wait_ge(w.ready[s], i + 1)
                    for g in range(GROUPS):
                        pe.wait_ge(banks_free[s], i * GROUPS + (g + 1))
                        w.product(m.bank[3 * s + g][:, 0:G], s, source, g)

        @block.scalar
        def _(act):
            if load:
                act.dma_start(m.h[:], m.dram["x"]).then_inc(residual_in, 16)
            for s in range(2):
                w.make_high(act, 0, s, first=True)

            def work(i, last):
                for s in range(2):
                    w.make_high(act, i + 1, s, last=last)
                    if following_norm:
                        for g in range(GROUPS):
                            act.wait_ge(banks_free[s], i * GROUPS + (GROUPS + g + 1))
                            following_norm.on_scalar(act, i * 2 + s, g)

            turns_but_last(act, turns, work)

        @block.vector
        def _(dve):
            if following_norm:
                following_norm.clear(dve)
            for s in range(2):
                dve.sem_inc(banks_free[s], GROUPS)
                w.make_low(dve, 0, s, first=True)
            if load:
                dve.wait_ge(residual_in, 16)

            def work(i, last):
                for s in range(2):
                    for g in range(GROUPS):
                        dve.wait_ge(w.done[s], i * GROUPS + (g + 1))
                        h = m.h[:, bass.ds(i * 2 + s, 1), cols(g)].rearrange("p a t -> p (a t)")
                        nc.vector.tensor_tensor(h, m.bank[3 * s + g][:, 0:G], h, ALU.add).then_inc(banks_free[s], 1)
                    w.make_low(dve, i + 1, s, last=last)
                    if following_norm:
                        for g in range(GROUPS):
                            following_norm.on_vector(dve, i * 2 + s, g)

            turns_but_last(dve, turns, work)


def gated_pair(nc, m, name, weights, sources, turns, function, finish, primed=False, following=None, norm_second=True,
               first_part=True, embedding=False, final=False):
    with ExitStack() as stack:
        sem = phase(nc, stack)
        w = SplitWeights(nc, sem, name, m.buffers, weights, primed, following)
        active = stack.enter_context(nc.sbuf_tensor(f"{name}_active", [P, GROUPS, G], F32))
        result = stack.enter_context(nc.sbuf_tensor(f"{name}_result", [P, GROUPS, G], F32))
        factor = NormFactor(nc, m, sem, name, (m.bank[6], m.bank[7], m.bank[5]))
        next_norm = NextNorm(nc, m, m.last_squares, sem, name) if final else None
        scaled = sem(f"{name}_scaled")
        active_ready = sem(f"{name}_active_ready")
        rescaled = sem(f"{name}_rescaled")
        multiplied = sem(f"{name}_multiplied")
        finished = sem(f"{name}_finished")
        high_kept = sem(f"{name}_high_kept")
        embedding_in = sem(f"{name}_embedding_in")
        embedding_high = sem(f"{name}_embedding_high")
        embedding_ready = sem(f"{name}_embedding_ready")
        block = stack.enter_context(nc.Block())

        @block.sync
        def _(sp):
            if embedding:
                sp.dma_start(m.p_raw[:], m.dram["p"]).then_inc(embedding_in, 16)
            w.load_all(sp, turns)

        @block.tensor
        def _(pe):
            if first_part:
                factor.mean(pe)
            with pe.Fori(0, turns) as i:
                for s in range(2):
                    pe.wait_ge(w.ready[s], i + 1)
                    if s and first_part:
                        pe.wait_ge(factor.root_ready, GROUPS)
                    if s and embedding:
                        pe.wait_ge(embedding_ready, 1)
                    for g in range(GROUPS):
                        pe.wait_ge(multiplied, i * GROUPS + (g + 1))
                        w.product(m.bank[3 * s + g][:, 0:G], s, sources[s], g)

        @block.scalar
        def _(act):
            for s in range(2):
                w.make_high(act, 0, s, first=True)
            if first_part:
                factor.root(act)
            if embedding:
                act.wait_ge(embedding_in, 16)
                nc.scalar.activation(m.p_in[0][:], m.p_raw[:], ACT.Copy).then_inc(embedding_high, 1)

            def work(i, last):
                w.make_high(act, i + 1, 0, last=last)
                for g in range(GROUPS):
                    act.wait_ge(scaled, i * GROUPS + (g + 1))
                    nc.scalar.activation(active[:, g], active[:, g], function).then_inc(active_ready, 1)
                for g in range(GROUPS):
                    if finish.high is not None:
                        act.wait_ge(multiplied, (i + 1) * GROUPS + (g + 1))
                        nc.scalar.activation(finish.high(i, g), result[:, g], ACT.Copy).then_inc(high_kept, 1)
                w.make_high(act, i + 1, 1, last=last)
                if final:
                    for g in range(GROUPS):
                        act.wait_ge(finished, i * GROUPS + (g + 1))
                        next_norm.on_scalar(act, i, g)

            turns_but_last(act, turns, work)

        @block.vector
        def _(dve):
            dve.sem_inc(multiplied, GROUPS)
            for s in range(2):
                w.make_low(dve, 0, s, first=True)
            if first_part:
                factor.invert(dve)
            if embedding:
                dve.wait_ge(embedding_high, 1)
                nc.vector.tensor_tensor(m.p_in[1][:], m.p_raw[:], m.p_in[0][:].bitcast(F32),
                                        ALU.subtract).then_inc(embedding_ready, 1)
            if final:
                next_norm.clear(dve)

            def work(i, last):
                for g in range(GROUPS):
                    dve.wait_ge(w.done[0], i * GROUPS + (g + 1))
                    nc.vector.tensor_tensor(active[:, g], m.bank[g][:, 0:G], m.scale[:, cols(g)],
                                            ALU.mult).then_inc(scaled, 1)
                w.make_low(dve, i + 1, 0, last=last)
                for g in range(GROUPS):
                    dve.wait_ge(active_ready, i * GROUPS + (g + 1))
                    if norm_second:
                        nc.vector.tensor_tensor(active[:, g], active[:, g], m.scale[:, cols(g)],
                                                ALU.mult).then_inc(rescaled, 1)
                for g in range(GROUPS):
                    if norm_second:
                        dve.wait_ge(rescaled, i * GROUPS + (g + 1))
                    dve.wait_ge(w.done[1], i * GROUPS + (g + 1))
                    nc.vector.tensor_tensor(result[:, g], m.bank[3 + g][:, 0:G], active[:, g],
                                            ALU.mult).then_inc(multiplied, 1)
                    if finish.high is not None:
                        dve.wait_ge(high_kept, i * GROUPS + (g + 1))
                        nc.vector.tensor_tensor(finish.low(i, g), result[:, g], finish.high(i, g).bitcast(F32),
                                                ALU.subtract).then_inc(finished, 1)
                    else:
                        dve.wait_ge(multiplied, (i + 1) * GROUPS + (g + 1))
                        h = m.h[:, bass.ds(i, 1), cols(g)].rearrange("p a t -> p (a t)")
                        nc.vector.tensor_tensor(h, h, result[:, g], ALU.add).then_inc(finished, 1)
                w.make_low(dve, i + 1, 1, last=last)
                if final:
                    for g in range(GROUPS):
                        next_norm.on_vector(dve, i, g)

            turns_but_last(dve, turns, work)


class SplitInto:

    def __init__(self, high=None, low=None):
        self.high, self.low = high, low


PARTS = ((0, 8), (8, 8), (16, 6))


def out_weights(m):
    return Weights(lambda i, s: m.dram["w_out"][i * 2 + s], (KC, KC))


def gate_up_weights(m, part):
    first, _ = PARTS[part]
    return Weights(lambda i, s: m.dram["w_gate_up"][i + first, :, s * KC:(s + 1) * KC], (KC, KC))


def down_weights(m, part):
    first, count = PARTS[part]
    return Weights(lambda i, s: m.dram["w_down"][i * 2 + s, :, first:first + count], (count, count))


def ple_weights(m):
    counts = (KC, DPLE // P)
    return Weights(lambda i, s: m.dram["w_ple"][i, :, s * KC:s * KC + counts[s]], counts)


def feed_forward(nc, m):
    def place(tensor):
        return lambda i, g: tensor[:, bass.ds(i, 1), cols(g)].rearrange("p a t -> p (a t)")

    for n, (first, count) in enumerate(PARTS):
        down = down_weights(m, n)
        last = n + 1 == len(PARTS)
        gated_pair(nc, m, f"ffn{n}", gate_up_weights(m, n), (m.normed, m.normed), count, ACT.Silu,
                   SplitInto(place(m.xn[0]), place(m.xn[1])), primed=True, following=down, first_part=n == 0)
        following = ple_weights(m) if last else gate_up_weights(m, n + 1)
        add_linear(nc, m, f"down{n}", down, m.xn, primed=True, following=following,
                   norm=(V_PLE, m.normed) if last else None)
        if n == 1:
            clear_semaphores(nc)


def gated_embedding(nc, m):
    gated_pair(nc, m, "ple", ple_weights(m), (m.normed, m.p_in), KC, ACT.Sigmoid, SplitInto(), primed=True,
               norm_second=False, embedding=True, final=True)


def layer(nc, d):
    m = Tensors(d)
    with ExitStack() as stack:
        def sb(name, shape, dtype=F32):
            return stack.enter_context(nc.sbuf_tensor(name, shape, dtype))

        psum = stack.enter_context(nc.psum_tensor("banks", [P, 8 * 512], F32))
        m.bank = [psum[:, i * 512:(i + 1) * 512] for i in range(8)]
        m.pair = [psum[:, i * 1024:(i + 1) * 1024] for i in range(2)]
        m.turn_bank = m.bank[4:6]
        m.identity = sb("identity_sb", [P, P])
        m.mean_weights = sb("mean_weights_sb", [P, P])
        m.vectors = sb("vectors_sb", [P, V_COLS])
        m.lower = sb("lower_bound", [P, 20])
        m.intra_mask = sb("intra_mask_sb", [P, P])
        m.row_pick = sb("row_pick_sb", [DEC, DEC, P])
        m.table = sb("table", [1, DEC * PAGES], I32)
        start = -(-nc.sbuf_base // 32) * 32
        m.xn = (sb("xn_high", [P, KC, T], F32R), sb("xn_low", [P, KC, T], F32R))
        m.over_xn = lambda: Overlay(nc, start, 2 * 4 * KC * T)
        mixers(nc, m, d, start)
        m.h = sb("h", [P, KC, T])
        m.total, m.scale = sb("square_total", [P, T]), sb("token_factor", [P, T])
        with ExitStack() as dense:
            m.normed = tuple(dense.enter_context(nc.sbuf_tensor(f"normed_{part}", [P, KC, T], F32R))
                             for part in ("high", "low"))
            m.buffers = SplitBuffers(nc, dense, "dense", KC)
            add_linear(nc, m, "out", out_weights(m), m.xn, following=gate_up_weights(m, 0), load=True,
                       norm=(V_FFN, m.normed))
            feed_forward(nc, m)
            over = m.over_xn()
            m.p_in = (over("p_high", [P, DPLE // P, T], F32R), over("p_low", [P, DPLE // P, T], F32R))
            m.p_raw = over("p_raw", [P, DPLE // P, T])
            m.last_squares = over("last_squares", [P, GROUPS, G])
            gated_embedding(nc, m)
        final_norm(nc, m)


def mixers(nc, m, d, start):
    with ExitStack() as stack:
        def sb(name, shape, dtype=F32):
            return stack.enter_context(nc.sbuf_tensor(name, shape, dtype))

        m.v_hg = sb("v_hg", [P, 9, 512])
        m.rows_stored = phase(nc, stack)("rows_stored")
        size = 32 * (2 * T * 4 // 32 + 2) + 2 * 4 * HGH * DEC
        over = Overlay(nc, nc.sbuf_top // 32 * 32 - size, size)
        m.total, m.scale = over("x_square_total", [P, T]), over("x_token_factor", [P, T])
        m.token_scale = over("x_token_factor_rows", [P, 9])
        m.decode_q, m.decode_forget = over("decode_q_b", [P, HGH, DEC]), over("decode_forget", [P, HGH, DEC])
        load_and_split(nc, m)
        lower_bound(nc, m)
        with ExitStack() as recurrent:
            m.q_b = recurrent.enter_context(nc.sbuf_tensor("q_b", [P, 4, T], F32))
            m.forget = recurrent.enter_context(nc.sbuf_tensor("forget", [P, 4, T], F32))
            project_features(nc, m, "recurrent", 0, ((m.q_b, ACT.Silu), (m.forget, ACT.Sigmoid)), norm=True)
            project_tokens(nc, m, "values", ((m.v_hg, 792, 512),))
            hgrn_prompt(nc, m)
        m.head_roots = sb("head_roots", [P, 9, HGH])
        m.gate_b = sb("gate_b", [P, 4, T])
        m.q_a = sb("q_a", [P, 4, T])
        m.k_slc = sb("k_slc_t", [P, T])
        m.k_win = sb("k_win_t", [P, T])
        m.kv_a = sb("kv_a", [P, 9, 512])
        m.kv_b = sb("kv_b", [P, 9, 280])
        project_features(nc, m, "query", 8, ((m.q_a, None), (m.gate_b, ACT.Silu)), decode=True)
        project_tokens(nc, m, "kv", ((m.kv_a, 0, 512), (m.kv_b, 512, 280)),
                       ((m.kv_a[:, :, 256:384], m.k_slc), (m.kv_b[:, :, 0:128], m.k_win)), store_rows(m))
        m.kc_prompt, m.vc_prompt = sb("kc_prompt", [P, P]), sb("vc_prompt", [P, P])
        m.kc_cache, m.vc_cache = sb("kc_cache", [P, DEC, P]), sb("vc_cache", [P, DEC, P])
        m.w1 = m.over_xn()("compress_w1", [P, 2, 2, PAIRS, HID])
        with ExitStack() as compression:
            def csb(name, shape):
                return compression.enter_context(nc.sbuf_tensor(name, shape, F32))

            m.w2_k, m.w2_v = csb("w2_k", [P, 2, KVH, P]), csb("w2_v", [P, 2, HEAD])
            m.pos, m.hidden_bias = csb("pos", [P, 2, 2, PAIRS]), csb("hidden_bias", [P, 4])
            per_page = PAGE // HALF
            m.cache_rows = csb("cache_rows", [P, 2, PAGES, PAIRS, 2, KVH, per_page])
            m.row_halves = m.cache_rows[0:SEQ // HALF, 1].rearrange("p a s c k n -> p (a s c k n)").rearrange(
                "p (a s d) -> p a s d", a=2 * KVH, s=HALF)
            sem = phase(nc, compression)
            m.table_in, m.weights_in, m.pos_in = sem("page_table_in"), sem("compress_w2_in"), sem("compress_pos_in")
            m.w1_in = [sem(f"compress_w1_in{l}") for l in range(2)]
            m.halves_in, m.page_in = sem("prompt_halves_in"), [sem(f"compress_page_in{s}") for s in range(2)]
            norm_recurrent(nc, m)
            compress(nc, m, True)
            compress(nc, m, False)
        m.o_nsa = sb("o_nsa", [P, 9, NSA])
        clear_semaphores(nc)
        m.row_sums = sb("row_sums", [P, 9])
        m.rest_t, m.new_t = sb("other_probs_turned", [P, 5, ROWS]), sb("new_probs_turned", [DEC, 2, ROWS])
        m.over_work = lambda: Overlay(nc, start, 7 * 4 * SEQ)
        behind = Overlay(nc, start + 7 * 4 * SEQ, 2 * 4 * KC * T - 7 * 4 * SEQ)
        m.slots = [behind(f"page_slot{n}", [P, PAGES // 2, 2 * P]) for n in range(4)]
        m.slc_t = behind("slc_probs_turned", [P, PAGES, ROWS])
        m.slots = [m.v_hg[:, 0:8, 0:256], m.v_hg[:, 0:8, 256:512], m.kv_a[:, 0:8, 0:256]] + [slot[:] for slot in m.slots]
        with ExitStack() as attention:
            def asb(name, shape):
                return attention.enter_context(nc.sbuf_tensor(name, shape, F32))

            m.gates = asb("gates", [P, QT, 24])
            m.masks = (asb("causal_add_sb", [P, P]), asb("window_add_sb", [P, P]),
                       asb("cmp_add_sb", [P, 56 + P]), asb("cmp_keep_sb", [P, 56 + P]))
            prepare_attention(nc, m)
            prompt_attention(nc, m, 0, m.dram["slc_k"])
            decode_scores(nc, m)
            prompt_attention(nc, m, 1, m.dram["slc_v"])
        decode_values(nc, m)
        mix_features(nc, m)
        clear_semaphores(nc)


def constants():
    f = np.float32
    s, t = np.arange(P)[:, None], np.arange(P)[None, :]
    c = {}
    c["identity"] = np.eye(P, dtype=f)
    c["mean_weights"] = np.full((P, P), 1.0 / DM, f)
    c["intra_mask"] = ((s // BLOCK32 == t // BLOCK32) & (s <= t)).astype(f)
    c["row_pick"] = np.repeat(np.eye(DEC, dtype=f)[:, :, None], P, axis=2)
    q, k = s, t
    c["causal_add"] = np.where(k > q, f(NEG), f(0))
    c["window_add"] = np.where(k <= q, f(NEG), f(0))
    keep = HALF * (np.arange(56 + P)[None, :] - 56) + 31 <= s
    c["cmp_keep"] = keep.astype(f)
    c["cmp_add"] = np.where(keep, f(0), f(NEG))
    r = np.arange(DEC * KVH * GQA)
    c["group_sum"] = (r[:, None] // GQA == r[None, :] // GQA).astype(f)
    c["own_column"] = (r[:, None] // 8 == np.arange(DEC)[None, :]).astype(f)
    b = np.arange(N_SEL)
    c["earlier"] = np.tile((b[None, :] < b[:, None]).astype(f).reshape(1, -1), (len(r), 1))
    return c


def columns(v):
    return v.reshape(-1, P).T


def weight_chunks(w, order=None):
    k, n = w.shape
    return np.ascontiguousarray(w.reshape(k // P, P, n // P, P).transpose(2, 1, 0, 3))


def laid_out(i):
    a = {}
    x = np.concatenate([i["x_prompt"][0], i["x_sample"][:, 0]])
    a["x"] = np.ascontiguousarray(x.T.reshape(KC, P, T).transpose(1, 0, 2))
    w = i["w_in"][0]
    start = np.cumsum([0, 512, 256, 256, 256, 24, 512, 512, 512, 512])
    qa, kvc, kvs, kvw, gate, qb, fb, vb, gb = (w[:, start[n]:start[n + 1]] for n in range(9))
    qa = qa.reshape(DM, KVH, GQA, HEAD).transpose(0, 2, 1, 3).reshape(DM, NSA)
    a["w_feature"] = weight_chunks(np.concatenate([qb, fb, qa, gb], axis=1))
    gate = gate.reshape(DM, 3, KVH * GQA)[:, [1, 2, 0]].transpose(0, 2, 1).reshape(DM, 24)
    token = np.concatenate([kvc, kvs, kvw, gate, vb], axis=1)
    a["w_token"] = np.ascontiguousarray(token.reshape(KC, P, -1).transpose(1, 0, 2))
    v = [i["norm_mix"][0], i["norm_nsa_out"][0], i["norm_hg_out"][0], i["norm_ffn"][0], i["norm_ple"][0],
         i["norm_final"], i["hg_lb"][0], i["hg_lb"][1]]
    extra = np.zeros((P, 3), np.float32)
    extra[:, 0] = 1e-6
    extra[:, 1] = np.arange(P) // 4 % 2 == 0
    extra[:, 2] = np.arange(P) // 4 % 2 == 1
    a["vectors"] = np.concatenate([np.ascontiguousarray(columns(x)) for x in v] + [extra], axis=1)
    a["window_rows"] = i["state_kv_win"][0].reshape(DEC, WINDOW, 256)
    a["state_hgrn"] = i["state_hgrn"][0]
    a["w_out"] = weight_chunks(i["w_out"][0])
    gate_up = i["w_gate_up"][0]
    a["w_gate_up"] = np.concatenate([weight_chunks(gate_up[:, :DFF]), weight_chunks(gate_up[:, DFF:])], axis=2)
    a["w_down"] = weight_chunks(i["w_down"][0])
    a["w_ple"] = np.concatenate([weight_chunks(i["w_ple_gate"][0]), weight_chunks(i["w_ple_proj"][0])], axis=2)
    p = np.concatenate([i["p_prompt"][0, 0], i["p_sample"][0, :, 0]])
    a["p"] = np.ascontiguousarray(p.T.reshape(DPLE // P, P, T).transpose(1, 0, 2))
    a["cmp_w1"] = np.ascontiguousarray(i["cmp_w1"][0].reshape(2, 2, PAIRS, P, HID).transpose(3, 0, 1, 2, 4))
    a["cmp_pos"] = np.ascontiguousarray(i["cmp_pos"][0].reshape(2, 2, PAIRS, P).transpose(3, 0, 1, 2))
    w2 = i["cmp_w2"][0].reshape(2, 2, P, HEAD)
    w2_k = np.zeros((P, 2, KVH, KVH, HEAD), np.float32)
    for k in range(KVH):
        w2_k[:, :, k, k] = w2[0].transpose(1, 0, 2)
    a["cmp_w2_k"] = w2_k.reshape(P, 2, KVH, P)
    a["cmp_w2_v"] = np.ascontiguousarray(w2[1].transpose(1, 0, 2))
    cache = i["cache_kv_cmp"][0].reshape(POOL, PAGE // HALF, PAIRS, 2, 2, KVH, HEAD)
    a["cache_cmp"] = np.ascontiguousarray(cache.transpose(0, 3, 6, 2, 4, 5, 1)).reshape(POOL, P, 256)
    cache = i["cache_kv_slc"][0].reshape(POOL, PAGE, 2, P)
    a["slc_k"] = np.ascontiguousarray(cache[:, :, 0].transpose(0, 2, 1))
    a["slc_v"] = np.ascontiguousarray(cache[:, :, 1])
    window = i["state_kv_win"][0].reshape(DEC, WINDOW, 2, P)
    a["win_k"] = np.ascontiguousarray(window[:, :, 0].transpose(0, 2, 1))
    a["win_v"] = np.ascontiguousarray(window[:, :, 1].reshape(DEC, 4, P, P).transpose(0, 2, 1, 3)).reshape(DEC, P, WINDOW)
    a["page_table"] = i["page_table"].reshape(1, -1)
    a.update(constants())
    return a


OUTPUTS = {
    "out_cmp_p": (SEQ, 256), "out_slc_p": (SEQ, 256), "out_win_p": (WINDOW, 256), "out_hgrn_p": (HGH, P, P),
    "out_cmp_s": (DEC, 256), "out_slc_s": (DEC, 256), "out_win_s": (DEC, WINDOW, 256),
    "out_hgrn_s": (DEC, HGH, P, P), "out_y": (P, KC, T),
}
SCRATCH = {"gate_rows": (DEC, 8, 3), "o_rows": (KVH * GQA, DEC * HEAD)}


def kernel(**inputs):
    import concourse.bacc as bacc
    from concourse.bass_utils import run_bass_kernel_spmd

    nc = bacc.Bacc("TRN2", target_bir_lowering=False, num_devices=1)
    arrays = {}
    handles = {}
    for name, a in laid_out({k: np.asarray(v) for k, v in inputs.items()}).items():
        arrays["in_" + name] = np.ascontiguousarray(a)
        handles[name] = nc.dram_tensor("in_" + name, a.shape, mybir.dt.from_np(a.dtype), kind="ExternalInput").ap()
    for name, shape in OUTPUTS.items():
        handles[name] = nc.dram_tensor(name, shape, F32, kind="ExternalOutput").ap()
    for name, shape in SCRATCH.items():
        handles[name] = nc.dram_tensor(name, shape, F32, kind="Internal").ap()
    layer(nc, handles)
    r = run_bass_kernel_spmd(nc, [arrays], core_ids=[0]).results[0]
    y = r["out_y"].transpose(1, 0, 2).reshape(DM, T).T
    kv = (2, KVH, HEAD)
    return (
        y[None, :SEQ], y[SEQ:, None],
        r["out_cmp_p"].reshape(1, 1, SEQ, *kv), r["out_slc_p"].reshape(1, 1, SEQ, *kv),
        r["out_win_p"].reshape(1, 1, WINDOW, *kv), r["out_hgrn_p"][None, None],
        r["out_cmp_s"].reshape(1, DEC, 1, *kv), r["out_slc_s"].reshape(1, DEC, 1, *kv),
        r["out_win_s"].reshape(1, DEC, WINDOW, *kv), r["out_hgrn_s"][None],
    )
```
